# Optimizing a Trainium2 kernel written in Bass

```python
import math
import jax, jax.numpy as jnp
from jax import lax
import numpy as np

D_MODEL = 1024
BATCH = 1
SEQ = 512
DEPTH = 2
DEC_BATCH = 8
DEC_SEQ = 1
PAST_LEN = 1024
PAGE_SIZE = 128

N_A = DEPTH // 2
HEAD_DIM = 64
MIX_WIDTH = D_MODEL
MEM_HEADS = 4
MEM_WIDTH = MEM_HEADS * HEAD_DIM
SEQ_WIDTH = MIX_WIDTH - MEM_WIDTH
SSM_GROUP = 16
SSM_GROUPS = SEQ_WIDTH // SSM_GROUP
SSM_STATE = 64
FOX_HEADS = SEQ_WIDTH // HEAD_DIM
N_MEM = 256
D_FF = (11 * D_MODEL) // 4
CONV_W = 3
Q_BLOCK = 128
EPS = 1e-6
NEG_INF = -1e30
EIG_CLIP = -1e-4
ATTN_SCALE = HEAD_DIM ** -0.5

kernel_name = 's5_fox_yoco_decoder_step'

F32 = jnp.float32

def rmsnorm(x, g):
    xf = x.astype(F32)
    y = xf * lax.rsqrt(jnp.mean(xf * xf, axis=-1, keepdims=True) + EPS)
    return y.astype(x.dtype) * g

def s5_discretize(lam_re, lam_im, log_dt, b_re, b_im):
    lr = jnp.minimum(lam_re.astype(F32), EIG_CLIP)
    li = lam_im.astype(F32)
    dt = jnp.exp(log_dt.astype(F32))[:, None]
    mag = jnp.exp(lr * dt)
    ar = mag * jnp.cos(li * dt)
    ai = mag * jnp.sin(li * dt)
    den = lr * lr + li * li
    nr = ar - 1.0
    fr = (nr * lr + ai * li) / den
    fi = (ai * lr - nr * li) / den
    br = b_re.astype(F32)
    bi = b_im.astype(F32)
    bbr = fr[..., None] * br - fi[..., None] * bi
    bbi = fr[..., None] * bi + fi[..., None] * br
    return ar, ai, bbr, bbi

def _ssm_combine(e1, e2):
    a1r, a1i, b1r, b1i = e1
    a2r, a2i, b2r, b2i = e2
    return (a2r * a1r - a2i * a1i, a2r * a1i + a2i * a1r,
            a2r * b1r - a2i * b1i + b2r, a2r * b1i + a2i * b1r + b2i)

def s5_mix(u, h0r, h0i, lam_re, lam_im, log_dt, b_re, b_im, c_re, c_im, d_skip, w_glu, b_glu):
    bsz, t, _ = u.shape
    ar, ai, bbr, bbi = s5_discretize(lam_re, lam_im, log_dt, b_re, b_im)
    uf = u.astype(F32).reshape(bsz, t, SSM_GROUPS, SSM_GROUP)
    bu_r = jnp.einsum('btgc,gpc->btgp', uf, bbr)
    bu_i = jnp.einsum('btgc,gpc->btgp', uf, bbi)
    a_r = jnp.broadcast_to(ar, (1, t) + ar.shape)
    a_i = jnp.broadcast_to(ai, (1, t) + ai.shape)
    pr, pim, hr, hi = lax.associative_scan(_ssm_combine, (a_r, a_i, bu_r, bu_i), axis=1)
    h0r = h0r.astype(F32)[:, None]
    h0i = h0i.astype(F32)[:, None]
    hr = hr + pr * h0r - pim * h0i
    hi = hi + pr * h0i + pim * h0r
    y = (jnp.einsum('btgp,gcp->btgc', hr, c_re.astype(F32))
         - jnp.einsum('btgp,gcp->btgc', hi, c_im.astype(F32)))
    y = y.reshape(bsz, t, SEQ_WIDTH) + d_skip.astype(F32) * u.astype(F32)
    y = jax.nn.gelu(y).astype(u.dtype)
    y = y * jax.nn.sigmoid(y @ w_glu + b_glu)
    return y, hr[:, -1], hi[:, -1]

def mem_kv(mem, g, w):
    kv = rmsnorm(mem, g) @ w
    k, v = jnp.split(kv, 2, axis=-1)
    shape = mem.shape[:2] + (MEM_HEADS, HEAD_DIM)
    return k.reshape(shape), v.reshape(shape)

def mem_attention(q, mk, mv):
    s = jnp.einsum('bthd,bmhd->bhtm', q, mk).astype(F32) * ATTN_SCALE
    p = jax.nn.softmax(s, axis=-1).astype(mv.dtype)
    return jnp.einsum('bhtm,bmhd->bthd', p, mv)

def shared_kv(s, g, w_kv, b_f):
    bsz, t, _ = s.shape
    z = rmsnorm(s, g) @ w_kv
    k = z[..., :SEQ_WIDTH].reshape(bsz, t, FOX_HEADS, HEAD_DIM)
    v = z[..., SEQ_WIDTH:2 * SEQ_WIDTH].reshape(bsz, t, FOX_HEADS, HEAD_DIM)
    logf = jax.nn.log_sigmoid(z[..., 2 * SEQ_WIDTH:].astype(F32) + b_f.astype(F32)).astype(s.dtype)
    return k, v, logf

def fox_block(q, k, v, cq, ck, qpos, kpos):
    s = jnp.einsum('bqhd,bkhd->bhqk', q, k).astype(F32) * ATTN_SCALE
    s = s + jnp.transpose(cq, (0, 2, 1))[..., None] - jnp.transpose(ck, (0, 2, 1))[:, :, None, :]
    mask = kpos[None, :] <= qpos[:, None]
    s = jnp.where(mask, s, NEG_INF)
    p = jax.nn.softmax(s, axis=-1).astype(v.dtype)
    return jnp.einsum('bhqk,bkhd->bqhd', p, v)

def fox_prompt(q, k, v, logf):
    bsz, t, h, dh = q.shape
    nb = t // Q_BLOCK
    c = jnp.cumsum(logf.astype(F32), axis=1)
    qb = q.reshape(bsz, nb, Q_BLOCK, h, dh).swapaxes(0, 1)
    cqb = c.reshape(bsz, nb, Q_BLOCK, h).swapaxes(0, 1)
    pos = jnp.arange(t, dtype=jnp.int32)
    posb = pos.reshape(nb, Q_BLOCK)
    out = lax.map(lambda blk: fox_block(blk[0], k, v, blk[1], c, blk[2], pos), (qb, cqb, posb))
    return out.swapaxes(0, 1).reshape(bsz, t, h, dh)

def fox_sample(q, k_new, v_new, logf_new, k_past, v_past, logf_past):
    k = jnp.concatenate([k_past, k_new.astype(k_past.dtype)], axis=1)
    v = jnp.concatenate([v_past, v_new.astype(v_past.dtype)], axis=1)
    logf = jnp.concatenate([logf_past.astype(F32), logf_new.astype(F32)], axis=1)
    c = jnp.cumsum(logf, axis=1)
    t_new = q.shape[1]
    total = k.shape[1]
    past = total - t_new
    kpos = jnp.arange(total, dtype=jnp.int32)
    return fox_block(q, k, v, c[:, past:], c, kpos[past:], kpos)

def causal_dwconv(u, prev, w, b):
    t = u.shape[1]
    ext = jnp.concatenate([prev.astype(u.dtype), u], axis=1)
    y = ext[:, 0:t] * w[0]
    for j in range(1, CONV_W):
        y = y + ext[:, j:j + t] * w[j]
    return y + b, ext[:, t:]

def conv_ffn(h, w_up, cw, cb, w_down, prev):
    u = h @ w_up
    y, new_prev = causal_dwconv(u, prev, cw, cb)
    g, val = jnp.split(y, 2, axis=-1)
    return (jax.nn.silu(g) * val) @ w_down, new_prev

def run_trunk(x, mem_ks, mem_vs, ssm_r0, ssm_i0, conv_prev, fox_attend, p):
    bsz, t, _ = x.shape
    new_r, new_i, new_conv = [], [], []
    kv_rows = None
    for l in range(DEPTH):
        if l == N_A:
            kv_rows = shared_kv(x, p['kv_norm'], p['w_kv'], p['b_f'])
        h = rmsnorm(x, p['norm_mix_pre'][l])
        z = h @ p['w_in'][l]
        z_seq = z[..., :SEQ_WIDTH]
        q_mem = z[..., SEQ_WIDTH:].reshape(bsz, t, MEM_HEADS, HEAD_DIM)
        if l < N_A:
            seq_out, hr, hi = s5_mix(z_seq, ssm_r0[l], ssm_i0[l], p['lam_re'][l], p['lam_im'][l],
                                     p['log_dt'][l], p['b_re'][l], p['b_im'][l], p['c_re'][l],
                                     p['c_im'][l], p['d_skip'][l], p['w_glu'][l], p['b_glu'][l])
            new_r.append(hr)
            new_i.append(hi)
        else:
            q = z_seq.reshape(bsz, t, FOX_HEADS, HEAD_DIM)
            seq_out = fox_attend(q, kv_rows[0], kv_rows[1], kv_rows[2]).reshape(bsz, t, SEQ_WIDTH)
        mem_out = mem_attention(q_mem, mem_ks[l], mem_vs[l]).reshape(bsz, t, MEM_WIDTH)
        o = jnp.concatenate([seq_out.astype(x.dtype), mem_out.astype(x.dtype)], axis=-1) @ p['w_out'][l]
        x = x + rmsnorm(o, p['norm_mix_post'][l])
        f, cp = conv_ffn(rmsnorm(x, p['norm_ffn_pre'][l]), p['w_up'][l], p['conv_w'][l],
                         p['conv_b'][l], p['w_down'][l], conv_prev[l])
        new_conv.append(cp)
        x = x + rmsnorm(f, p['norm_ffn_post'][l])
    return x, jnp.stack(new_r), jnp.stack(new_i), jnp.stack(new_conv), kv_rows

def setup_inputs(seed: int = 0) -> dict:
    key = jax.random.key(seed)
    ks = iter(jax.random.split(key, 48))

    def nrm(shape, scale):
        return jax.random.normal(next(ks), shape, F32) * scale

    n_pages = PAST_LEN // PAGE_SIZE
    n_used = DEC_BATCH * n_pages
    n_pool = n_used + max(1, n_used // 4)
    f2 = 2 * D_FF
    g, pp, cc = SSM_GROUPS, SSM_STATE, SSM_GROUP
    d = D_MODEL
    out = {}
    out['x_prompt'] = nrm((BATCH, SEQ, d), 1.0)
    out['x_sample'] = nrm((DEC_BATCH, DEC_SEQ, d), 1.0)
    out['state_ssm_re'] = nrm((N_A, DEC_BATCH, g, pp), 0.5)
    out['state_ssm_im'] = nrm((N_A, DEC_BATCH, g, pp), 0.5)
    out['cache_k'] = nrm((n_pool, PAGE_SIZE, FOX_HEADS, HEAD_DIM), 1.0)
    out['cache_v'] = nrm((n_pool, PAGE_SIZE, FOX_HEADS, HEAD_DIM), 1.0)
    out['cache_logf'] = jax.nn.log_sigmoid(nrm((n_pool, PAGE_SIZE, FOX_HEADS), 1.0) + 2.5)
    out['cache_mem_k'] = nrm((DEPTH, DEC_BATCH, N_MEM, MEM_HEADS, HEAD_DIM), 1.0)
    out['cache_mem_v'] = nrm((DEPTH, DEC_BATCH, N_MEM, MEM_HEADS, HEAD_DIM), 1.0)
    out['state_ffn_conv'] = nrm((DEPTH, DEC_BATCH, CONV_W - 1, f2), 1.0)
    out['page_table'] = jax.random.permutation(next(ks), n_pool)[:n_used].reshape(DEC_BATCH, n_pages).astype(jnp.int32)
    out['mem_prompt'] = nrm((BATCH, N_MEM, d), 1.0)
    out['w_in'] = nrm((DEPTH, d, MIX_WIDTH), d ** -0.5)
    out['w_out'] = nrm((DEPTH, MIX_WIDTH, d), MIX_WIDTH ** -0.5)
    out['norm_mix_pre'] = 1.0 + nrm((DEPTH, d), 0.05)
    out['norm_mix_post'] = 1.0 + nrm((DEPTH, d), 0.05)
    out['norm_ffn_pre'] = 1.0 + nrm((DEPTH, d), 0.05)
    out['norm_ffn_post'] = 1.0 + nrm((DEPTH, d), 0.05)
    out['mem_norm'] = 1.0 + nrm((DEPTH, d), 0.05)
    out['w_mem_kv'] = nrm((DEPTH, d, 2 * MEM_WIDTH), d ** -0.5)
    out['lam_re'] = -0.5 + nrm((N_A, g, pp), 0.01)
    out['lam_im'] = math.pi * jnp.arange(pp, dtype=F32) + nrm((N_A, g, pp), 0.01)
    out['log_dt'] = jax.random.uniform(next(ks), (N_A, g), F32, math.log(1e-3), math.log(1e-1))
    out['b_re'] = nrm((N_A, g, pp, cc), (2.0 * cc) ** -0.5)
    out['b_im'] = nrm((N_A, g, pp, cc), (2.0 * cc) ** -0.5)
    out['c_re'] = nrm((N_A, g, cc, pp), 0.5)
    out['c_im'] = nrm((N_A, g, cc, pp), 0.5)
    out['d_skip'] = nrm((N_A, SEQ_WIDTH), 0.5)
    out['w_glu'] = nrm((N_A, SEQ_WIDTH, SEQ_WIDTH), SEQ_WIDTH ** -0.5)
    out['b_glu'] = nrm((N_A, SEQ_WIDTH), 0.01)
    out['kv_norm'] = 1.0 + nrm((d,), 0.05)
    out['w_kv'] = nrm((d, 2 * SEQ_WIDTH + FOX_HEADS), d ** -0.5)
    out['b_f'] = jax.random.uniform(next(ks), (FOX_HEADS,), F32, 1.0, 4.0)
    out['w_up'] = nrm((DEPTH, d, f2), d ** -0.5)
    out['conv_w'] = nrm((DEPTH, CONV_W, f2), CONV_W ** -0.5)
    out['conv_b'] = nrm((DEPTH, f2), 0.01)
    out['w_down'] = nrm((DEPTH, D_FF, d), D_FF ** -0.5)
    return out

def reference(x_prompt, x_sample, state_ssm_re, state_ssm_im, cache_k, cache_v, cache_logf,
              cache_mem_k, cache_mem_v, state_ffn_conv, page_table, mem_prompt,
              w_in, w_out, norm_mix_pre, norm_mix_post, norm_ffn_pre, norm_ffn_post,
              mem_norm, w_mem_kv, lam_re, lam_im, log_dt, b_re, b_im, c_re, c_im, d_skip,
              w_glu, b_glu, kv_norm, w_kv, b_f, w_up, conv_w, conv_b, w_down):
    p = dict(w_in=w_in, w_out=w_out, norm_mix_pre=norm_mix_pre, norm_mix_post=norm_mix_post,
             norm_ffn_pre=norm_ffn_pre, norm_ffn_post=norm_ffn_post, lam_re=lam_re, lam_im=lam_im,
             log_dt=log_dt, b_re=b_re, b_im=b_im, c_re=c_re, c_im=c_im, d_skip=d_skip,
             w_glu=w_glu, b_glu=b_glu, kv_norm=kv_norm, w_kv=w_kv, b_f=b_f, w_up=w_up,
             conv_w=conv_w, conv_b=conv_b, w_down=w_down)

    bp = x_prompt.shape[0]
    mem_pairs = [mem_kv(mem_prompt, mem_norm[l], w_mem_kv[l]) for l in range(DEPTH)]
    p_mem_k = jnp.stack([m[0] for m in mem_pairs])
    p_mem_v = jnp.stack([m[1] for m in mem_pairs])
    zeros_ssm = jnp.zeros((N_A, bp, SSM_GROUPS, SSM_STATE), F32)
    zeros_conv = jnp.zeros((DEPTH, bp, CONV_W - 1, 2 * D_FF), x_prompt.dtype)
    y_prompt, p_ssm_re, p_ssm_im, p_conv, p_kv = run_trunk(
        x_prompt, p_mem_k, p_mem_v, zeros_ssm, zeros_ssm, zeros_conv, fox_prompt, p)
    p_k, p_v, p_logf = p_kv

    bs = x_sample.shape[0]
    k_past = cache_k[page_table].reshape(bs, -1, FOX_HEADS, HEAD_DIM)
    v_past = cache_v[page_table].reshape(bs, -1, FOX_HEADS, HEAD_DIM)
    logf_past = cache_logf[page_table].reshape(bs, -1, FOX_HEADS)

    def fox_attend_sample(q, k_new, v_new, logf_new):
        return fox_sample(q, k_new, v_new, logf_new, k_past, v_past, logf_past)

    y_sample, s_ssm_re, s_ssm_im, s_conv, s_kv = run_trunk(
        x_sample, cache_mem_k, cache_mem_v, state_ssm_re, state_ssm_im, state_ffn_conv,
        fox_attend_sample, p)
    s_k, s_v, s_logf = s_kv

    return (y_prompt, y_sample, p_ssm_re, p_ssm_im, p_k, p_v, p_logf, p_mem_k, p_mem_v, p_conv,
            s_ssm_re, s_ssm_im, s_k, s_v, s_logf, s_conv)


_drawn_inputs = setup_inputs


def setup_inputs(seed=0):
    import zlib

    import numpy as np

    out = dict(_drawn_inputs(seed))
    spreads = {}
    factors = {'lam_re': 4.14, 'b_glu': 8.0, 'conv_b': 4.861}
    for name, (base, spread) in spreads.items():
        noise = np.random.default_rng([zlib.crc32(name.encode()), seed]).standard_normal(out[name].shape)
        drawn = base * np.exp(spread * noise) if base else spread * noise
        out[name] = __import__('jax').numpy.asarray(drawn.astype(out[name].dtype))
    for name, factor in factors.items():
        out[name] = (out[name] * factor).astype(out[name].dtype)
    return out
```

```python
import math
from contextlib import ExitStack

import numpy as np

import concourse.bass as bass
from concourse import mybir

F32 = mybir.dt.float32
F32R = mybir.dt.float32r
I32 = mybir.dt.int32
ALU = mybir.AluOpType
ACT = mybir.ActivationFunctionType
AX = mybir.AxisListType

P = 128
T = 512
NB = 8
NT = T + NB
HALF = ((0, 264), (264, NT))
D = 1024
KD = D // P
DFF = 2816
KF = DFF // P
KH = KF // 2
SEQW = 768
KS = SEQW // P
HEADS = 12
MEMH = 4
DH = 64
NMEM = 256
PAST = 1024
PAGE = 128
PAGES = PAST // PAGE
GROUPS, STATE, CH = 48, 64, 16
PAIRS = GROUPS // 2
CHUNK = 8
NCH = T // CHUNK
THIRDS = 3
TP = PAIRS // THIRDS
TG = GROUPS // THIRDS
EPS = 1e-6
NEG = -1e30
SCALE = DH ** -0.5
TWO_PI = 2 * math.pi
ROUND = 12582912.0
PI_LO = 3.1415925


class Own:

    def __init__(self, eng, step):
        self.eng, self.step, self.n, self.last = eng, step, 0, None

    def do(self, ins):
        self.n += 1
        ins.then_inc(self.step, 1)
        self.last = (self.step, self.n)

    def tell(self, ins, sem, value):
        ins.then_inc(sem, 1)
        self.last = (sem, value)

    def mark(self, sem):
        self.sync()
        self.eng.sem_inc(sem, 1)

    def sync(self):
        self.eng.wait_ge(*self.last)


def phases():
    out = [("memkv0", KD, 4), ("memkv1", KD, 4), ("win0", KD, 8), ("glu", KS, 6), ("wout0", KD, 8)]
    for l in range(2):
        if l:
            out += [("kv", KD, 12), ("kvf", KD, 1), ("win1", KD, 8), ("wout1", KD, 8)]
        for f in range(2):
            out += [(f"up{l}{f}", KD, 2 * KH), (f"down{l}{f}", KH, 8)]
    table, base = {}, 0
    for n, (name, kb, panels) in enumerate(out):
        nxt = out[n + 1][0] if n + 1 < len(out) else None
        table[name] = (kb, panels, base, nxt)
        base += panels
    return table, base


def same_side(a):
    return [8 * (a // 2) + 2 * n + a % 2 for n in range(4)]


def misc_jobs():
    jobs = [("rows",), *[("conv", l, a) for l in range(2) for a in range(2)],
            *[("state", l, a) for l in range(2) for a in range(2)], ("lam",)]
    jobs += [("memT", a) for a in range(4)] + [("xT", k) for k in range(KD)] + [("xsT",)]
    jobs += [("ms_mem",)] + [("memtok", l, m) for l in range(2) for m in range(4)]
    jobs += [("ms", "x0", 0), ("ms", "x0", 1)]
    jobs += [("h0", ri, a) for ri in range(2) for a in range(2)]
    for t in range(THIRDS):
        jobs += [("cT", t), *[("bT", t, a) for a in range(TP // 2)], *[("K", t, a) for a in range(TG // 4)]]
        jobs += [("V", t, a) for a in range((TP + 2) // 3)] + [("Y", t, a) for a in range(TG // 4)]
    jobs += [("fin", ri) for ri in range(2)]
    for l in range(2):
        if l:
            jobs += [x for m in range(12) for x in (("kvtok", m), ("kvsamp", m))]
            jobs += [("logf",)]
            jobs += [x for h in range(HEADS) for q in range(4) for x in (("fS", h, q), ("fT", h, q), ("fO", h, q))]
        jobs += [("qrow", l, a) for a in range(2)]
        jobs += [x for h in range(MEMH) for x in (
            ("mS", l, h, 0), ("mS", l, h, 1), ("mT", l, h, 0), ("mT", l, h, 1), ("mO", l, h))]
        jobs += [("mq", l, b) for b in range(NB)]
        jobs += [("mmaxT", l), ("mmax", l), ("mden", l), ("mpv", l)]
        if l:
            jobs += [("dtot",)] + [("dc", a) for a in range(2)]
            jobs += [("fq", b, a) for b in range(NB) for a in range(2)]
            jobs += [("fmaxT",), ("fmax",), ("fden",)] + [("fpv", b) for b in range(NB)]
        jobs += [("ms", f"o{l}", 0), ("ms", f"o{l}", 1), ("ms", f"f{l}", 0), ("ms", f"f{l}", 1)]
        jobs += [("cout", l, a) for a in range(KF * 2 // 4)]
        jobs += [("ms", f"d{l}", 0), ("ms", f"d{l}", 1)]
        if l == 0:
            jobs += [("ms", "x1", 0), ("ms", "x1", 1)]
    jobs += [("yT", c, a) for c in range(5) for a in range(2)]
    return {name: j for j, name in enumerate(jobs)}


def program(nc, I, O):
    PH, PANELS = phases()
    J = misc_jobs()
    ctx = ExitStack()
    with ctx:
        def sb(name, shape, dt=F32):
            return ctx.enter_context(nc.sbuf_tensor(name, shape, dt))

        ident = sb("ident", [P, P])
        ones = sb("ones", [P, P])
        meanw = sb("meanw", [P, P])
        tri = sb("tri", [P, P])
        causal = sb("causal", [P, P])
        sel = sb("sel", [NB, NB, P])
        gains = sb("gains", [P, 100])
        convw = sb("convw", [P, 2, 4 * 2 * KF])
        convs = sb("convs", [P, 2, 2 * NB, 2 * KF])
        newconv = sb("newconv", [P, 2 * KF, 2 + NB])
        rstd = sb("rstd", [P, NT])
        sd = sb("sd", [P, NT])
        sumsq = sb("sumsq", [P, NT])
        sq = sb("sq", [P, 2, NT])
        rstd_mem = sb("rstd_mem", [P, NMEM])
        x = sb("x", [P, KD, NT])
        y = sb("y", [P, KD, NT])
        raw = [sb(f"raw{s}", [P, KH, P]) for s in range(2)]
        w_hi = [sb(f"w_hi{s}", [P, KH, P], F32R) for s in range(2)]
        w_lo = [sb(f"w_lo{s}", [P, KH, P], F32R) for s in range(2)]
        mem_kT = sb("mem_kT", [P, 2, 2, NMEM])
        mem_tok = sb("mem_tok", [P, 2, 2, 512])
        qrow = sb("qrow", [NB, D])
        bf = sb("bf", [HEADS, 1])
        eps = sb("eps", [P, 1])
        qs = sb("qs", [P, 6, NB])
        pages = sb("pages", [1, NB * PAGES], I32)

        class Arena:

            def __init__(self, at, top):
                self.at, self.top = at, top

            def __call__(self, name, shape, dt=F32):
                size = (int(np.prod(shape[1:])) * 4 + 31) // 32 * 32
                assert self.at + size <= self.top, (name, self.at + size - self.top)
                t = nc.alloc_sbuf_tensor_at(name, shape, dt, offset=self.at)
                self.at += size
                return t

        nc_base = nc.sbuf_base
        start = (nc.sbuf_base + 31) // 32 * 32
        top = nc.sbuf_usable_end // 32 * 32
        split = Arena(start, top)
        x_hi = split("x_hi", [P, KD, NT], F32R)
        x_lo = split("x_lo", [P, KD, NT], F32R)
        free = split.at

        a = Arena(free, top - 2560)
        x_tok = a("x_tok", [P, 4, D])
        xs_tok = a("xs_tok", [NB, D])
        mem_in = a("mem_in", [P, 2, D])
        memT = a("memT", [P, KD, NMEM])
        rows = a("rows", [100, P])
        crow = a("crow", [88, 4, P])
        srow = a("srow", [P, 2, 6, P])
        lrow = a("lrow", [P, P])
        dtrow = a("dtrow", [PAIRS, 2])

        early = top - 2560
        e = Arena(early, top)
        lam = e("lam", [P, P])
        hrow = e("hrow", [96, 2, 2, P])
        a = Arena(start, early)
        s5s = a("s5s", [P, 16, PAIRS])
        pw_r = a("pw_r", [P, PAIRS, CHUNK + 1])
        pw_i = a("pw_i", [P, PAIRS, CHUNK + 1])
        h0 = a("h0", [P, 2, NB, PAIRS])
        hfin = a("hfin", [P, 2, 1 + NB, PAIRS])
        hout = a("hout", [108, 2, 2, P])
        b_in = a("b_in", [P, 2, TP, CH])
        bb = a("bb", [P, 2, TP, CH])
        c_in = a("c_in", [P, 2, 2, 2, STATE])
        cT = a("cT", [P, 2, TP, CH])
        bp = a("bp", [P, 2, TP, CHUNK * CH])
        bT = a("bT", [P, TP, 2, P])
        cp = a("cp", [P, 2, TP, (CHUNK + 1) * CH])
        kern = a("kern", [CH, TG, P])
        toep = a("toep", [P, TG, P])
        u = a("u", [P, TG, NCH + 2 * NB])
        v = a("v", [P, 2, TP, NCH + NB])
        e_r = a("e_r", [P, TP, NCH])
        e_i = a("e_i", [P, TP, NCH])
        decay = a("decay", [P, TP, NCH])
        tmp = [a(f"tmp{n}", [P, TP * (CHUNK + 1) * CH]) for n in range(3)]
        hp = a("hp", [P, 2, TP, NB + 1 + NCH])
        yb = a("yb", [P, TG, NB + NCH])
        yz = a("yz", [P, 2, NT])
        a = Arena(free, top)
        gate = a("gate", [P, KS, NT])

        def mem_buffers(a, l):
            return dict(
                p=a(f"mp{l}", [P, 2, 2, NMEM]), pT=a(f"mpT{l}", [P, 2, T]), st=a(f"mst{l}", [P, 2, 8]),
                k=a(f"mk{l}", [P, 2, 2, NMEM]), v=a(f"mv{l}", [P, NB, 2, NMEM]), prod=a(f"mprod{l}", [P, 2, NMEM]),
                s=a(f"ms{l}", [P, NB, 2, MEMH]), dst=a(f"mdst{l}", [P, 8, NB * MEMH]))

        mb = [mem_buffers(a, 0)]

        a = Arena(free, top)
        h_hi = a("h_hi", [P, KH, NT], F32R)
        h_lo = a("h_lo", [P, KH, NT], F32R)
        uc = [a(f"uc{s}", [P, 2 + NT]) for s in range(2)]
        yc = [a(f"yc{s}", [P, NT]) for s in range(2)]
        hf = a("hf", [P, NT])
        sg = a("sg", [P, NT])
        a = Arena(free, top)
        crows = a("crows", [2 + NB, 2 * KF, P])
        a = Arena(free, top)
        ytok = [a(f"ytok{s}", [P, D]) for s in range(2)]

        a = Arena(free, top)
        qh = a("qh", [P, HEADS, T])
        kh = a("kh", [P, HEADS, T])
        after_heads = a.at
        vtok = y[:, 0:6, :].rearrange("p a b -> p (a b)")[:, 0:4 * SEQW].rearrange("p (c f) -> p c f", c=4)
        kvs = a("kvs", [NB, 2, SEQW])
        lfs = a("lfs", [NB, HEADS])
        keep = a.at
        kvT = a("kvT", [P, NT])
        ktok = [a(f"ktok{s}", [P, 4, P]) for s in range(2)]
        lf = a("lf", [HEADS, 3, NT])
        lft = a("lft", [P, 4, HEADS])
        a = Arena(keep, top)
        pa = a("pa", [P, T])
        paT = a("paT", [P, T])
        pst = a("pst", [P, 8])
        mba = Arena(free, after_heads)
        mb.append(mem_buffers(mba, 1))
        a = Arena(mba.at, after_heads)
        NPG = 4
        page = [a(f"page{n}", [P, SEQW]) for n in range(NPG)]
        logf = a("logf", [P, NB, PAGES, HEADS])
        a = Arena(free, mba.at)
        qb = [a(f"qb{n}", [P, SEQW]) for n in range(2)]
        prod = a("prod", [P, SEQW])
        sc = a("sc", [P, NB, PAGES + 1, HEADS])
        pre = a("pre", [P, NB, PAGES, HEADS])
        fst = a("fst", [P, 8, NB * HEADS])
        lmask = a("lmask", [NB, NB, HEADS])

        z_dram = nc.dram_tensor("z_scratch", [SEQW, NT], F32, kind="Internal").ap()
        y_dram = nc.dram_tensor("y_scratch", [SEQW, NT], F32, kind="Internal").ap()

        assert nc.sbuf_base == nc_base

        big = [ctx.enter_context(nc.psum_tensor(f"big{n}", [P, 512], F32)) for n in range(4)]
        misc = [ctx.enter_context(nc.psum_tensor(f"misc{n}", [P, 512], F32)) for n in range(4)]

        def sem(name):
            return ctx.enter_context(nc.semaphore(name))

        raw_loaded = [sem(f"raw_loaded{s}") for s in range(2)]
        hi_made, lo_made = sem("hi_made"), sem("lo_made")
        panel_done, panel_read = sem("panel_done"), sem("panel_read")
        misc_full = [sem(f"misc_full{n}") for n in range(4)]
        misc_free = [sem(f"misc_free{n}") for n in range(4)]
        act_step, dve_step, pool_step = sem("act_step"), sem("dve_step"), sem("pool_step")
        S = {}

        def s_(name):
            if name not in S:
                S[name] = sem(name)
            return S[name]

        def bank(job):
            return misc[J[job] % 4]

        def full(eng, job):
            eng.wait_ge(misc_full[J[job] % 4], J[job] // 4 + 1)

        def freed(own, ins, job):
            own.tell(ins, misc_free[J[job] % 4], J[job] // 4 + 1)

        OFF = dict(mix_pre=0, mix_post=16, ffn_pre=32, ffn_post=48, mem=64, kv=80, dskip=88, bglu=94)

        def gain(name, k, l=0):
            c = OFF[name] + (l * KD if name not in ("kv", "dskip", "bglu") else 0) + k
            return gains[:, c:c + 1]

        def dep_loop(eng, count):
            return eng.Fori(0, count)

        block = ctx.enter_context(nc.Block())

        @block.sync
        def _(sp):
            stores = [0]

            def load(dst, src, sm, **kw):
                sp.dma_start(dst, src, **kw).then_inc(s_(sm), 16)

            def store(dst, src, **kw):
                sp.dma_start(dst, src, **kw).then_inc(s_("stored"), 16)
                stores[0] += 1

            def weights(name, src, after=None):
                kb, n, base, _ = PH[name]

                def one(i, q, half):
                    slot = (base + half) % 2
                    if not isinstance(q, int) or q >= 2:
                        sp.wait_ge(lo_made, q - 1)
                    view = src(i)
                    sp.dma_start(raw[slot][:, 0:kb, 0:view.shape[2]], view).then_inc(raw_loaded[slot], 16)

                if n <= 2 or base < 2 or after is not None:
                    for i in range(n):
                        one(i, base + i, i % 2)
                        if after is not None:
                            after(i)
                else:
                    with sp.Fori(0, n // 2) as it:
                        for half in range(2):
                            one(it * 2 + half, it * 2 + (base + half), half)

            def cols(w, rows=None):
                w = w if rows is None else w[rows[0]:rows[1], :]
                v3 = w.rearrange("(k p) n -> p k n", p=P)
                return lambda i: v3[:, :, bass.ds(i * P, P)]

            for n, nm in enumerate(("norm_mix_pre", "norm_mix_post", "norm_ffn_pre", "norm_ffn_post", "mem_norm")):
                load(rows[16 * n:16 * n + 16, :], I[nm].rearrange("l (k p) -> (l k) p", p=P), "rows_in")
            load(rows[80:88, :], I["kv_norm"].rearrange("(k p) -> k p", p=P), "rows_in")
            load(rows[88:94, :], I["d_skip"].rearrange("l (k p) -> (l k) p", p=P), "rows_in")
            load(rows[94:100, :], I["b_glu"].rearrange("l (k p) -> (l k) p", p=P), "rows_in")
            load(mem_in[:], I["mem_prompt"].rearrange("b (c p) d -> p (b c) d", p=P), "mem_in")
            load(x_tok[:], I["x_prompt"].rearrange("b (c p) d -> p (b c) d", p=P), "x_in")
            load(xs_tok[:], I["x_sample"].rearrange("b t d -> (b t) d"), "x_in")
            for l in range(2):
                taps = I["conv_w"][l].rearrange("t (f p) -> (t f) p", p=P)
                load(crow[:, 2 * l, :], taps[0:88, :], "conv_in")
                load(crow[0:44, 2 * l + 1, :], taps[88:132, :], "conv_in")
                load(crow[44:88, 2 * l + 1, :], I["conv_b"][l].rearrange("(f p) -> f p", p=P), "conv_in")
                st = I["state_ffn_conv"][l].rearrange("b t (f p) -> (b t f) p", p=P)
                load(srow[:, l, 0:5, :], st[0:640, :].rearrange("(r q) p -> q r p", q=P), "conv_in")
                load(srow[0:64, l, 5, :], st[640:704, :], "conv_in")
            sp.wait_ge(s_("lrow_zero"), 1)
            load(lrow[0:24, :], I["lam_re"][0].rearrange("(j g) p -> j (g p)", g=2), "lam_in")
            load(lrow[32:56, :], I["lam_im"][0].rearrange("(j g) p -> j (g p)", g=2), "lam_in")
            load(dtrow[:], I["log_dt"][0].rearrange("(j g) -> j g", g=2), "lam_in")
            load(pages[:], I["page_table"].rearrange("(a b) p -> a (b p)", a=1), "pages_in")
            load(bf[:], I["b_f"].rearrange("(h a) -> h a", a=1), "bf_in")
            for ri, nm in enumerate(("state_ssm_re", "state_ssm_im")):
                st = I[nm][0].rearrange("b (j g) p -> (b j) (g p)", g=2)
                for half in range(2):
                    load(hrow[:, ri, half, :], st[96 * half:96 * half + 96, :], "h0_in")

            weights("memkv0", cols(I["w_mem_kv"][0]))
            weights("memkv1", cols(I["w_mem_kv"][1]))
            for l in range(2):
                sp.wait_ge(s_("memtok_ready"), 4 * (l + 1))
                for nm, c in (("prompt_mem_k", 0), ("prompt_mem_v", 256)):
                    store(O[nm][l, 0].rearrange("(c p) h d -> p c (h d)", p=P), mem_tok[:, l, :, c:c + 256])
            weights("win0", cols(I["w_in"][0]))

            zs3 = z_dram.rearrange("(g c) n -> c g n", c=CH)
            ys3 = y_dram.rearrange("(g c) n -> c g n", c=CH)
            sp.wait_ge(s_("z_ready"), 8)
            for m in range(KS):
                sp.dma_start(z_dram[m * P:(m + 1) * P, :], y[:, m, :]).then_inc(s_("z_out"), 16)
            for t in range(THIRDS):
                g0 = t * TG
                if t:
                    sp.wait_ge(s_("s5_built"), t)
                for ri, nm in enumerate(("b_re", "b_im")):
                    load(b_in[:, ri], I[nm][0, g0:g0 + TG].rearrange("(j g) p c -> (g p) j c", g=2), "bc_in")
                for ri, nm in enumerate(("c_re", "c_im")):
                    for dup in range(2):
                        load(c_in[:, ri, :, dup, :],
                             I[nm][0, g0:g0 + TG].rearrange("(t g) c p -> (g c) t p", g=8), "bc_in")
                if t == 0:
                    sp.wait_ge(s_("z_out"), 16 * KS)
                    sp.wait_ge(s_("s5_zero"), 1)
                else:
                    sp.wait_ge(misc_full[J[("Y", t - 1, 3)] % 4], J[("Y", t - 1, 3)] // 4 + 1)
                for tau in range(CHUNK):
                    j = CHUNK - 1 - tau
                    load(u[CH * tau:CH * tau + CH, :, NB:NB + NCH], zs3[:, g0:g0 + TG, j * NCH:(j + 1) * NCH], "u_in")
                load(u[P - CH:P, :, 0:NB], zs3[:, g0:g0 + TG, T:NT], "u_in")
                load(u[0:CH, :, NB + NCH:], zs3[:, g0:g0 + TG, T:NT], "u_in")
                sp.wait_ge(s_("kern_ready"), 4 * (t + 1))
                for tau in range(CHUNK):
                    load(toep[CH * tau:CH * tau + CH, :, (CHUNK - 1 - tau) * CH:P],
                         kern[:, :, 0:(tau + 1) * CH], "toep_in")
                sp.wait_ge(s_("yb_ready"), 4 * (t + 1))
                for i in range(CHUNK):
                    sp.dma_start(ys3[:, g0:g0 + TG, i * NCH:(i + 1) * NCH],
                                 yb[CH * i:CH * i + CH, :, NB:]).then_inc(s_("y_out"), 16)
                sp.dma_start(ys3[:, g0:g0 + TG, T:NT], yb[0:CH, :, 0:NB]).then_inc(s_("y_out"), 16)
                sp.wait_ge(s_("y_out"), 16 * 9 * (t + 1))
                if t:
                    sp.wait_ge(s_("yz_used"), t)
                load(yz[:], y_dram[g0 * CH:(g0 + TG) * CH, :].rearrange("(m p) n -> p m n", p=P), "yz_in")
            sp.wait_ge(s_("hout_ready"), 2)
            for ri, (pn, sn) in enumerate((("prompt_ssm_re", "sample_ssm_re"), ("prompt_ssm_im", "sample_ssm_im"))):
                store(O[pn][0, 0].rearrange("(j g) p -> j (g p)", g=2), hout[0:24, ri, 0, :])
                so = O[sn][0].rearrange("b (j g) p -> (b j) (g p)", g=2)
                store(so[0:84, :], hout[24:108, ri, 0, :])
                store(so[84:192, :], hout[:, ri, 1, :])
            weights("glu", cols(I["w_glu"][0]))

            def mem_loads(l, m):
                if l == 0:
                    sp.wait_ge(s_("gated"), KS)
                load(m["v"][:].rearrange("p b c n -> p (b c) n"),
                     I["cache_mem_v"][l].rearrange("b (c p) h d -> p (b c) (h d)", p=P), "mv_in")
                for b in range(NB):
                    if b >= 2:
                        sp.wait_ge(s_("mk_used"), NB * l + b - 1)
                    load(m["k"][:, b % 2], I["cache_mem_k"][l, b].rearrange("(c p) h d -> p c (h d)", p=P),
                         f"mk_in{b % 2}")

            mem_loads(0, mb[0])
            weights("wout0", cols(I["w_out"][0]))

            def ffn_weights(l):
                for f in range(2):
                    wu = I["w_up"][l].rearrange("(k p) n -> p k n", p=P)

                    def up(i, wu=wu, f=f):
                        it, half = i
                        return wu[:, :, bass.ds(it * P + (f * KH + half * KF) * P, P)]

                    kb, n, base, _ = PH[f"up{l}{f}"]
                    with sp.Fori(0, KH) as it:
                        for half in range(2):
                            slot = (base + half) % 2
                            sp.wait_ge(lo_made, it * 2 + (base + half - 1))
                            sp.dma_start(raw[slot][:, 0:KD, :], up((it, half))).then_inc(raw_loaded[slot], 16)
                    weights(f"down{l}{f}", cols(I["w_down"][l], (f * KH * P, (f + 1) * KH * P)))
                store(O["sample_ffn_conv"][l, :, 0, :], I["state_ffn_conv"][l, :, 1, :])
                sp.wait_ge(s_("crows_ready"), KF * 2 // 4 * (l + 1))
                flat = crows[:].rearrange("r f p -> r (f p)")
                sp.dma_start(O["prompt_ffn_conv"][l, 0], flat[0:2]).then_inc(s_("crows_out"), 16)
                sp.dma_start(O["sample_ffn_conv"][l, :, 1, :], flat[2:2 + NB]).then_inc(s_("crows_out"), 16)

            ffn_weights(0)

            def store_k(i):
                m = i - 4
                if 0 <= m < 6:
                    sp.wait_ge(s_("ktok_ready"), m + 1)
                    sp.dma_start(O["prompt_k"][0].rearrange("(c p) h d -> p c (h d)", p=P)[:, :, m * P:(m + 1) * P],
                                 ktok[m % 2][:]).then_inc(s_(f"ktok_out{m % 2}"), 16)

            weights("kv", cols(I["w_kv"]), store_k)
            wf = I["w_kv"].rearrange("(k p) n -> p k n", p=P)
            weights("kvf", lambda i: wf[:, :, 2 * SEQW:2 * SEQW + HEADS])
            sp.wait_ge(s_("vtok_ready"), 6)
            store(O["prompt_v"][0].rearrange("(c p) h d -> p c (h d)", p=P), vtok)
            sp.wait_ge(s_("kvs_ready"), 12)
            store(O["sample_k"].rearrange("b t h d -> (b t) (h d)"), kvs[:, 0, :])
            store(O["sample_v"].rearrange("b t h d -> (b t) (h d)"), kvs[:, 1, :])
            sp.wait_ge(s_("logf_ready"), 2)
            store(O["prompt_logf"][0].rearrange("(c p) h -> p c h", p=P), lft[:, 0:4, :])
            store(O["sample_logf"].rearrange("b t h -> (b t) h"), lfs[:])
            sp.wait_ge(s_("c_ready"), 3)
            load(qh[DH:DH + 1, :, :], lf[:, 2, 0:T], "aug_in")
            load(kh[DH + 1:DH + 2, :, :], lf[:, 0, 0:T], "aug_in")
            weights("win1", cols(I["w_in"][1]))
            sp.wait_ge(s_("heads_done"), 1)
            mem_loads(1, mb[1])
            sp.wait_ge(s_("pages_in"), 16)

            def page_id(n):
                return sp.value_load(pages[0:1, bass.ds(n, 1)], min_val=0, max_val=I["cache_k"].shape[0] - 1)

            with sp.Fori(0, NB) as b:
                for pg in range(PAGES):
                    load(logf[:, bass.ds(b, 1), pg, :].rearrange("p a h -> p (a h)"),
                         I["cache_logf"][bass.ds(page_id(b * PAGES + pg), 1)].rearrange("a t h -> (a t) h"), "logf_in")

            def page_load(cache, n, slot, after=None, count=None):
                if after is not None:
                    sp.wait_ge(after, count)
                load(page[slot][:], cache[bass.ds(page_id(n), 1)].rearrange("a t h d -> (a t) (h d)"),
                     f"page_in{slot}")

            for n in range(NPG):
                page_load(I["cache_k"], n, n)
            for cache, used in ((I["cache_k"], s_("k_used")), (I["cache_v"], s_("v_used"))):
                with sp.Fori(0, NB - 1) as b:
                    for pg in range(PAGES):
                        page_load(cache, b * PAGES + (pg + NPG), pg % NPG, used, b * PAGES + (pg + 1))
                last = (NB - 1) * PAGES
                for n in range(last, last + PAGES - NPG):
                    page_load(cache, n + NPG, n % NPG, used, n + 1)
                if used is s_("k_used"):
                    for n in range(NPG):
                        page_load(I["cache_v"], n, n, used, NB * PAGES - NPG + n + 1)
            weights("wout1", cols(I["w_out"][1]))
            ffn_weights(1)
            for c in range(5):
                sp.wait_ge(s_("ytok_ready"), 2 * (c + 1))
                dst = O["y_prompt"][0, c * P:(c + 1) * P, :] if c < 4 else O["y_sample"].rearrange("b t d -> (b t) d")
                sp.dma_start(dst, ytok[c % 2][0:(P if c < 4 else NB), :]).then_inc(s_(f"ytok_out{c % 2}"), 16)
            sp.wait_ge(s_("stored"), 16 * stores[0])
            sp.wait_ge(s_("crows_out"), 16 * 4)
            for s in range(2):
                sp.wait_ge(s_(f"ktok_out{s}"), 16 * 3)
                sp.wait_ge(s_(f"ytok_out{s}"), 16 * (3 - s))

        @block.gpsimd
        def _(pool):
            own = Own(pool, pool_step)
            own.do(pool.memset(ident[:], 0.0))
            own.do(pool.memset(ones[:], 1.0))
            own.do(pool.memset(meanw[:], 1.0 / D))
            own.do(pool.memset(tri[:], 1.0))
            own.do(pool.memset(causal[:], 0.0))
            own.do(pool.memset(sel[:], 0.0))
            own.tell(pool.memset(lrow[:], 0.0), s_("lrow_zero"), 1)
            own.sync()
            own.do(pool.affine_select(out=ident[:], in_=ident[:], compare_op=ALU.not_equal, fill=1.0, base=0,
                                      pattern=[[-1, P]], channel_multiplier=1))
            own.do(pool.affine_select(out=tri[:], in_=tri[:], compare_op=ALU.is_ge, fill=0.0, base=0,
                                      pattern=[[1, P]], channel_multiplier=-1))
            own.do(pool.affine_select(out=causal[:], in_=causal[:], compare_op=ALU.is_ge, fill=NEG / SCALE, base=0,
                                      pattern=[[-1, P]], channel_multiplier=1))
            own.tell(pool.affine_select(out=sel[:], in_=sel[:], compare_op=ALU.not_equal, fill=1.0, base=0,
                                        pattern=[[-1, NB], [0, P]], channel_multiplier=1), s_("consts"), 1)

            def lo(q, slot, kb):
                pool.wait_ge(hi_made, q + 1)
                pool.tensor_tensor(w_lo[slot][:, 0:kb, :], raw[slot][:, 0:kb, :],
                                   w_hi[slot][:, 0:kb, :].bitcast(F32), ALU.subtract).then_inc(lo_made, 1)

            for name, (kb, n, base, _) in PH.items():
                if n <= 2:
                    for i in range(n):
                        lo(base + i, (base + i) % 2, kb)
                    continue
                with pool.Fori(0, n // 2) as it:
                    for half in range(2):
                        lo(it * 2 + (base + half), (base + half) % 2, kb)

        @block.vector
        def _(dve):
            own = Own(dve, dve_step)
            do, tell, sync, mark = own.do, own.tell, own.sync, own.mark
            V = dve
            stat = [0, 0]

            def evac(job, dst, src):
                full(dve, job)
                freed(own, V.tensor_copy(dst, src), job)

            def sum_squares(count, cols):
                for k in range(count):
                    dve.wait_ge(s_("sq_made"), stat[0] + 1)
                    if k == 0:
                        ins = V.tensor_copy(sumsq[:, 0:cols], sq[:, stat[0] % 2, 0:cols])
                    else:
                        sync()
                        ins = V.tensor_tensor(sumsq[:, 0:cols], sumsq[:, 0:cols], sq[:, stat[0] % 2, 0:cols], ALU.add)
                    stat[0] += 1
                    tell(ins, s_("sq_used"), stat[0])

            nstd = [0]

            def reciprocal_std(dst, cols):
                nstd[0] += 1
                dve.wait_ge(s_("root_made"), nstd[0])
                tell(V.reciprocal(dst[:, 0:cols], sd[:, 0:cols]), s_("rstd_ready"), nstd[0])
                sync()

            def split_lo(k, src, g, dst, cols=slice(0, NT), hi=None):
                stat[1] += 1
                dve.wait_ge(s_("xhi_made"), stat[1])
                h = x_hi[:, k, cols].bitcast(F32)
                if g is None:
                    ins = V.tensor_tensor(x_lo[:, k, cols], src, h, ALU.subtract)
                else:
                    ins = V.scalar_tensor_tensor(x_lo[:, k, cols], src, g, h, ALU.mult, ALU.subtract)
                tell(ins, s_("xlo_made"), stat[1])

            dve.wait_ge(s_("lam_in"), 48)
            dve.wait_ge(s_("lrow_zero"), 1)
            do(V.tensor_copy(lrow[64:64 + PAIRS, :].rearrange("j (g p) -> j g p", g=2),
                             dtrow[:].unsqueeze(2).to_broadcast([PAIRS, 2, STATE])))
            mark(s_("lrow_ready"))
            do(V.memset(eps[:], EPS))
            mark(s_("h_made"))
            evac(("rows",), gains[:], bank(("rows",))[:, 0:100])
            for l in range(2):
                for a_ in range(2):
                    evac(("conv", l, a_), convw[:, l, 88 * a_:88 * a_ + 88], bank(("conv", l, a_))[:, 0:88])
            for l in range(2):
                flat = convs[:, l].rearrange("p r f -> p (r f)")
                for a_ in range(2):
                    w = 512 if a_ == 0 else 192
                    evac(("state", l, a_), flat[:, 512 * a_:512 * a_ + w], bank(("state", l, a_))[:, 0:w])
            evac(("lam",), lam[:, 0:96], bank(("lam",))[:, 0:96])
            mark(s_("lam_ready"))
            for a_ in range(4):
                full(dve, ("memT", a_))
                freed(own, V.tensor_copy(memT[:, 2 * a_:2 * a_ + 2, :].rearrange("p k t -> p (k t)"),
                                         bank(("memT", a_))[:, :]), ("memT", a_))
            sync()
            mark(s_("mem_ready"))
            for k in range(KD):
                evac(("xT", k), x[:, k, 0:T], bank(("xT", k))[:, :])
            evac(("xsT",), x[:, :, T:NT], bank(("xsT",))[:, 0:KD * NB].rearrange("p (k b) -> p k b", b=NB))
            sync()
            mark(s_("x_ready"))

            sum_squares(KD, NMEM)
            def sums_ready():
                mark(s_("sumsq_ready"))

            sums_ready()
            reciprocal_std(rstd_mem, NMEM)
            for l in range(2):
                for k in range(KD):
                    split_lo(k, memT[:, k, :], gain("mem", k, l), None, slice(l * NMEM, (l + 1) * NMEM))
            for l in range(2):
                base = PH[f"memkv{l}"][2]
                for m in range(4):
                    q = base + m
                    dve.wait_ge(panel_done, q + 1)
                    src = big[2 * (q % 2)][:, 0:NMEM]
                    dst = mem_kT[:, l, m, :] if m < 2 else sq[:, m - 2, 0:NMEM]
                    if l and m >= 2:
                        full(dve, ("memtok", 0, m))
                    tell(V.tensor_tensor(dst, src, rstd_mem[:], ALU.mult), panel_read, q + 1)
                for m in range(4):
                    full(dve, ("memtok", l, m))
                    freed(own, V.tensor_copy(mem_tok[:, l, :, m * P:(m + 1) * P],
                                             bank(("memtok", l, m))[:, 0:256].rearrange("p (c f) -> p c f", c=2)),
                          ("memtok", l, m))
                    sync()
                    mark(s_("memtok_ready"))

            def pre_norm(name, l):
                for k in range(KD):
                    split_lo(k, x[:, k, :], gain(name, k, l), None)

            sum_squares(KD, NT)
            sums_ready()
            pre_norm("mix_pre", 0)
            reciprocal_std(rstd, NT)

            def read_panel(q, dst_of, mult=True):
                slot = q % 2
                dve.wait_ge(panel_done, q + 1)
                for n, (c0, c1) in enumerate(HALF):
                    dst, src, r = dst_of(n, c0, c1), big[2 * slot + n][:, 0:c1 - c0], rstd[:, c0:c1]
                    if len(dst.shape) == 3:
                        src = src[:, 0:(c1 - c0) // 8 * 8].rearrange("p (k j) -> p k j", j=CHUNK)[:, 0:dst.shape[1], :]
                        r = r.rearrange("p (k j) -> p k j", j=CHUNK)[:, 0:dst.shape[1], :]
                    ins = V.tensor_tensor(dst, src, r, ALU.mult)
                    if n == 0 or len(dst.shape) == 3:
                        do(ins)
                if len(dst.shape) == 3:
                    ins = V.tensor_tensor(dst_of(2, T, NT), big[2 * slot + 1][:, T - HALF[1][0]:NT - HALF[1][0]],
                                          rstd[:, T:NT], ALU.mult)
                tell(ins, panel_read, q + 1)

            def by_chunk(tile):
                return tile[:, 0:T].rearrange("p (j k) -> p k j", j=CHUNK)

            K0 = HALF[0][1] // CHUNK
            for m in range(8):
                q = PH["win0"][2] + m
                if m < KS:
                    pick = {0: by_chunk(y[:, m, :])[:, 0:K0, :], 1: by_chunk(y[:, m, :])[:, K0:NCH, :],
                            2: y[:, m, T:NT]}
                    read_panel(q, lambda n, c0, c1: pick[n])
                else:
                    read_panel(q, lambda n, c0, c1: y[:, m, c0:c1])
                sync()
                mark(s_("z_ready"))

            lr_, li_, dt_ = lam[:, 0:PAIRS], lam[:, 32:32 + PAIRS], lam[:, 64:64 + PAIRS]

            def sl(n):
                return s5s[:, n, :]

            def tt(o, a_, b_, op):
                do(V.tensor_tensor(o, a_, b_, op))
                sync()

            def ts(o, a_, c0, c1, o0, o1):
                do(V.tensor_scalar(o, a_, c0, c1, o0, o1))
                sync()

            LR, X1, TH, MAG, SN, CS, R8, FR, FI, T0, T1, T2, R1, R2, UR, UI = range(16)
            sync()
            ts(sl(LR), lr_, -1e-4, None, ALU.min, ALU.bypass)
            dve.wait_ge(s_("s5_act"), 1)
            tt(sl(X1), sl(LR), dt_, ALU.mult)
            tt(sl(TH), li_, dt_, ALU.mult)
            for dst, shift in ((R1, 0.0), (R2, math.pi / 2)):
                ts(sl(T0), sl(TH), 1.0 / TWO_PI, shift / TWO_PI, ALU.mult, ALU.add)
                ts(sl(T0), sl(T0), ROUND, -ROUND, ALU.add, ALU.add)
                c1 = 6.28125
                c2 = float(np.float32(TWO_PI - c1))
                c3 = TWO_PI - c1 - c2
                ts(sl(T1), sl(T0), -c1, None, ALU.mult, ALU.bypass)
                tt(sl(dst), sl(TH), sl(T1), ALU.add)
                ts(sl(T1), sl(T0), -c2, None, ALU.mult, ALU.bypass)
                tt(sl(dst), sl(dst), sl(T1), ALU.add)
                ts(sl(T1), sl(T0), -c3, None, ALU.mult, ALU.bypass)
                tt(sl(dst), sl(dst), sl(T1), ALU.add)
                if shift:
                    ts(sl(dst), sl(dst), shift, None, ALU.add, ALU.bypass)
                ts(sl(dst), sl(dst), PI_LO, -PI_LO, ALU.min, ALU.max)
            tell(V.tensor_copy(sl(T2), sl(R1)), s_("angles_ready"), 1)
            sync()
            dve.wait_ge(s_("s5_act"), 5)
            AR, AI = pw_r[:, :, 1], pw_i[:, :, 1]
            tt(AR, sl(MAG), sl(CS), ALU.mult)
            tt(AI, sl(MAG), sl(SN), ALU.mult)
            tt(sl(T0), sl(LR), sl(LR), ALU.mult)
            tt(sl(T1), li_, li_, ALU.mult)
            tt(sl(T0), sl(T0), sl(T1), ALU.add)
            do(V.reciprocal(sl(T0), sl(T0)))
            sync()
            ts(sl(T2), AR, -1.0, None, ALU.add, ALU.bypass)
            tt(sl(FR), sl(T2), sl(LR), ALU.mult)
            tt(sl(T1), AI, li_, ALU.mult)
            tt(sl(FR), sl(FR), sl(T1), ALU.add)
            tt(sl(FR), sl(FR), sl(T0), ALU.mult)
            tt(sl(FI), AI, sl(LR), ALU.mult)
            tt(sl(T1), sl(T2), li_, ALU.mult)
            tt(sl(FI), sl(FI), sl(T1), ALU.subtract)
            tt(sl(FI), sl(FI), sl(T0), ALU.mult)

            def cmul(o_r, o_i, a_r, a_i, b_r, b_i, t0, conj=False, neg_i=False):
                tt(o_r, a_r, b_r, ALU.mult)
                tt(t0, a_i, b_i, ALU.mult)
                tt(o_r, o_r, t0, ALU.add if conj else ALU.subtract)
                tt(o_i, a_r, b_i, ALU.mult)
                tt(t0, a_i, b_r, ALU.mult)
                if neg_i:
                    do(V.scalar_tensor_tensor(o_i, o_i, -1.0, t0, ALU.mult, ALU.subtract))
                    sync()
                else:
                    tt(o_i, o_i, t0, ALU.subtract if conj else ALU.add)

            do(V.memset(pw_r[:, :, 0:1], 1.0))
            do(V.memset(pw_i[:, :, 0:1], 0.0))
            sync()
            for m in (1, 2, 4):
                w_r = pw_r[:, :, m:m + 1].to_broadcast([P, PAIRS, m])
                w_i = pw_i[:, :, m:m + 1].to_broadcast([P, PAIRS, m])
                tv = tmp[0][:, 0:PAIRS * m].rearrange("p (j m) -> p j m", m=m)
                cmul(pw_r[:, :, m + 1:2 * m + 1], pw_i[:, :, m + 1:2 * m + 1], w_r, w_i,
                     pw_r[:, :, 1:m + 1], pw_i[:, :, 1:m + 1], tv)
            do(V.tensor_copy(sl(UR), sl(CS)))
            do(V.tensor_copy(sl(UI), sl(SN)))
            sync()

            def square(w_r, w_i, t0, t1):
                tt(t0, w_r, w_r, ALU.mult)
                tt(t1, w_i, w_i, ALU.mult)
                tt(w_i, w_r, w_i, ALU.mult)
                ts(w_i, w_i, 2.0, None, ALU.mult, ALU.bypass)
                tt(w_r, t0, t1, ALU.subtract)

            for _ in range(3):
                square(sl(UR), sl(UI), sl(T0), sl(T1))
            for ri in range(2):
                for half in range(2):
                    evac(("h0", ri, half), h0[:, ri].rearrange("p b j -> p (b j)")[:, 96 * half:96 * half + 96],
                         bank(("h0", ri, half))[:, 0:96])
            do(V.memset(u[:], 0.0))
            do(V.memset(toep[:], 0.0))
            do(V.memset(hp[:, :, :, NB:NB + 1], 0.0))
            sync()
            tell(V.memset(e_i[:, :, 0:1], 0.0), s_("s5_zero"), 1)
            do(V.memset(e_r[:, :, 0:1], 1.0))
            sync()

            for t in range(THIRDS):
                j0 = t * TP
                js = slice(j0, j0 + TP)
                dve.wait_ge(s_("bc_in"), 16 * 6 * (t + 1))
                tv = tmp[0][:, 0:TP * CH].rearrange("p (j c) -> p j c", c=CH)
                f_r = s5s[:, FR, js].unsqueeze(2).to_broadcast([P, TP, CH])
                f_i = s5s[:, FI, js].unsqueeze(2).to_broadcast([P, TP, CH])
                cmul(bb[:, 0], bb[:, 1], f_r, f_i, b_in[:, 0], b_in[:, 1], tv)
                full(dve, ("cT", t))
                for ri in range(2):
                    srcc = bank(("cT", t))[:, 256 * ri:256 * ri + 256].rearrange(
                        "p (j g c) -> p j g c", g=2, c=CH)
                    do(V.tensor_copy(cT[0:64, ri], srcc[0:64, :, 0, :]))
                    ins = V.tensor_copy(cT[64:128, ri], srcc[64:128, :, 1, :])
                    if ri == 0:
                        do(ins)
                freed(own, ins, ("cT", t))
                sync()
                mark(s_("s5_built"))
                n = CHUNK
                ap_r = pw_r[:, js, 0:n].unsqueeze(3).to_broadcast([P, TP, n, CH])
                ap_i = pw_i[:, js, 0:n].unsqueeze(3).to_broadcast([P, TP, n, CH])
                tv = tmp[0][:, 0:TP * n * CH].rearrange("p (j n c) -> p j n c", n=n, c=CH)
                cmul(bp[:, 0].rearrange("p j (n c) -> p j n c", c=CH), bp[:, 1].rearrange("p j (n c) -> p j n c", c=CH),
                     ap_r, ap_i, bb[:, 0].unsqueeze(2).to_broadcast([P, TP, n, CH]),
                     bb[:, 1].unsqueeze(2).to_broadcast([P, TP, n, CH]), tv)
                mark(s_("bp_ready"))
                n = CHUNK + 1
                ap_r = pw_r[:, js, 0:n].unsqueeze(3).to_broadcast([P, TP, n, CH])
                ap_i = pw_i[:, js, 0:n].unsqueeze(3).to_broadcast([P, TP, n, CH])
                tv = tmp[0][:, 0:TP * n * CH].rearrange("p (j n c) -> p j n c", n=n, c=CH)
                cmul(cp[:, 0].rearrange("p j (n c) -> p j n c", c=CH), cp[:, 1].rearrange("p j (n c) -> p j n c", c=CH),
                     ap_r, ap_i, cT[:, 0].unsqueeze(2).to_broadcast([P, TP, n, CH]),
                     cT[:, 1].unsqueeze(2).to_broadcast([P, TP, n, CH]), tv, neg_i=True)
                mark(s_("cp_ready"))
                for a_ in range(TP // 2):
                    evac(("bT", t, a_), bT[:, 2 * a_:2 * a_ + 2].rearrange("p j r n -> p (j r n)"),
                         bank(("bT", t, a_))[:, :])
                sync()
                mark(s_("bT_ready"))
                for a_ in range(TG // 4):
                    if t and a_ == 0:
                        dve.wait_ge(s_("toep_in"), 16 * CHUNK * t)
                    evac(("K", t, a_), kern[:, same_side(a_)[0]:same_side(a_)[-1] + 1:2, :],
                         bank(("K", t, a_))[0:CH, :].rearrange("p (g n) -> p g n", g=4))
                    sync()
                    mark(s_("kern_ready"))
                w_r, w_i, s0, s1 = (s5s[:, n_, js] for n_ in (X1, TH, T0, T1))
                do(V.tensor_copy(w_r, s5s[:, UR, js]))
                do(V.tensor_copy(w_i, s5s[:, UI, js]))
                do(V.tensor_copy(decay[:], s5s[:, R8, js].unsqueeze(2).to_broadcast([P, TP, NCH])))
                sync()
                do(V.memset(decay[:, :, 0:1], 0.0))
                m = 1
                while m < NCH:
                    tv = tmp[0][:, 0:TP * m].rearrange("p (j m) -> p j m", m=m)
                    cmul(e_r[:, :, m:2 * m], e_i[:, :, m:2 * m], w_r.unsqueeze(2).to_broadcast([P, TP, m]),
                         w_i.unsqueeze(2).to_broadcast([P, TP, m]), e_r[:, :, 0:m], e_i[:, :, 0:m], tv)
                    square(w_r, w_i, s0, s1)
                    m *= 2
                for a_ in range((TP + 2) // 3):
                    n = min(3, TP - 3 * a_)
                    full(dve, ("V", t, a_))
                    src = bank(("V", t, a_))[:, 0:n * 2 * (NCH + NB)].rearrange("p (j r k) -> p j r k", r=2, k=NCH + NB)
                    do(V.tensor_copy(v[:, 0, 3 * a_:3 * a_ + n], src[:, :, 0, :]))
                    freed(own, V.tensor_copy(v[:, 1, 3 * a_:3 * a_ + n], src[:, :, 1, :]), ("V", t, a_))
                sync()
                w_ = [tmp[n_][:, 0:TP * NCH].rearrange("p (j k) -> p j k", k=NCH) for n_ in range(3)]
                cmul(w_[0], w_[1], e_r[:], e_i[:], v[:, 0, :, 0:NCH], v[:, 1, :, 0:NCH], w_[2], conj=True)
                flat = [tmp[n_][:, 0:TP * NCH] for n_ in range(2)]
                dflat = decay[:].rearrange("p j k -> p (j k)")
                g_ = tmp[2][:, 0:TP * NCH]
                g2 = tmp[0][:, TP * NCH:2 * TP * NCH]
                do(V.tensor_tensor_scan(g_, dflat, flat[0], 0.0, ALU.mult, ALU.add))
                do(V.tensor_tensor_scan(g2, dflat, flat[1], 0.0, ALU.mult, ALU.add))
                sync()
                g2v = g2.rearrange("p (j k) -> p j k", k=NCH)
                cmul(hp[:, 0, :, NB + 1:], hp[:, 1, :, NB + 1:], e_r[:], e_i[:], w_[2], g2v, w_[1])
                hT = h0[:].rearrange("p r b j -> p r j b")
                for ri in range(2):
                    do(V.tensor_copy(hp[:, ri, :, 0:NB], hT[:, ri, js, :]))
                sync()
                mark(s_("hp_ready"))
                fT = hfin[:].rearrange("p r b j -> p r j b")
                a_r = pw_r[:, js, 1:2].to_broadcast([P, TP, NB])
                a_i = pw_i[:, js, 1:2].to_broadcast([P, TP, NB])
                tv = tmp[0][:, 0:TP * NB].rearrange("p (j b) -> p j b", b=NB)
                cmul(fT[:, 0, js, 1:], fT[:, 1, js, 1:], a_r, a_i, hT[:, 0, js, :], hT[:, 1, js, :], tv)
                for ri in range(2):
                    tt(fT[:, ri, js, 1:], fT[:, ri, js, 1:], v[:, ri, :, NCH:], ALU.add)
                    do(V.tensor_copy(fT[:, ri, js, 0:1], hp[:, ri, :, NB + NCH:]))
                if t:
                    dve.wait_ge(s_("y_out"), 16 * 9 * t)
                for a_ in range(TG // 4):
                    evac(("Y", t, a_), yb[:, same_side(a_)[0]:same_side(a_)[-1] + 1:2, :],
                         bank(("Y", t, a_))[:, 0:4 * (NB + NCH)].rearrange("p (g n) -> p g n", g=4))
                    sync()
                    mark(s_("yb_ready"))
                dve.wait_ge(s_("yz_in"), 16 * (t + 1))
                for m in range(2):
                    k = 2 * t + m
                    do(V.scalar_tensor_tensor(y[:, k, :], y[:, k, :], gain("dskip", k), yz[:, m, :], ALU.mult, ALU.add))
                sync()
                mark(s_("yz_used"))
            mark(s_("hfin_ready"))
            for ri in range(2):
                full(dve, ("fin", ri))
                freed(own, V.tensor_copy(hout[:, ri].rearrange("p a n -> p (a n)"), bank(("fin", ri))[0:108, 0:256]),
                      ("fin", ri))
                sync()
                mark(s_("hout_ready"))
            dve.wait_ge(s_("stored"), 16 * 10)
            dve.wait_ge(s_("gelu_made"), THIRDS)
            mark(s_("x_free"))

            def time_order(tile):
                return tile[:, 0:T].rearrange("p (j k) -> p k j", j=CHUNK)

            for k in range(KS):
                stat[1] += 2
                dve.wait_ge(s_("xhi_made"), stat[1])
                for c, (dst, srcv) in enumerate((
                        (slice(0, T), time_order(y[:, k, :])), (slice(T, NT), y[:, k, T:NT]))):
                    h = x_hi[:, k, dst].bitcast(F32)
                    o = x_lo[:, k, dst]
                    if c == 0:
                        h = h.rearrange("p (k j) -> p k j", j=CHUNK)
                        o = o.rearrange("p (k j) -> p k j", j=CHUNK)
                    tell(V.tensor_tensor(o, srcv, h, ALU.subtract), s_("xlo_made"), stat[1] - 1 + c)
            for m in range(KS):
                q = PH["glu"][2] + m
                dve.wait_ge(panel_done, q + 1)
                do(V.tensor_scalar(gate[:, m, 0:264], big[2 * (q % 2)][:, 0:264], gain("bglu", m), None, ALU.add, ALU.bypass))
                tell(V.tensor_scalar(gate[:, m, 264:NT], big[2 * (q % 2) + 1][:, 0:256], gain("bglu", m), None,
                                     ALU.add, ALU.bypass), panel_read, q + 1)
            sync()
            mark(s_("gate_ready"))
            for m in range(KS):
                dve.wait_ge(s_("sig_made"), m + 1)
                gt = gate[:, m, 0:T].rearrange("p (k j) -> p k j", j=CHUNK)
                do(V.tensor_tensor(gt, gt, time_order(y[:, m, :]), ALU.mult))
                do(V.tensor_tensor(gate[:, m, T:NT], gate[:, m, T:NT], y[:, m, T:NT], ALU.mult))
                sync()
                mark(s_("gated"))
                split_lo(m, gate[:, m, :], None, None)

            def mem_attention(l, m_):
                qm = y[:, 6:8, :]
                m = m_
                for a_ in range(2):
                    evac(("qrow", l, a_), qrow[:, 512 * a_:512 * a_ + 512], bank(("qrow", l, a_))[0:NB, :])
                sync()
                mark(s_("qrow_ready"))
                for h in range(MEMH):
                    for a_ in range(2):
                        n = 8 * l + 2 * h + a_
                        full(dve, ("mS", l, h, a_))
                        if n >= 2:
                            prev = ("mT", l, (2 * h + a_ - 2) // 2, a_) if 2 * h + a_ >= 2 else ("mT", 0, 3, a_)
                            full(dve, prev)
                        st = m["st"][:, a_, :]
                        do(V.tensor_reduce(st[:, 0:2], bank(("mS", l, h, a_))[:].rearrange("p (q k) -> p q k", q=2),
                                           AX.X, ALU.max))
                        sync()
                        tell(V.tensor_scalar(st[:, 2:4], st[:, 0:2], -SCALE, None, ALU.mult, ALU.bypass),
                             s_("mneg"), n + 1)
                        dve.wait_ge(s_("mexp"), n + 1)
                        do(V.reciprocal(st[:, 6:8], st[:, 4:6]))
                        sync()
                        for qq in range(2):
                            pp = m["p"][:, a_, qq, :]
                            do(V.tensor_scalar(pp, pp, st[:, 6 + qq:7 + qq], None, ALU.mult, ALU.bypass))
                        sync()
                        mark(s_("mp_ready"))
                    for a_ in range(2):
                        if h and a_ == 0:
                            full(dve, ("mO", l, h - 1))
                        evac(("mT", l, h, a_), m["pT"][:, :, 256 * a_:256 * a_ + 256],
                             bank(("mT", l, h, a_))[:].rearrange("p (k q) -> p k q", k=2))
                    sync()
                    mark(s_("mpT_ready"))
                    full(dve, ("mO", l, h))
                    r = slice(DH * (h % 2), DH * (h % 2) + DH)
                    src = bank(("mO", l, h))[r, :]
                    do(V.tensor_copy(x_hi[r, 6 + h // 2, 0:T], src))
                    sync()
                    freed(own, V.tensor_tensor(x_lo[r, 6 + h // 2, 0:T], src,
                                               x_hi[r, 6 + h // 2, 0:T].bitcast(F32), ALU.subtract), ("mO", l, h))
                for b in range(NB):
                    dve.wait_ge(s_(f"mk_in{b % 2}"), 16 * (4 * l + b // 2 + 1))
                    full(dve, ("mq", l, b))
                    q_b = bank(("mq", l, b))[:, 0:256].unsqueeze(1).to_broadcast([P, 2, 256])
                    ins = V.tensor_tensor(m["prod"][:], m["k"][:, b % 2], q_b, ALU.mult)
                    freed(own, ins, ("mq", l, b))
                    sync()
                    tell(V.tensor_reduce(m["s"][:, b], m["prod"][:].rearrange("p c (h d) -> p c h d", d=DH), AX.X,
                                         ALU.add), s_("mk_used"), NB * l + b + 1)
                    sync()
                sv = m["s"][:].rearrange("p b c h -> p (b c h)")
                do(V.tensor_scalar(sv, sv, SCALE, None, ALU.mult, ALU.bypass))
                sync()
                decode_softmax(m["s"], m["dst"], MEMH, 2, ("mmaxT", l), ("mmax", l), ("mden", l), l)
                full(dve, ("mpv", l))
                pv = bank(("mpv", l))[:, 0:NB * 2 * 2].rearrange("p (b f e) -> p f b e", f=2, e=2)
                for e in range(2):
                    r = slice(DH * e, DH * e + DH)
                    do(V.tensor_copy(x_hi[r, 6:8, T:NT], pv[r, :, :, e]))
                sync()
                for e in range(2):
                    r = slice(DH * e, DH * e + DH)
                    ins = V.tensor_tensor(x_lo[r, 6:8, T:NT], pv[r, :, :, e], x_hi[r, 6:8, T:NT].bitcast(F32),
                                          ALU.subtract)
                    if e == 0:
                        do(ins)
                freed(own, ins, ("mpv", l))
                sync()
                mark(s_("mem_done"))

            ndec = [0]

            def decode_softmax(s, st, H, pgs, jT, jM, jD, l):
                BH = NB * H
                n = ndec[0] = ndec[0] + 1
                m1, mx, dg, sm, inv = (st[:, k_, 0:BH] for k_ in range(5))
                do(V.tensor_reduce(m1.rearrange("p (b h) -> p b h", h=H), s[:].rearrange("p b g h -> p b h g"),
                                   AX.X, ALU.max))
                sync()
                mark(s_("dmax1"))
                full(dve, jT)
                freed(own, V.tensor_reduce(mx[0:BH, 0:1], bank(jT)[0:BH, 0:P], AX.X, ALU.max), jT)
                sync()
                tell(V.tensor_scalar(dg[0:BH, :], ident[0:BH, 0:BH], mx[0:BH, 0:1], None, ALU.mult, ALU.bypass),
                     s_("dmax2"), n)
                full(dve, jM)
                mb_ = bank(jM)[:, 0:BH].rearrange("p (b h) -> p b h", h=H).unsqueeze(2).to_broadcast([P, NB, pgs, H])
                freed(own, V.tensor_tensor(s[:], s[:], mb_, ALU.subtract), jM)
                sync()
                mark(s_("dexp_in"))
                dve.wait_ge(s_("dexp"), n)
                do(V.tensor_reduce(sm.rearrange("p (b h) -> p b h", h=H), s[:].rearrange("p b g h -> p b h g"),
                                   AX.X, ALU.add))
                sync()
                mark(s_("dsum"))
                full(dve, jD)
                freed(own, V.reciprocal(inv, bank(jD)[:, 0:BH]), jD)
                sync()
                iv = inv.rearrange("p (b h) -> p b h", h=H).unsqueeze(2).to_broadcast([P, NB, pgs, H])
                tell(V.tensor_tensor(s[:], s[:], iv, ALU.mult), s_("dp_ready"), n)
                sync()

            mem_attention(0, mb[0])

            npost = [0]

            def post_norm(name, l, nxt, nl):
                sum_squares(KD, NT)
                sums_ready()
                reciprocal_std(rstd, NT)
                for k in range(KD):
                    do(V.scalar_tensor_tensor(y[:, k, :], y[:, k, :], gain(name, k, l), rstd[:], ALU.mult, ALU.mult))
                    sync()
                    npost[0] += 1
                    tell(V.tensor_tensor(x[:, k, :], x[:, k, :], y[:, k, :], ALU.add), s_("x_updated"), npost[0])
                if nxt is not None:
                    pre_norm(nxt, nl)
                    sum_squares(KD, NT)
                    sums_ready()
                    reciprocal_std(rstd, NT)

            def copy_out(ph):
                for m in range(8):
                    q = PH[ph][2] + m
                    dve.wait_ge(panel_done, q + 1)
                    do(V.tensor_copy(y[:, m, 0:264], big[2 * (q % 2)][:, 0:264]))
                    tell(V.tensor_copy(y[:, m, 264:NT], big[2 * (q % 2) + 1][:, 0:256]), panel_read, q + 1)
                sync()
                nproj[0] += 1
                mark(s_("y_full"))

            nproj = [0]

            def ffn(l):
                for f in range(2):
                    _, n, base, _ = PH[f"up{l}{f}"]
                    step0, r = own.n, None
                    K = 10
                    if f == 0:
                        for s in range(2):
                            do(V.memset(uc[s][:, 0:2], 0.0))
                        sync()
                        step0 = own.n
                    done = 22 * l + 11 * f
                    with dve.Fori(0, KH) as it:
                        c = [0]

                        def st(ins):
                            c[0] += 1
                            ins.then_inc(dve_step, 1)

                        def sy():
                            dve.wait_ge(dve_step, it * K + (step0 + c[0]))

                        for half in range(2):
                            q = it * 2 + (base + half)
                            slot = (base + half) % 2
                            fb = it + (f * KH + half * KF)
                            w_ = [convw[:, l, bass.ds(it + (f * KH + half * KF + 44 * tp), 1)] for tp in range(3)]
                            uu, yy = uc[half], yc[half]
                            dve.wait_ge(panel_done, q + 1)
                            st(V.tensor_tensor(uu[:, 2:266], big[2 * slot][:, 0:264], rstd[:, 0:264], ALU.mult))
                            V.tensor_tensor(uu[:, 266:2 + NT], big[2 * slot + 1][:, 0:256], rstd[:, 264:NT],
                                            ALU.mult).then_inc(panel_read, 1)
                            dve.wait_ge(s_("tap_made"), it * 2 + (2 * done + half + 1))
                            st(V.scalar_tensor_tensor(yy[:, 0:T], uu[:, 1:1 + T], w_[1], yy[:, 0:T], ALU.mult, ALU.add))
                            old = convs[:, l, :, bass.ds(it + (f * KH + half * KF), 1)].rearrange(
                                "p (b t) a -> p t (b a)", t=2)
                            st(V.scalar_tensor_tensor(yy[:, T:NT], old[:, 1], w_[1], yy[:, T:NT], ALU.mult, ALU.add))
                            sy()
                            st(V.scalar_tensor_tensor(yy[:, 0:T], uu[:, 0:T], w_[0], yy[:, 0:T], ALU.mult, ALU.add))
                            V.scalar_tensor_tensor(yy[:, T:NT], old[:, 0], w_[0], yy[:, T:NT], ALU.mult,
                                                   ALU.add).then_inc(s_("conv_made"), 1)
                        dve.wait_ge(s_("silu_made"), it + (done + 1))
                        dve.wait_ge(s_("conv_made"), it * 2 + (2 * done + 2))
                        st(V.tensor_tensor(hf[:], sg[:], yc[1][:], ALU.mult))
                        sy()
                        st(V.tensor_copy(h_hi[:, bass.ds(it, 1), :].rearrange("p a t -> p (a t)"), hf[:]))
                        sy()
                        V.tensor_tensor(h_lo[:, bass.ds(it, 1), :].rearrange("p a t -> p (a t)"), hf[:],
                                        h_hi[:, bass.ds(it, 1), :].rearrange("p a t -> p (a t)").bitcast(F32),
                                        ALU.subtract).then_inc(s_("h_made"), 1)
                    own.n = step0 + KH * c[0]
                    assert c[0] == K, c[0]
                    base = PH[f"down{l}{f}"][2]
                    with dve.Fori(0, 4) as it:
                        for half in range(2):
                            slot = (base + half) % 2
                            dve.wait_ge(panel_done, it * 2 + (base + half + 1))
                            for n_, (c0, c1) in enumerate(HALF):
                                dst = y[:, bass.ds(it * 2 + half, 1), c0:c1].rearrange("p a t -> p (a t)")
                                src = big[2 * slot + n_][:, 0:c1 - c0]
                                ins = V.tensor_copy(dst, src) if f == 0 else V.tensor_tensor(dst, dst, src, ALU.add)
                                ins.then_inc(panel_read if n_ else dve_step, 1)
                    own.n += 8
                nproj[0] += 1
                dve.wait_ge(panel_read, base + 8)
                mark(s_("y_full"))
                for a_ in range(KF * 2 // 4):
                    full(dve, ("cout", l, a_))
                    if l and a_ == 0:
                        dve.wait_ge(s_("crows_out"), 32)
                    freed(own, V.tensor_copy(crows[:, 4 * a_:4 * a_ + 4, :].rearrange("r f p -> r (f p)"),
                                             bank(("cout", l, a_))[0:2 + NB, :]), ("cout", l, a_))
                    sync()
                    mark(s_("crows_ready"))

            copy_out("wout0")
            post_norm("mix_post", 0, "ffn_pre", 0)
            ffn(0)
            post_norm("ffn_post", 0, "kv", 0)

            dve.wait_ge(s_("crows_out"), 32)
            do(V.memset(qh[DH:DH + 2, :, :], 1.0))
            do(V.memset(kh[DH:DH + 2, :, :], 1.0))
            mark(s_("kh_clear"))
            for m in range(12):
                q = PH["kv"][2] + m
                if m:
                    full(dve, ("kvsamp", m - 1))
                    if m <= 6:
                        dve.wait_ge(s_("kh_made"), m)
                read_panel(q, lambda n, c0, c1: kvT[:, c0:c1])
                sync()
                mark(s_("kvT_ready"))
                if m < 6 and m >= 2:
                    dve.wait_ge(s_(f"ktok_out{m % 2}"), 16 * (m // 2))
                dst = ktok[m % 2][:] if m < 6 else vtok[:, :, (m - 6) * P:(m - 5) * P]
                evac(("kvtok", m), dst, bank(("kvtok", m))[:].rearrange("p (c f) -> p c f", c=4))
                sync()
                mark(s_("ktok_ready" if m < 6 else "vtok_ready"))
                evac(("kvsamp", m), kvs[:, m // 6, (m % 6) * P:(m % 6 + 1) * P], bank(("kvsamp", m))[0:NB, 0:P])
                sync()
                mark(s_("kvs_ready"))
            q = PH["kvf"][2]
            dve.wait_ge(panel_done, q + 1)
            z_, m_, l_ = lf[:, 0, :], lf[:, 1, :], lf[:, 2, :]
            do(V.tensor_tensor(z_[:, 0:264], big[2 * (q % 2)][0:HEADS, 0:264], rstd[0:HEADS, 0:264], ALU.mult))
            tell(V.tensor_tensor(z_[:, 264:NT], big[2 * (q % 2) + 1][0:HEADS, 0:256], rstd[0:HEADS, 264:NT], ALU.mult),
                 panel_read, q + 1)
            sync()
            dve.wait_ge(s_("bf_in"), 16)
            ts(z_, z_, bf[:, 0:1], None, ALU.add, ALU.bypass)
            ts(m_, z_, -1.0, None, ALU.mult, ALU.bypass)
            tell(V.tensor_tensor(m_, m_, z_, ALU.min), s_("nabs_ready"), 1)
            dve.wait_ge(s_("log_made"), 1)
            tell(V.scalar_tensor_tensor(m_, z_, 0.0, l_, ALU.min, ALU.subtract), s_("lf_ready"), 1)
            sync()
            do(V.memset(z_, 1.0))
            sync()
            do(V.tensor_tensor_scan(l_[:, 0:T], z_[:, 0:T], m_[:, 0:T], 0.0, ALU.mult, ALU.add))
            sync()
            do(V.tensor_scalar(lf[:, 0, 0:T], l_[:, 0:T], -1.0 / SCALE, None, ALU.mult, ALU.bypass))
            sync()
            do(V.tensor_scalar(l_[:, 0:T], l_[:, 0:T], 1.0 / SCALE, None, ALU.mult, ALU.bypass))
            sync()
            for n in range(3):
                mark(s_("c_ready"))
            full(dve, ("logf",))
            do(V.tensor_copy(lft[:, 0:4, :], bank(("logf",))[:, 0:48].rearrange("p (c h) -> p c h", h=HEADS)))
            freed(own, V.tensor_copy(lfs[:], bank(("logf",))[0:NB, 48:60]), ("logf",))
            sync()
            for n in range(2):
                mark(s_("logf_ready"))

            pre_norm("mix_pre", 1)
            for m in range(8):
                q = PH["win1"][2] + m
                slot = q % 2
                dve.wait_ge(panel_done, q + 1)
                if m < 6:
                    for n, (c0, c1) in enumerate(HALF):
                        e1 = min(c1, T)
                        for e in range(2):
                            r = slice(DH * e, DH * e + DH)
                            do(V.tensor_tensor(qh[0:DH, 2 * m + e, c0:e1], big[2 * slot + n][r, 0:e1 - c0],
                                               rstd[r, c0:e1], ALU.mult))
                    tell(V.tensor_tensor(qs[:, m, :], big[2 * slot + 1][:, 248:256], rstd[:, T:NT], ALU.mult),
                         panel_read, q + 1)
                else:
                    do(V.tensor_tensor(y[:, m, 0:264], big[2 * slot][:, 0:264], rstd[:, 0:264], ALU.mult))
                    tell(V.tensor_tensor(y[:, m, 264:NT], big[2 * slot + 1][:, 0:256], rstd[:, 264:NT], ALU.mult),
                         panel_read, q + 1)
            sync()
            mark(s_("q1_ready"))

            for h in range(HEADS):
                for qi in range(4):
                    n = 4 * h + qi
                    N = (qi + 1) * P
                    s, st = bank(("fS", h, qi)), pst[:, 4 * (n % 2):4 * (n % 2) + 4]
                    full(dve, ("fS", h, qi))
                    do(V.tensor_tensor(s[:, qi * P:N], s[:, qi * P:N], causal[:], ALU.add))
                    sync()
                    do(V.tensor_reduce(st[:, 0:1], s[:, 0:N], AX.X, ALU.max))
                    sync()
                    tell(V.tensor_scalar(st[:, 1:2], st[:, 0:1], -SCALE, None, ALU.mult, ALU.bypass), s_("fneg"), n + 1)
                    dve.wait_ge(s_("fexp"), n + 1)
                    do(V.reciprocal(st[:, 3:4], st[:, 2:3]))
                    sync()
                    tell(V.tensor_scalar(pa[:, 0:N], pa[:, 0:N], st[:, 3:4], None, ALU.mult, ALU.bypass),
                         s_("pa_ready"), n + 1)
                    full(dve, ("fT", h, qi))
                    freed(own, V.tensor_copy(paT[:, 0:N], bank(("fT", h, qi))[:, 0:N]), ("fT", h, qi))
                    sync()
                    mark(s_("paT_ready"))
                    full(dve, ("fO", h, qi))
                    r = slice(DH * (h % 2), DH * (h % 2) + DH)
                    src, cc = bank(("fO", h, qi))[r, 0:P], slice(qi * P, qi * P + P)
                    if n == 0:
                        dve.wait_ge(panel_done, PH["win1"][2] + 8)
                    do(V.tensor_copy(x_hi[r, h // 2, cc], src))
                    sync()
                    freed(own, V.tensor_tensor(x_lo[r, h // 2, cc], src, x_hi[r, h // 2, cc].bitcast(F32),
                                               ALU.subtract), ("fO", h, qi))
            sync()
            mark(s_("heads_done"))
            mem_attention(1, mb[1])

            BH = NB * HEADS
            s6 = sc[:].rearrange("p b g h -> p g b h")
            dve.wait_ge(s_("logf_in"), 16 * NB * PAGES)
            do(V.memset(sc[:], NEG))
            do(V.memset(pre[:, :, 0, :], 0.0))
            sync()
            for pg in range(1, PAGES):
                tt(pre[:, :, pg, :], pre[:, :, pg - 1, :], logf[:, :, pg - 1, :], ALU.add)
            tot = fst[:, 5, 0:BH].rearrange("p (b h) -> p b h", h=HEADS)
            tt(tot, pre[:, :, PAGES - 1, :], logf[:, :, PAGES - 1, :], ALU.add)
            idb = ident[0:NB, 0:NB].unsqueeze(2).to_broadcast([NB, NB, HEADS])
            tt(lmask[:], idb, lfs[:].unsqueeze(1).to_broadcast([NB, NB, HEADS]), ALU.mult)
            mark(s_("pre_ready"))
            full(dve, ("dtot",))
            freed(own, V.tensor_copy(fst[:, 6, 0:BH], bank(("dtot",))[:, 0:BH]), ("dtot",))
            sync()
            cq = fst[:, 6, 0:BH].rearrange("p (b h) -> p b h", h=HEADS)
            for a_ in range(2):
                full(dve, ("dc", a_))
                bs = slice(4 * a_, 4 * a_ + 4)
                src = bank(("dc", a_))[:, 0:384].rearrange("p (b g h) -> p b g h", b=4, h=HEADS)
                freed(own, V.tensor_tensor(pre[:, bs], cq[:, bs].unsqueeze(2).to_broadcast([P, 4, PAGES, HEADS]), src,
                                           ALU.subtract), ("dc", a_))
            sync()
            for b in range(NB):
                for a_ in range(2):
                    full(dve, ("fq", b, a_))
                    freed(own, V.tensor_copy(qb[b % 2][:, 384 * a_:384 * a_ + 384], bank(("fq", b, a_))[:, 0:384]),
                          ("fq", b, a_))
                sync()
                for pg in range(PAGES):
                    n = b * PAGES + pg
                    dve.wait_ge(s_(f"page_in{n % NPG}"), 16 * (n // NPG + 1))
                    do(V.tensor_tensor(prod[:], page[n % NPG][:], qb[b % 2][:], ALU.mult))
                    sync()
                    tell(V.tensor_reduce(sc[:, b, pg, :], prod[:].rearrange("p (h d) -> p h d", d=DH), AX.X, ALU.add),
                         s_("k_used"), n + 1)
                    sync()
                do(V.tensor_tensor(prod[0:NB, :], kvs[:, 0, :], qb[b % 2][0:NB, :], ALU.mult))
                sync()
                do(V.tensor_reduce(fst[0:NB, 7, 0:HEADS], prod[0:NB, :].rearrange("p (h d) -> p h d", d=DH),
                                   AX.X, ALU.add))
                sync()
                do(V.tensor_scalar(fst[0:NB, 7, 12:13], ident[0:NB, b:b + 1], SCALE, None, ALU.mult, ALU.bypass))
                do(V.tensor_scalar(fst[0:NB, 7, 13:14], ident[0:NB, b:b + 1], -NEG, NEG, ALU.mult, ALU.add))
                sync()
                do(V.tensor_scalar(sc[0:NB, b, PAGES, :], fst[0:NB, 7, 0:HEADS], fst[0:NB, 7, 12:13],
                                   fst[0:NB, 7, 13:14], ALU.mult, ALU.add))
                sync()
            do(V.scalar_tensor_tensor(sc[:, :, 0:PAGES, :].rearrange("p b g h -> p b (g h)"),
                                      sc[:, :, 0:PAGES, :].rearrange("p b g h -> p b (g h)"), SCALE,
                                      pre[:].rearrange("p b g h -> p b (g h)"), ALU.mult, ALU.add))
            sync()
            decode_softmax(sc, fst, HEADS, PAGES + 1, ("fmaxT",), ("fmax",), ("fden",), 1)
            for b in range(NB):
                full(dve, ("fpv", b))
                pv = bank(("fpv", b))[:, 0:12].rearrange("p (f e) -> p f e", e=2)
                for e in range(2):
                    r = slice(DH * e, DH * e + DH)
                    do(V.tensor_copy(x_hi[r, 0:6, T + b:T + b + 1], pv[r, :, e:e + 1]))
                sync()
                for e in range(2):
                    r = slice(DH * e, DH * e + DH)
                    ins = V.tensor_tensor(x_lo[r, 0:6, T + b:T + b + 1], pv[r, :, e:e + 1],
                                          x_hi[r, 0:6, T + b:T + b + 1].bitcast(F32), ALU.subtract)
                    if e == 0:
                        do(ins)
                freed(own, ins, ("fpv", b))
            sync()
            mark(s_("fox_done"))
            dve.wait_ge(s_("stored"), 16 * 16)
            copy_out("wout1")
            post_norm("mix_post", 1, "ffn_pre", 1)
            ffn(1)
            post_norm("ffn_post", 1, None, 0)
            dve.wait_ge(s_("crows_out"), 64)
            for c in range(5):
                rows_ = P if c < 4 else NB
                if c >= 2:
                    dve.wait_ge(s_(f"ytok_out{c % 2}"), 16 * (c // 2))
                for a_ in range(2):
                    evac(("yT", c, a_), ytok[c % 2][0:rows_, 512 * a_:512 * a_ + 512], bank(("yT", c, a_))[0:rows_, :])
                    sync()
                    mark(s_("ytok_ready"))

        @block.scalar
        def _(act):
            own = Own(act, act_step)
            do, tell, sync, mark = own.do, own.tell, own.sync, own.mark
            A = act
            stat = [0, 0, 0]

            def hi(kb, half_c, it=None):
                slot = half_c % 2
                if it is None:
                    q, loads = half_c, half_c // 2 + 1
                else:
                    q, loads = it * 2 + half_c, it + (half_c // 2 + 1)
                act.wait_ge(raw_loaded[slot], loads * 16)
                if it is not None or q >= 2:
                    act.wait_ge(panel_done, q - 1)
                A.activation(w_hi[slot][:, 0:kb, :], raw[slot][:, 0:kb, :], ACT.Copy).then_inc(hi_made, 1)

            def run(name, work=None, ahead=True, started=True):
                kb, n, base, nxt = PH[name]
                work = work or (lambda it, half: None)
                if not started:
                    hi(kb, base)
                pairs = n // 2
                unrolled = base < 2 or pairs < 2
                if not unrolled:
                    with act.Fori(0, pairs - 1) as it:
                        for half in range(2):
                            hi(kb, base + half + 1, it)
                            work(it, half)
                for i in range(0 if unrolled else n - 2, n):
                    if i + 1 < n:
                        hi(kb, base + i + 1)
                    elif ahead:
                        hi(PH[nxt][0], base + n)
                    work(i // 2, i % 2)

            def squares(count, src, cols, ready):
                for k in range(count):
                    ready(k)
                    n = stat[0]
                    if n >= 2:
                        act.wait_ge(s_("sq_used"), n - 1)
                    stat[0] += 1
                    tell(A.activation(sq[:, n % 2, 0:cols], src(k), ACT.Square), s_("sq_made"), n + 1)

            def root(jobs):
                if stat[2]:
                    act.wait_ge(s_("rstd_ready"), stat[2])
                for job, c0, c1 in jobs:
                    full(act, job)
                    freed(own, A.activation(sd[:, c0:c1], bank(job)[:, 0:c1 - c0], ACT.Sqrt, bias=eps[:, 0:1]), job)
                stat[2] += 1
                mark(s_("root_made"))

            def root_x(name):
                root([(("ms", name, n), c0, c1) for n, (c0, c1) in enumerate(HALF)])

            def split_hi(k, src, g=None, cols=slice(0, NT)):
                stat[1] += 1
                o = x_hi[:, k, cols]
                if len(src.shape) == 3:
                    o = o.rearrange("p (k j) -> p k j", j=CHUNK)
                ins = A.activation(o, src, ACT.Copy, scale=1.0 if g is None else g)
                tell(ins, s_("xhi_made"), stat[1])

            hi(KD, 0)
            act.wait_ge(s_("mem_ready"), 1)
            squares(KD, lambda k: memT[:, k, :], NMEM, lambda k: None)
            for l in range(2):
                for k in range(KD):
                    split_hi(k, memT[:, k, :], gain("mem", k, l), slice(l * NMEM, (l + 1) * NMEM))
            root([(("ms_mem",), 0, NMEM)])
            run("memkv0")
            run("memkv1")
            act.wait_ge(s_("x_ready"), 1)
            squares(KD, lambda k: x[:, k, :], NT, lambda k: None)
            act.wait_ge(panel_done, 8)
            for k in range(KD):
                split_hi(k, x[:, k, :], gain("mix_pre", k, 0))
            root_x("x0")
            run("win0", ahead=False)

            act.wait_ge(s_("lam_ready"), 1)
            tell(A.activation(lam[:, 64:64 + PAIRS], lam[:, 64:64 + PAIRS], ACT.Exp), s_("s5_act"), 1)
            act.wait_ge(s_("angles_ready"), 1)
            for n, (dst, src, fn, sca) in enumerate((
                    (3, 1, ACT.Exp, 1.0), (6, 1, ACT.Exp, 8.0), (4, 12, ACT.Sin, 1.0), (5, 13, ACT.Sin, 1.0))):
                tell(A.activation(s5s[:, dst, :], s5s[:, src, :], fn, scale=sca), s_("s5_act"), n + 2)
            for t in range(THIRDS):
                act.wait_ge(s_("yz_used"), t + 1)
                for m in range(2):
                    k = 2 * t + m
                    do(A.activation(y[:, k, :], y[:, k, :], ACT.Gelu_apprx_tanh))
                mark(s_("gelu_made"))
            act.wait_ge(s_("x_free"), 1)
            for k in range(KS):
                split_hi(k, y[:, k, 0:T].rearrange("p (j k) -> p k j", j=CHUNK), None, slice(0, T))
                split_hi(k, y[:, k, T:NT], None, slice(T, NT))
            run("glu", ahead=False, started=False)
            act.wait_ge(s_("gate_ready"), 1)
            for m in range(KS):
                tell(A.activation(gate[:, m, :], gate[:, m, :], ACT.Sigmoid), s_("sig_made"), m + 1)
            for m in range(KS):
                act.wait_ge(s_("gated"), m + 1)
                split_hi(m, gate[:, m, :])

            def mem_attention(l, m):
                for h in range(MEMH):
                    for a_ in range(2):
                        n = 8 * l + 2 * h + a_
                        act.wait_ge(s_("mneg"), n + 1)
                        for qq in range(2):
                            st = m["st"][:, a_, :]
                            ins = A.activation(m["p"][:, a_, qq, :], bank(("mS", l, h, a_))[:, 256 * qq:256 * qq + 256],
                                               ACT.Exp, bias=st[:, 2 + qq:3 + qq], scale=SCALE,
                                               accum_out=st[:, 4 + qq:5 + qq])
                            if qq:
                                freed(own, ins, ("mS", l, h, a_))
                            else:
                                do(ins)
                        mark(s_("mexp"))
                act.wait_ge(s_("dexp_in"), 1 if l == 0 else 2)
                tell(A.activation(m["s"][:], m["s"][:], ACT.Exp), s_("dexp"), 1 if l == 0 else 2)

            mem_attention(0, mb[0])
            ny = [0]

            def post(name, post_name, l, nxt, nl):
                ny[0] += 1
                act.wait_ge(s_("y_full"), ny[0])
                squares(KD, lambda k: y[:, k, :], NT, lambda k: None)
                root_x(f"{post_name}{l}")
                if nxt is not None:
                    for k in range(KD):
                        act.wait_ge(s_("x_updated"), 8 * (ny[0] - 1) + k + 1)
                        split_hi(k, x[:, k, :], gain(nxt, k, nl))
                    squares(KD, lambda k: x[:, k, :], NT, lambda k: None)
                    root_x(name)

            def ffn(l):
                for f in range(2):
                    base = PH[f"up{l}{f}"][2]
                    done = 22 * l + 11 * f

                    def work(it, half):
                        fb = it + (f * KH + half * KF)
                        uu, yy = uc[half], yc[half]
                        act.wait_ge(panel_read, it * 2 + (base + half + 1))
                        A.activation(newconv[:, bass.ds(fb, 1), :].rearrange("p a t -> p (a t)"),
                                     uu[:, T:T + 2 + NB], ACT.Copy).then_inc(act_step, 1)
                        act.wait_ge(s_("h_made"), it + (done + 1))
                        A.activation(yy[:], uu[:, 2:2 + NT], ACT.Identity,
                                     bias=convw[:, l, bass.ds(it + (f * KH + half * KF + 132), 1)],
                                     scale=convw[:, l, bass.ds(it + (f * KH + half * KF + 88), 1)]
                                     ).then_inc(s_("tap_made"), 1)
                        if half == 1:
                            act.wait_ge(s_("conv_made"), it * 2 + (2 * done + 1))
                            A.activation(sg[:], yc[0][:], ACT.Silu).then_inc(s_("silu_made"), 1)

                    run(f"up{l}{f}", work)
                    run(f"down{l}{f}", ahead=(f == 0))
                    own.n += 22

            run("wout0", ahead=False, started=False)
            post("f0", "o", 0, "ffn_pre", 0)
            hi(KD, PH["up00"][2])
            ffn(0)
            post("x1", "d", 0, "kv", 0)

            def kv_work(m):
                act.wait_ge(s_("kvT_ready"), m + 1)
                if m == 0:
                    act.wait_ge(s_("kh_clear"), 1)
                if m < 6:
                    do(A.activation(kh[0:DH, 2 * m, :], kvT[0:DH, 0:T], ACT.Copy))
                    tell(A.activation(kh[0:DH, 2 * m + 1, :], kvT[DH:P, 0:T], ACT.Copy), s_("kh_made"), m + 1)

            kb, n, base, _ = PH["kv"]
            hi(kb, base)
            for m in range(n):
                hi(KD, base + m + 1)
                kv_work(m)
            act.wait_ge(s_("nabs_ready"), 1)
            do(A.activation(lf[:, 2, :], lf[:, 1, :], ACT.Exp))
            sync()
            tell(A.activation(lf[:, 2, :], lf[:, 2, :], ACT.Ln, bias=1.0), s_("log_made"), 1)
            act.wait_ge(panel_done, PH["kvf"][2] + 1)
            for k in range(KD):
                split_hi(k, x[:, k, :], gain("mix_pre", k, 1))
            run("win1", ahead=False, started=False)
            for s in range(2):
                act.wait_ge(s_(f"ktok_out{s}"), 48)
            for n in range(4 * HEADS):
                h, qi = n // 4, n % 4
                N = (qi + 1) * P
                st = pst[:, 4 * (n % 2):4 * (n % 2) + 4]
                act.wait_ge(s_("fneg"), n + 1)
                if n:
                    full(act, ("fT", (n - 1) // 4, (n - 1) % 4))
                freed(own, A.activation(pa[:, 0:N], bank(("fS", h, qi))[:, 0:N], ACT.Exp, bias=st[:, 1:2], scale=SCALE,
                                        accum_out=st[:, 2:3]), ("fS", h, qi))
                mark(s_("fexp"))
            mem_attention(1, mb[1])
            act.wait_ge(s_("dexp_in"), 3)
            tell(A.activation(sc[:], sc[:], ACT.Exp), s_("dexp"), 3)
            run("wout1", ahead=False, started=False)
            post("f1", "o", 1, "ffn_pre", 1)
            hi(KD, PH["up10"][2])
            ffn(1)
            post("", "d", 1, None, 0)

        @block.tensor
        def _(pe):
            def kv_turn(m):
                pe.wait_ge(s_("kvT_ready"), m + 1)
                o = take(("kvtok", m))
                for c in range(4):
                    ins = turn(o[:, c * P:c * P + P], kvT[:, c * P:c * P + P], P)
                give(ins, ("kvtok", m))
                give(turn(take(("kvsamp", m))[0:NB, 0:P], kvT[:, T:NT], P), ("kvsamp", m))

            order = [0]

            def take(job):
                j = J[job]
                assert j == order[0], (job, j, order[0])
                order[0] += 1
                if j >= 4:
                    pe.wait_ge(misc_free[j % 4], j // 4)
                return bank(job)

            def give(ins, job):
                ins.then_inc(misc_full[J[job] % 4], 1)

            def product(q, slot, kb, rhs, cols, wait_k=None, free=True):
                pe.wait_ge(lo_made, q + 1)
                if free:
                    pe.wait_ge(panel_read, q - 1)
                for k in range(kb):
                    if wait_k is not None:
                        wait_k(k)
                    xh, xl = rhs(k)
                    for n_, (w, r) in enumerate(((w_hi, xh), (w_hi, xl), (w_lo, xh))):
                        for b_, (c0, c1) in enumerate(cols):
                            ins = pe.matmul(big[2 * slot + b_][:, 0:c1 - c0], w[slot][:, k, :], r[:, c0:c1],
                                            start=(k == 0 and n_ == 0), stop=(k == kb - 1 and n_ == 2))
                ins.then_inc(panel_done, 1)

            xs_ = lambda k: (x_hi[:, k, :], x_lo[:, k, :])

            def phase(name, rhs=xs_, cols=HALF, wait_k=None):
                kb, n, base, _ = PH[name]
                peel = 2 if wait_k is not None else 0
                if base < 2 or n <= 2:
                    peel = n
                for i in range(peel):
                    product(base + i, (base + i) % 2, kb, rhs, cols, wait_k if i == 0 else None, base + i >= 2)
                if n > peel:
                    with pe.Fori(0, (n - peel) // 2) as it:
                        for half in range(2):
                            c = base + peel + half
                            product(it * 2 + c, c % 2, kb, rhs, cols)

            nsplit = [0]

            def x_split(k):
                pe.wait_ge(s_("xlo_made"), nsplit[0] + k + 1)

            nsums = [0]

            def stats(jobs):
                nsums[0] += 1
                pe.wait_ge(s_("sumsq_ready"), nsums[0])
                for job, c0, c1 in jobs:
                    o = take(job)
                    give(pe.matmul(o[:, 0:c1 - c0], meanw[:], sumsq[:, c0:c1], start=True, stop=True), job)

            def stats_x(name):
                stats([(("ms", name, n), c0, c1) for n, (c0, c1) in enumerate(HALF)])

            def turn(o, src, n):
                return pe.transpose(o, src, ident[0:n, 0:n])

            pe.wait_ge(s_("consts"), 1)
            pe.wait_ge(s_("rows_in"), 16 * 8)
            give(turn(take(("rows",))[:, 0:100], rows[:], 100), ("rows",))
            pe.wait_ge(s_("conv_in"), 16 * 10)
            for l in range(2):
                for a_ in range(2):
                    job = ("conv", l, a_)
                    give(turn(take(job)[:, 0:88], crow[:, 2 * l + a_, :], 88), job)
            for l in range(2):
                for a_ in range(2):
                    job = ("state", l, a_)
                    o = take(job)
                    for n in range(4 if a_ == 0 else 2):
                        r = 4 * a_ + n
                        m = P if r < 5 else 64
                        ins = turn(o[:, n * P:n * P + m], srow[0:m, l, r, :], m)
                    give(ins, job)
            pe.wait_ge(s_("lrow_ready"), 1)
            pe.wait_ge(s_("lam_in"), 48)
            give(turn(take(("lam",))[:, 0:96], lrow[0:96, :], 96), ("lam",))
            pe.wait_ge(s_("mem_in"), 16)
            for a_ in range(4):
                o = take(("memT", a_))
                for n in range(4):
                    k, c = 2 * a_ + n // 2, n % 2
                    ins = turn(o[:, n * P:n * P + P], mem_in[:, c, k * P:k * P + P], P)
                give(ins, ("memT", a_))
            pe.wait_ge(s_("x_in"), 32)
            for k in range(KD):
                o = take(("xT", k))
                for c in range(4):
                    ins = turn(o[:, c * P:c * P + P], x_tok[:, c, k * P:k * P + P], P)
                give(ins, ("xT", k))
            o = take(("xsT",))
            for k in range(KD):
                ins = turn(o[:, k * NB:k * NB + NB], xs_tok[:, k * P:k * P + P], NB)
            give(ins, ("xsT",))

            stats([(("ms_mem",), 0, NMEM)])
            pe.wait_ge(s_("xlo_made"), 2 * KD)
            nsplit[0] += 2 * KD
            for l in range(2):
                phase(f"memkv{l}", cols=((l * NMEM, (l + 1) * NMEM),))
                for m in range(4):
                    job = ("memtok", l, m)
                    o = take(job)
                    q = PH[f"memkv{l}"][2] + m
                    pe.wait_ge(panel_read, q + 1)
                    src = mem_kT[:, l, m, :] if m < 2 else sq[:, m - 2, 0:NMEM]
                    for c in range(2):
                        ins = turn(o[:, c * P:c * P + P], src[:, c * P:c * P + P], P)
                    give(ins, job)
            stats_x("x0")
            phase("win0", wait_k=x_split)
            nsplit[0] += KD

            pe.wait_ge(s_("h0_in"), 64)
            for ri in range(2):
                for half in range(2):
                    job = ("h0", ri, half)
                    give(turn(take(job)[:, 0:96], hrow[:, ri, half, :], 96), job)
            for t in range(THIRDS):
                pe.wait_ge(s_("bc_in"), 16 * 6 * (t + 1))
                job = ("cT", t)
                o = take(job)
                for ri in range(2):
                    for m in range(2):
                        ins = turn(o[:, 256 * ri + P * m:256 * ri + P * m + P],
                                   c_in[:, ri, m].rearrange("p d n -> p (d n)"), P)
                give(ins, job)
                pe.wait_ge(s_("bp_ready"), t + 1)
                for a_ in range(TP // 2):
                    job = ("bT", t, a_)
                    o = take(job)
                    for n in range(4):
                        ins = turn(o[:, n * P:n * P + P], bp[:, n % 2, 2 * a_ + n // 2, :], P)
                    give(ins, job)
                pe.wait_ge(s_("cp_ready"), t + 1)
                for a_ in range(TG // 4):
                    job = ("K", t, a_)
                    o = take(job)
                    for n, g in enumerate(same_side(a_)):
                        r = slice(STATE * (g % 2), STATE * (g % 2) + STATE)
                        for ri in range(2):
                            ins = pe.matmul(o[0:CH, n * P:n * P + P], bb[r, ri, g // 2, :], cp[r, ri, g // 2, 0:P],
                                            start=(ri == 0), stop=(ri == 1))
                    give(ins, job)
                pe.wait_ge(s_("u_in"), 16 * 10 * (t + 1))
                pe.wait_ge(s_("bT_ready"), t + 1)
                for a_ in range((TP + 2) // 3):
                    job = ("V", t, a_)
                    o = take(job)
                    W = NCH + NB
                    for n in range(min(3, TP - 3 * a_)):
                        j = 3 * a_ + n
                        for ri in range(2):
                            for e in range(2):
                                r = slice(STATE * e, STATE * e + STATE)
                                ins = pe.matmul(o[r, (2 * n + ri) * W:(2 * n + ri + 1) * W], bT[:, j, ri, r],
                                                u[:, 2 * j + e, NB:], start=True, stop=True)
                    give(ins, job)
                pe.wait_ge(s_("toep_in"), 16 * CHUNK * (t + 1))
                pe.wait_ge(s_("hp_ready"), t + 1)
                for a_ in range(TG // 4):
                    job = ("Y", t, a_)
                    o = take(job)
                    for n, g in enumerate(same_side(a_)):
                        r = slice(STATE * (g % 2), STATE * (g % 2) + STATE)
                        oo = o[:, n * W:(n + 1) * W]
                        pe.matmul(oo, cp[r, 0, g // 2, CH:], hp[r, 0, g // 2, 0:W], start=True, stop=False)
                        pe.matmul(oo, cp[r, 1, g // 2, CH:], hp[r, 1, g // 2, 0:W], start=False, stop=False)
                        ins = pe.matmul(oo, toep[:, g, :], u[:, g, 0:W], start=False, stop=True)
                    give(ins, job)
            pe.wait_ge(s_("hfin_ready"), 1)
            for ri in range(2):
                job = ("fin", ri)
                o = take(job)
                for a_ in range(2):
                    ins = turn(o[0:108, a_ * P:a_ * P + P],
                               hfin[:, ri].rearrange("p b j -> p (b j)")[:, 108 * a_:108 * a_ + 108], P)
                give(ins, job)
            pe.wait_ge(s_("xlo_made"), nsplit[0] + 2 * KS)
            nsplit[0] += 2 * KS
            phase("glu")

            ndec = [0]

            def decode_max(jT, jM, jD, st, BH):
                ndec[0] += 1
                pe.wait_ge(s_("dmax1"), ndec[0])
                give(turn(take(jT)[0:BH, 0:P], st[:, 0, 0:BH], P), jT)
                pe.wait_ge(s_("dmax2"), ndec[0])
                give(pe.matmul(take(jM)[:, 0:BH], ones[0:BH, :], st[0:BH, 2, 0:BH], start=True, stop=True), jM)
                pe.wait_ge(s_("dsum"), ndec[0])
                give(pe.matmul(take(jD)[:, 0:BH], ones[:], st[:, 3, 0:BH], start=True, stop=True), jD)
                pe.wait_ge(s_("dp_ready"), ndec[0])

            def q_rows(l):
                for a_ in range(2):
                    job = ("qrow", l, a_)
                    o = take(job)
                    for n in range(4):
                        k = 4 * a_ + n
                        src = y[:, k, T:NT] if (k >= 6 or l == 0) else qs[:, k, :]
                        ins = turn(o[0:NB, n * P:n * P + P], src, P)
                    give(ins, job)

            def mem_attention(l, m):
                if l == 0:
                    q_rows(l)
                for h in range(MEMH):
                    r = slice(DH * (h % 2), DH * (h % 2) + DH)
                    for a_ in range(2):
                        job = ("mS", l, h, a_)
                        o = take(job)
                        for qq in range(2):
                            c = (2 * a_ + qq) * P
                            ins = pe.matmul(o[:, 256 * qq:256 * qq + 256], y[r, 6 + h // 2, c:c + P],
                                            mem_kT[r, l, h // 2, :], start=True, stop=True)
                        give(ins, job)
                    for a_ in range(2):
                        pe.wait_ge(s_("mp_ready"), 8 * l + 2 * h + a_ + 1)
                        job = ("mT", l, h, a_)
                        o = take(job)
                        for kc in range(2):
                            for qq in range(2):
                                ins = turn(o[:, (2 * kc + qq) * P:(2 * kc + qq + 1) * P],
                                           m["p"][:, a_, qq, kc * P:kc * P + P], P)
                        give(ins, job)
                    pe.wait_ge(s_("mpT_ready"), 4 * l + h + 1)
                    job = ("mO", l, h)
                    o = take(job)
                    for kc in range(2):
                        ins = pe.matmul(o[r, :], mem_tok[:, l, kc, 256 + h * DH:256 + h * DH + DH], m["pT"][:, kc, :],
                                        start=(kc == 0), stop=(kc == 1))
                    give(ins, job)
                pe.wait_ge(s_("qrow_ready"), l + 1)
                for b in range(NB):
                    job = ("mq", l, b)
                    give(pe.matmul(take(job)[:, 0:256], sel[:, b, :], qrow[:, SEQW:D], start=True, stop=True), job)
                decode_max(("mmaxT", l), ("mmax", l), ("mden", l), m["dst"], NB * MEMH)
                pe.wait_ge(s_("mv_in"), 16 * (l + 1))
                job = ("mpv", l)
                o = take(job)
                for b in range(NB):
                    for f in range(2):
                        for c in range(2):
                            cc = (2 * b + f) * 2
                            ins = pe.matmul(o[:, cc:cc + 2], m["v"][:, b, c, f * P:f * P + P],
                                            m["s"][:, b, c, 2 * f:2 * f + 2], start=(c == 0), stop=(c == 1))
                give(ins, job)

            mem_attention(0, mb[0])
            nsplit[0] += KS
            pe.wait_ge(s_("xlo_made"), nsplit[0])
            pe.wait_ge(s_("mem_done"), 1)
            phase("wout0")

            def ffn(l):
                for f in range(2):
                    phase(f"up{l}{f}", wait_k=x_split if f == 0 else None)
                    if f == 0:
                        nsplit[0] += KD
                    pe.wait_ge(s_("h_made"), 1 + 22 * l + 11 * (f + 1))
                    phase(f"down{l}{f}", rhs=lambda k: (h_hi[:, k, :], h_lo[:, k, :]))
                pe.wait_ge(s_("tap_made"), 44 * (l + 1))
                for a_ in range(KF * 2 // 4):
                    job = ("cout", l, a_)
                    o = take(job)
                    for n in range(4):
                        ins = turn(o[0:2 + NB, n * P:n * P + P], newconv[:, 4 * a_ + n, :], P)
                    give(ins, job)

            stats_x("o0")
            stats_x("f0")
            ffn(0)
            stats_x("d0")
            stats_x("x1")

            kb, n, base, _ = PH["kv"]
            for m in range(n):
                product(base + m, (base + m) % 2, kb, xs_, HALF, x_split if m == 0 else None)
                if m:
                    kv_turn(m - 1)
            nsplit[0] += KD
            kv_turn(11)
            q = PH["kvf"][2]
            pe.wait_ge(lo_made, q + 1)
            pe.wait_ge(panel_read, q - 1)
            for k in range(KD):
                for n_, (w, r_) in enumerate(((w_hi, x_hi), (w_hi, x_lo), (w_lo, x_hi))):
                    for b_, (c0, c1) in enumerate(HALF):
                        ins = pe.matmul(big[2 * (q % 2) + b_][:, 0:c1 - c0], w[q % 2][:, k, :], r_[:, k, c0:c1],
                                        start=(k == 0 and n_ == 0), stop=(k == KD - 1 and n_ == 2))
            ins.then_inc(panel_done, 1)
            pe.wait_ge(s_("lf_ready"), 1)
            job = ("logf",)
            o = take(job)
            for c in range(4):
                turn(o[:, 12 * c:12 * c + 12], lf[:, 1, c * P:c * P + P], HEADS)
            give(turn(o[0:NB, 48:60], lf[:, 1, T:NT], HEADS), job)
            phase("win1", wait_k=x_split)
            nsplit[0] += KD

            pe.wait_ge(s_("aug_in"), 32)
            pe.wait_ge(s_("q1_ready"), 1)
            pe.wait_ge(s_("kh_made"), 6)
            pe.wait_ge(s_("vtok_ready"), 6)
            for n in range(4 * HEADS):
                h, qi = n // 4, n % 4
                N = (qi + 1) * P
                job = ("fS", h, qi)
                give(pe.matmul(take(job)[:, 0:N], qh[0:DH + 2, h, qi * P:qi * P + P], kh[0:DH + 2, h, 0:N],
                               start=True, stop=True), job)
                job = ("fT", h, qi)
                pe.wait_ge(s_("pa_ready"), n + 1)
                o = take(job)
                for kc in range(qi + 1):
                    ins = turn(o[:, kc * P:kc * P + P], pa[:, kc * P:kc * P + P], P)
                give(ins, job)
                pe.wait_ge(s_("paT_ready"), n + 1)
                job = ("fO", h, qi)
                o = take(job)
                for kc in range(qi + 1):
                    ins = pe.matmul(o[DH * (h % 2):DH * (h % 2) + DH, 0:P], vtok[:, kc, h * DH:h * DH + DH],
                                    paT[:, kc * P:kc * P + P], start=(kc == 0), stop=(kc == qi))
                give(ins, job)
            q_rows(1)
            mem_attention(1, mb[1])

            BH = NB * HEADS
            pe.wait_ge(s_("pre_ready"), 1)
            job = ("dtot",)
            o = take(job)
            pe.matmul(o[:, 0:BH], ones[:], fst[:, 5, 0:BH], start=True, stop=False)
            give(pe.matmul(o[:, 0:BH], ones[0:NB, :], lmask[:].rearrange("r b h -> r (b h)"), start=False, stop=True), job)
            for a_ in range(2):
                job = ("dc", a_)
                o = take(job)
                bs = slice(4 * a_, 4 * a_ + 4)
                pe.matmul(o[:, 0:384], tri[:], logf[:, bs].rearrange("p b g h -> p (b g h)"), start=True, stop=False)
                give(pe.matmul(o[:, 0:384], ones[:], pre[:, bs].rearrange("p b g h -> p (b g h)"), start=False,
                               stop=True), job)
            for b in range(NB):
                for a_ in range(2):
                    job = ("fq", b, a_)
                    give(pe.matmul(take(job)[:, 0:384], sel[:, b, :], qrow[:, 384 * a_:384 * a_ + 384], start=True,
                                   stop=True), job)
            decode_max(("fmaxT",), ("fmax",), ("fden",), fst, BH)
            for b in range(NB):
                job = ("fpv", b)
                o = take(job)
                for pg in range(PAGES + 1):
                    n = b * PAGES + pg
                    if pg < PAGES:
                        pe.wait_ge(s_(f"page_in{n % NPG}"), 16 * (NB * PAGES // NPG + n // NPG + 1))
                    for f in range(6):
                        if pg < PAGES:
                            vv, pp = page[n % NPG][:, f * P:f * P + P], sc[:, b, pg, 2 * f:2 * f + 2]
                        else:
                            vv, pp = kvs[:, 1, f * P:f * P + P], sc[0:NB, b, PAGES, 2 * f:2 * f + 2]
                        ins = pe.matmul(o[:, 2 * f:2 * f + 2], vv, pp, start=(pg == 0 and f == 0),
                                        stop=(pg == PAGES and f == 5), skip_group_check=True)
                    if pg < PAGES:
                        ins.then_inc(s_("v_used"), 1)
                give(ins, job)
            pe.wait_ge(s_("fox_done"), 1)
            pe.wait_ge(s_("mem_done"), 2)
            phase("wout1")
            stats_x("o1")
            stats_x("f1")
            ffn(1)
            stats_x("d1")
            pe.wait_ge(s_("x_updated"), 32)
            for c in range(5):
                for a_ in range(2):
                    job = ("yT", c, a_)
                    o = take(job)
                    for n in range(4):
                        k = 4 * a_ + n
                        if c < 4:
                            ins = turn(o[:, n * P:n * P + P], x[:, k, c * P:c * P + P], P)
                        else:
                            ins = turn(o[0:NB, n * P:n * P + P], x[:, k, T:NT], P)
                    give(ins, job)


OUTS = [
    ("y_prompt", (1, T, D)), ("y_sample", (NB, 1, D)),
    ("prompt_ssm_re", (1, 1, GROUPS, STATE)), ("prompt_ssm_im", (1, 1, GROUPS, STATE)),
    ("prompt_k", (1, T, HEADS, DH)), ("prompt_v", (1, T, HEADS, DH)), ("prompt_logf", (1, T, HEADS)),
    ("prompt_mem_k", (2, 1, NMEM, MEMH, DH)), ("prompt_mem_v", (2, 1, NMEM, MEMH, DH)),
    ("prompt_ffn_conv", (2, 1, 2, 2 * DFF)),
    ("sample_ssm_re", (1, NB, GROUPS, STATE)), ("sample_ssm_im", (1, NB, GROUPS, STATE)),
    ("sample_k", (NB, 1, HEADS, DH)), ("sample_v", (NB, 1, HEADS, DH)), ("sample_logf", (NB, 1, HEADS)),
    ("sample_ffn_conv", (2, NB, 2, 2 * DFF)),
]


def kernel(**inputs):
    from concourse import bacc
    from concourse.bass_utils import run_bass_kernel_spmd

    nc = bacc.Bacc("TRN2", target_bir_lowering=False, num_devices=1)
    arrays, ins, outs = {}, {}, {}
    for name, a in inputs.items():
        a = np.ascontiguousarray(a)
        arrays[f"in_{name}"] = a
        ins[name] = nc.dram_tensor(f"in_{name}", a.shape, mybir.dt.from_np(a.dtype), kind="ExternalInput").ap()
    for name, shape in OUTS:
        outs[name] = nc.dram_tensor(f"out_{name}", shape, F32, kind="ExternalOutput").ap()
    program(nc, ins, outs)
    r = run_bass_kernel_spmd(nc, [arrays], core_ids=[0])
    return tuple(r.results[0][f"out_{name}"] for name, _ in OUTS)
```

```python
import math
from contextlib import ExitStack

import numpy as np

import concourse.bass as bass
from concourse import mybir

F32 = mybir.dt.float32
F32R = mybir.dt.float32r
I32 = mybir.dt.int32
ALU = mybir.AluOpType
ACT = mybir.ActivationFunctionType
AX = mybir.AxisListType

P = 128
T = 512
NB = 8
NT = T + NB
HALF = ((0, 264), (264, NT))
D = 1024
KD = D // P
DFF = 2816
KF = DFF // P
KH = KF // 2
SEQW = 768
KS = SEQW // P
HEADS = 12
MEMH = 4
DH = 64
NMEM = 256
PAST = 1024
PAGE = 128
PAGES = PAST // PAGE
GROUPS, STATE, CH = 48, 64, 16
PAIRS = GROUPS // 2
CHUNK = 8
NCH = T // CHUNK
THIRDS = 3
TP = PAIRS // THIRDS
TG = GROUPS // THIRDS
EPS = 1e-6
NEG = -1e30
SCALE = DH ** -0.5
TWO_PI = 2 * math.pi
ROUND = 12582912.0
PI_LO = 3.1415925


class Own:

    def __init__(self, eng, step):
        self.eng, self.step, self.n, self.last = eng, step, 0, None

    def do(self, ins):
        self.n += 1
        ins.then_inc(self.step, 1)
        self.last = (self.step, self.n)

    def tell(self, ins, sem, value):
        ins.then_inc(sem, 1)
        self.last = (sem, value)

    def mark(self, sem):
        self.sync()
        self.eng.sem_inc(sem, 1)

    def sync(self):
        self.eng.wait_ge(*self.last)


def phases():
    out = [("memkv0", KD, 4), ("memkv1", KD, 4), ("win0", KD, 8), ("glu", KS, 6), ("wout0", KD, 8)]
    for l in range(2):
        if l:
            out += [("kv", KD, 12), ("kvf", KD, 1), ("win1", KD, 8), ("wout1", KD, 8)]
        for f in range(2):
            out += [(f"up{l}{f}", KD, 2 * KH), (f"down{l}{f}", KH, 8)]
    table, base = {}, 0
    for n, (name, kb, panels) in enumerate(out):
        nxt = out[n + 1][0] if n + 1 < len(out) else None
        table[name] = (kb, panels, base, nxt)
        base += panels
    return table, base


def same_side(a):
    return [8 * (a // 2) + 2 * n + a % 2 for n in range(4)]


def misc_jobs():
    jobs = [("rows",), *[("conv", l, a) for l in range(2) for a in range(2)],
            *[("state", l, a) for l in range(2) for a in range(2)], ("lam",)]
    jobs += [("memT", a) for a in range(4)] + [("xT", k) for k in range(KD)] + [("xsT",)]
    jobs += [("ms_mem",)] + [("memtok", l, m) for l in range(2) for m in range(4)]
    jobs += [("ms", "x0", 0), ("ms", "x0", 1)]
    jobs += [("h0", ri, a) for ri in range(2) for a in range(2)]
    for t in range(THIRDS):
        jobs += [("cT", t), *[("bT", t, a) for a in range(TP // 2)], *[("K", t, a) for a in range(TG // 4)]]
        jobs += [("V", t, a) for a in range((TP + 2) // 3)] + [("Y", t, a) for a in range(TG // 4)]
    jobs += [("fin", ri) for ri in range(2)]
    for l in range(2):
        if l:
            jobs += [x for m in range(12) for x in (("kvtok", m), ("kvsamp", m))]
            jobs += [("logf",)]
        jobs += [("qrow", l, a) for a in range(2)]
        if l:
            jobs += [("fmaxT",), ("fmax",), ("fden",)]
        for h in range(MEMH):
            jobs += [("mS", l, h, 0), ("mS", l, h, 1)]
            jobs += [("fpv", 2 * h - 1)] if l and h else []
            jobs += [("mT", l, h, 0), ("mT", l, h, 1)]
            jobs += [("fpv", 2 * h)] if l else []
            jobs += [("mO", l, h)]
        jobs += [("fpv", NB - 1)] if l else []
        jobs += [("mq", l, b) for b in range(NB)]
        jobs += [("mmaxT", l), ("mmax", l), ("mden", l), ("mpv", l)]
        jobs += [("ms", f"o{l}", 0), ("ms", f"o{l}", 1), ("ms", f"f{l}", 0), ("ms", f"f{l}", 1)]
        jobs += [("cout", l, a) for a in range(KF * 2 // 4)]
        jobs += [("ms", f"d{l}", 0), ("ms", f"d{l}", 1)]
        if l == 0:
            jobs += [("ms", "x1", 0), ("ms", "x1", 1)]
    jobs += [("yT", c, a) for c in range(5) for a in range(2)]
    return {name: j for j, name in enumerate(jobs)}


STEPS = HEADS + 3
DECAY_STEP = HEADS


def q_step(b):
    return 3 * b // 2


def fox_jobs():
    jobs = []
    for i in range(STEPS):
        jobs += [("S", i, a) for a in range(3)] if i < HEADS else []
        jobs += [("R", i - 3)] if i >= 3 else []
        jobs += [("T", i - 1, a) for a in range(3)] if 1 <= i <= HEADS else []
        jobs += [("q", b, a) for b in range(NB) if q_step(b) == i for a in range(2)]
        jobs += [("dtot",), ("dc", 0), ("dc", 1)] if i == DECAY_STEP else []
        jobs += [("M", i)] if i < HEADS else []
        jobs += [("O", i - 2)] if 2 <= i <= HEADS + 1 else []
    return {name: j for j, name in enumerate(jobs)}


def program(nc, I, O):
    PH, PANELS = phases()
    J, FJ = misc_jobs(), fox_jobs()
    ctx = ExitStack()
    with ctx:
        def sb(name, shape, dt=F32):
            return ctx.enter_context(nc.sbuf_tensor(name, shape, dt))

        ident = sb("ident", [P, P])
        ones = sb("ones", [P, P])
        meanw = sb("meanw", [P, P])
        tri = sb("tri", [P, P])
        causal = sb("causal", [P, P])
        sel = sb("sel", [NB, NB, P])
        gains = sb("gains", [P, 100])
        convw = sb("convw", [P, 2, 4 * 2 * KF])
        convs = sb("convs", [P, 2, 2 * NB, 2 * KF])
        newconv = sb("newconv", [P, 2 * KF, 2 + NB])
        stats_at = nc.sbuf_base
        rstd = sb("rstd", [P, NT])
        sd = sb("sd", [P, NT])
        sumsq = sb("sumsq", [P, NT])
        sq = sb("sq", [P, 2, NT])
        stats_end = nc.sbuf_base
        rstd_mem = sb("rstd_mem", [P, NMEM])
        x = sb("x", [P, KD, NT])
        y = sb("y", [P, KD, NT])
        weights_at = nc.sbuf_base
        raw = [sb(f"raw{s}", [P, KH, P]) for s in range(2)]
        w_hi = [sb(f"w_hi{s}", [P, KH, P], F32R) for s in range(2)]
        w_lo = [sb(f"w_lo{s}", [P, KH, P], F32R) for s in range(2)]
        weights_end = nc.sbuf_base
        mem_kT = sb("mem_kT", [P, 2, 2, NMEM])
        mem_tok = sb("mem_tok", [P, 2, 2, 512])
        qrow = sb("qrow", [NB, D])
        bf = sb("bf", [HEADS, 1])
        eps = sb("eps", [P, 1])
        qs = sb("qs", [P, 6, NB])
        pages = sb("pages", [1, NB * PAGES], I32)

        class Arena:

            def __init__(self, at, top):
                self.at, self.top = at, top

            def __call__(self, name, shape, dt=F32):
                size = (int(np.prod(shape[1:])) * 4 + 31) // 32 * 32
                assert self.at + size <= self.top, (name, self.at + size - self.top)
                t = nc.alloc_sbuf_tensor_at(name, shape, dt, offset=self.at)
                self.at += size
                return t

        nc_base = nc.sbuf_base
        start = (nc.sbuf_base + 31) // 32 * 32
        top = nc.sbuf_usable_end // 32 * 32
        split = Arena(start, top)
        x_hi = split("x_hi", [P, KD, NT], F32R)
        x_lo = split("x_lo", [P, KD, NT], F32R)
        free = split.at
        split = Arena(start, free)
        kvq = split("kvq", [P, KD, NT])[0:NB].rearrange("p a b -> p (a b)")[:, 0:SEQW]
        x_out = split("x_out", [P, KD, NT])

        a = Arena(free, top - 2560)
        x_tok = a("x_tok", [P, 4, D])
        xs_tok = a("xs_tok", [NB, D])
        mem_in = a("mem_in", [P, 2, D])
        memT = a("memT", [P, KD, NMEM])
        rows = a("rows", [100, P])
        crow = a("crow", [88, 4, P])
        srow = a("srow", [P, 2, 6, P])
        lrow = a("lrow", [P, P])
        dtrow = a("dtrow", [PAIRS, 2])

        early = top - 2560
        e = Arena(early, top)
        lam = e("lam", [P, P])
        hrow = e("hrow", [96, 2, 2, P])
        a = Arena(start, early)
        s5s = a("s5s", [P, 16, PAIRS])
        pw_r = a("pw_r", [P, PAIRS, CHUNK + 1])
        pw_i = a("pw_i", [P, PAIRS, CHUNK + 1])
        h0 = a("h0", [P, 2, NB, PAIRS])
        hfin = a("hfin", [P, 2, 1 + NB, PAIRS])
        hout = a("hout", [108, 2, 2, P])
        b_in = a("b_in", [P, 2, TP, CH])
        bb = a("bb", [P, 2, TP, CH])
        c_in = a("c_in", [P, 2, 2, 2, STATE])
        cT = a("cT", [P, 2, TP, CH])
        bp = a("bp", [P, 2, TP, CHUNK * CH])
        bT = a("bT", [P, TP, 2, P])
        cp = a("cp", [P, 2, TP, (CHUNK + 1) * CH])
        kern = a("kern", [CH, TG, P])
        toep = a("toep", [P, TG, P])
        u = a("u", [P, TG, NCH + 2 * NB])
        v = a("v", [P, 2, TP, NCH + NB])
        e_r = a("e_r", [P, TP, NCH])
        e_i = a("e_i", [P, TP, NCH])
        decay = a("decay", [P, TP, NCH])
        tmp = [a(f"tmp{n}", [P, TP * (CHUNK + 1) * CH]) for n in range(3)]
        hp = a("hp", [P, 2, TP, NB + 1 + NCH])
        yb = a("yb", [P, TG, NB + NCH])
        yz = a("yz", [P, 2, NT])
        a = Arena(free, top)
        gate = a("gate", [P, KS, NT])

        def mem_buffers(a, l):
            return dict(
                p=a(f"mp{l}", [P, 2, 2, NMEM]), pT=a(f"mpT{l}", [P, 2, T]), st=a(f"mst{l}", [P, 2, 8]),
                k=a(f"mk{l}", [P, 2, 2, NMEM]), v=a(f"mv{l}", [P, NB, 2, NMEM]), prod=a(f"mprod{l}", [P, 2, NMEM]),
                s=a(f"ms{l}", [P, NB, 2, MEMH]), dst=a(f"mdst{l}", [P, 8, NB * MEMH]))

        mb = [mem_buffers(a, 0)]

        a = Arena(free, top)
        h_hi = a("h_hi", [P, KH, NT], F32R)
        h_lo = a("h_lo", [P, KH, NT], F32R)
        uc = [a(f"uc{s}", [P, 2 + NT]) for s in range(2)]
        yc = [a(f"yc{s}", [P, NT]) for s in range(2)]
        hf = a("hf", [P, NT])
        sg = a("sg", [P, NT])
        a = Arena(free, top)
        crows = a("crows", [2 + NB, 2 * KF, P])
        a = Arena(free, top)
        ytok = [a(f"ytok{s}", [P, D]) for s in range(2)]

        a = Arena(free, top)
        qh = a("qh", [P, HEADS, T])
        kh = a("kh", [P, HEADS, T])
        after_heads = a.at
        vtok = y[:, 0:6, :].rearrange("p a b -> p (a b)").rearrange("p (c h d) -> p c h d", c=4, h=HEADS)
        kvs = a("kvs", [NB, 2, SEQW])
        lfs = a("lfs", [NB, HEADS])
        keep = a.at
        kvT = a("kvT", [P, NT])
        ktok = [a(f"ktok{s}", [P, 4, P]) for s in range(2)]
        lf = a("lf", [HEADS, 3, NT])
        lft = a("lft", [P, 4, HEADS])
        a = Arena(keep, top)
        PT = [a(f"PT{s}", [P, 1280]) for s in range(2)]
        nmax = [a(f"nmax{s}", [P, 4]) for s in range(2)]
        rinv = a("rinv", [1, T])
        lmask = a("lmask", [NB, NB, HEADS])
        mba = Arena(free, after_heads)
        mb.append(mem_buffers(mba, 1))
        a = Arena(weights_at, weights_end)
        page = [a(f"page{n}", [P, SEQW]) for n in range(PAGES)]
        qb = [a(f"qb{n}", [P, SEQW]) for n in range(2)]
        logf = a("logf", [P, NB, PAGES, HEADS])
        a = Arena(stats_at, stats_end)
        sc = a("sc", [P, NB, PAGES + 1, HEADS])
        pre = a("pre", [P, NB, PAGES, HEADS])
        fst = a("fst", [P, 8, NB * HEADS])
        causal_t = a("causal_t", [P, P])
        block_diag, vm = qb[1], qb[0]

        z_dram = nc.dram_tensor("z_scratch", [SEQW, NT], F32, kind="Internal").ap()
        y_dram = nc.dram_tensor("y_scratch", [SEQW, NT], F32, kind="Internal").ap()

        assert nc.sbuf_base == nc_base

        big = [ctx.enter_context(nc.psum_tensor(f"big{n}", [P, 512], F32)) for n in range(4)]
        misc = [ctx.enter_context(nc.psum_tensor(f"misc{n}", [P, 512], F32)) for n in range(4)]

        def sem(name):
            return ctx.enter_context(nc.semaphore(name))

        raw_loaded = [sem(f"raw_loaded{s}") for s in range(2)]
        hi_made, lo_made = sem("hi_made"), sem("lo_made")
        panel_done, panel_read = sem("panel_done"), sem("panel_read")
        misc_full = [sem(f"misc_full{n}") for n in range(4)]
        misc_free = [sem(f"misc_free{n}") for n in range(4)]
        act_step, dve_step, pool_step = sem("act_step"), sem("dve_step"), sem("pool_step")
        S = {}

        def s_(name):
            if name not in S:
                S[name] = sem(name)
            return S[name]

        fox = big + misc
        fox_full = [sem(f"fox_full{n}") for n in range(8)]
        fox_free = [sem(f"fox_free{n}") for n in range(8)]

        def place(job):
            if job in J:
                j = J[job]
                return misc[j % 4], misc_full[j % 4], misc_free[j % 4], j // 4
            j = FJ[job]
            return fox[j % 8], fox_full[j % 8], fox_free[j % 8], j // 8

        def bank(job):
            return place(job)[0]

        def full(eng, job):
            _, made, _, before = place(job)
            eng.wait_ge(made, before + 1)

        def freed(own, ins, job):
            _, _, free_, before = place(job)
            own.tell(ins, free_, before + 1)

        OFF = dict(mix_pre=0, mix_post=16, ffn_pre=32, ffn_post=48, mem=64, kv=80, dskip=88, bglu=94)

        def gain(name, k, l=0):
            c = OFF[name] + (l * KD if name not in ("kv", "dskip", "bglu") else 0) + k
            return gains[:, c:c + 1]

        def dep_loop(eng, count):
            return eng.Fori(0, count)

        block = ctx.enter_context(nc.Block())

        @block.sync
        def _(sp):
            stores = [0]

            def load(dst, src, sm, **kw):
                sp.dma_start(dst, src, **kw).then_inc(s_(sm), 16)

            def store(dst, src, **kw):
                sp.dma_start(dst, src, **kw).then_inc(s_("stored"), 16)
                stores[0] += 1

            def weights(name, src, after=None):
                kb, n, base, _ = PH[name]

                def one(i, q, half):
                    slot = (base + half) % 2
                    if not isinstance(q, int) or q >= 2:
                        sp.wait_ge(lo_made, q - 1)
                    view = src(i)
                    sp.dma_start(raw[slot][:, 0:kb, 0:view.shape[2]], view).then_inc(raw_loaded[slot], 16)

                if n <= 2 or base < 2 or after is not None:
                    for i in range(n):
                        one(i, base + i, i % 2)
                        if after is not None:
                            after(i)
                else:
                    with sp.Fori(0, n // 2) as it:
                        for half in range(2):
                            one(it * 2 + half, it * 2 + (base + half), half)

            def cols(w, rows=None):
                w = w if rows is None else w[rows[0]:rows[1], :]
                v3 = w.rearrange("(k p) n -> p k n", p=P)
                return lambda i: v3[:, :, bass.ds(i * P, P)]

            for n, nm in enumerate(("norm_mix_pre", "norm_mix_post", "norm_ffn_pre", "norm_ffn_post", "mem_norm")):
                load(rows[16 * n:16 * n + 16, :], I[nm].rearrange("l (k p) -> (l k) p", p=P), "rows_in")
            load(rows[80:88, :], I["kv_norm"].rearrange("(k p) -> k p", p=P), "rows_in")
            load(rows[88:94, :], I["d_skip"].rearrange("l (k p) -> (l k) p", p=P), "rows_in")
            load(rows[94:100, :], I["b_glu"].rearrange("l (k p) -> (l k) p", p=P), "rows_in")
            load(mem_in[:], I["mem_prompt"].rearrange("b (c p) d -> p (b c) d", p=P), "mem_in")
            load(x_tok[:], I["x_prompt"].rearrange("b (c p) d -> p (b c) d", p=P), "x_in")
            load(xs_tok[:], I["x_sample"].rearrange("b t d -> (b t) d"), "x_in")
            for l in range(2):
                taps = I["conv_w"][l].rearrange("t (f p) -> (t f) p", p=P)
                load(crow[:, 2 * l, :], taps[0:88, :], "conv_in")
                load(crow[0:44, 2 * l + 1, :], taps[88:132, :], "conv_in")
                load(crow[44:88, 2 * l + 1, :], I["conv_b"][l].rearrange("(f p) -> f p", p=P), "conv_in")
                st = I["state_ffn_conv"][l].rearrange("b t (f p) -> (b t f) p", p=P)
                load(srow[:, l, 0:5, :], st[0:640, :].rearrange("(r q) p -> q r p", q=P), "conv_in")
                load(srow[0:64, l, 5, :], st[640:704, :], "conv_in")
            sp.wait_ge(s_("lrow_zero"), 1)
            load(lrow[0:24, :], I["lam_re"][0].rearrange("(j g) p -> j (g p)", g=2), "lam_in")
            load(lrow[32:56, :], I["lam_im"][0].rearrange("(j g) p -> j (g p)", g=2), "lam_in")
            load(dtrow[:], I["log_dt"][0].rearrange("(j g) -> j g", g=2), "lam_in")
            load(pages[:], I["page_table"].rearrange("(a b) p -> a (b p)", a=1), "pages_in")
            load(bf[:], I["b_f"].rearrange("(h a) -> h a", a=1), "bf_in")
            for ri, nm in enumerate(("state_ssm_re", "state_ssm_im")):
                st = I[nm][0].rearrange("b (j g) p -> (b j) (g p)", g=2)
                for half in range(2):
                    load(hrow[:, ri, half, :], st[96 * half:96 * half + 96, :], "h0_in")

            weights("memkv0", cols(I["w_mem_kv"][0]))
            weights("memkv1", cols(I["w_mem_kv"][1]))
            for l in range(2):
                sp.wait_ge(s_("memtok_ready"), 4 * (l + 1))
                for nm, c in (("prompt_mem_k", 0), ("prompt_mem_v", 256)):
                    store(O[nm][l, 0].rearrange("(c p) h d -> p c (h d)", p=P), mem_tok[:, l, :, c:c + 256])
            weights("win0", cols(I["w_in"][0]))

            zs3 = z_dram.rearrange("(g c) n -> c g n", c=CH)
            ys3 = y_dram.rearrange("(g c) n -> c g n", c=CH)
            sp.wait_ge(s_("z_ready"), 8)
            for m in range(KS):
                sp.dma_start(z_dram[m * P:(m + 1) * P, :], y[:, m, :]).then_inc(s_("z_out"), 16)
            for t in range(THIRDS):
                g0 = t * TG
                if t:
                    sp.wait_ge(s_("s5_built"), t)
                for ri, nm in enumerate(("b_re", "b_im")):
                    load(b_in[:, ri], I[nm][0, g0:g0 + TG].rearrange("(j g) p c -> (g p) j c", g=2), "bc_in")
                for ri, nm in enumerate(("c_re", "c_im")):
                    for dup in range(2):
                        load(c_in[:, ri, :, dup, :],
                             I[nm][0, g0:g0 + TG].rearrange("(t g) c p -> (g c) t p", g=8), "bc_in")
                if t == 0:
                    sp.wait_ge(s_("z_out"), 16 * KS)
                    sp.wait_ge(s_("s5_zero"), 1)
                else:
                    sp.wait_ge(misc_full[J[("Y", t - 1, 3)] % 4], J[("Y", t - 1, 3)] // 4 + 1)
                for tau in range(CHUNK):
                    j = CHUNK - 1 - tau
                    load(u[CH * tau:CH * tau + CH, :, NB:NB + NCH], zs3[:, g0:g0 + TG, j * NCH:(j + 1) * NCH], "u_in")
                load(u[P - CH:P, :, 0:NB], zs3[:, g0:g0 + TG, T:NT], "u_in")
                load(u[0:CH, :, NB + NCH:], zs3[:, g0:g0 + TG, T:NT], "u_in")
                sp.wait_ge(s_("kern_ready"), 4 * (t + 1))
                for tau in range(CHUNK):
                    load(toep[CH * tau:CH * tau + CH, :, (CHUNK - 1 - tau) * CH:P],
                         kern[:, :, 0:(tau + 1) * CH], "toep_in")
                sp.wait_ge(s_("yb_ready"), 4 * (t + 1))
                for i in range(CHUNK):
                    sp.dma_start(ys3[:, g0:g0 + TG, i * NCH:(i + 1) * NCH],
                                 yb[CH * i:CH * i + CH, :, NB:]).then_inc(s_("y_out"), 16)
                sp.dma_start(ys3[:, g0:g0 + TG, T:NT], yb[0:CH, :, 0:NB]).then_inc(s_("y_out"), 16)
                sp.wait_ge(s_("y_out"), 16 * 9 * (t + 1))
                if t:
                    sp.wait_ge(s_("yz_used"), t)
                load(yz[:], y_dram[g0 * CH:(g0 + TG) * CH, :].rearrange("(m p) n -> p m n", p=P), "yz_in")
            sp.wait_ge(s_("hout_ready"), 2)
            for ri, (pn, sn) in enumerate((("prompt_ssm_re", "sample_ssm_re"), ("prompt_ssm_im", "sample_ssm_im"))):
                store(O[pn][0, 0].rearrange("(j g) p -> j (g p)", g=2), hout[0:24, ri, 0, :])
                so = O[sn][0].rearrange("b (j g) p -> (b j) (g p)", g=2)
                store(so[0:84, :], hout[24:108, ri, 0, :])
                store(so[84:192, :], hout[:, ri, 1, :])
            weights("glu", cols(I["w_glu"][0]))

            def mem_v(l, m):
                load(m["v"][:].rearrange("p b c n -> p (b c) n"),
                     I["cache_mem_v"][l].rearrange("b (c p) h d -> p (b c) (h d)", p=P), "mv_in")

            def mem_k(l, m, b):
                if b >= 2:
                    sp.wait_ge(s_("mk_used"), NB * l + b - 1)
                load(m["k"][:, b % 2], I["cache_mem_k"][l, b].rearrange("(c p) h d -> p c (h d)", p=P),
                     f"mk_in{b % 2}")

            sp.wait_ge(s_("gated"), KS)
            mem_v(0, mb[0])
            for b in range(NB):
                mem_k(0, mb[0], b)
            weights("wout0", cols(I["w_out"][0]))

            def ffn_weights(l):
                for f in range(2):
                    wu = I["w_up"][l].rearrange("(k p) n -> p k n", p=P)

                    def up(i, wu=wu, f=f):
                        it, half = i
                        return wu[:, :, bass.ds(it * P + (f * KH + half * KF) * P, P)]

                    kb, n, base, _ = PH[f"up{l}{f}"]
                    with sp.Fori(0, KH) as it:
                        for half in range(2):
                            slot = (base + half) % 2
                            sp.wait_ge(lo_made, it * 2 + (base + half - 1))
                            sp.dma_start(raw[slot][:, 0:KD, :], up((it, half))).then_inc(raw_loaded[slot], 16)
                    weights(f"down{l}{f}", cols(I["w_down"][l], (f * KH * P, (f + 1) * KH * P)))
                store(O["sample_ffn_conv"][l, :, 0, :], I["state_ffn_conv"][l, :, 1, :])
                sp.wait_ge(s_("crows_ready"), KF * 2 // 4 * (l + 1))
                flat = crows[:].rearrange("r f p -> r (f p)")
                sp.dma_start(O["prompt_ffn_conv"][l, 0], flat[0:2]).then_inc(s_("crows_out"), 16)
                sp.dma_start(O["sample_ffn_conv"][l, :, 1, :], flat[2:2 + NB]).then_inc(s_("crows_out"), 16)

            ffn_weights(0)

            def store_k(i):
                m = i - 4
                if 0 <= m < 6:
                    sp.wait_ge(s_("ktok_ready"), m + 1)
                    sp.dma_start(O["prompt_k"][0].rearrange("(c p) h d -> p c (h d)", p=P)[:, :, m * P:(m + 1) * P],
                                 ktok[m % 2][:]).then_inc(s_(f"ktok_out{m % 2}"), 16)

            weights("kv", cols(I["w_kv"]), store_k)
            wf = I["w_kv"].rearrange("(k p) n -> p k n", p=P)
            weights("kvf", lambda i: wf[:, :, 2 * SEQW:2 * SEQW + HEADS])
            sp.wait_ge(s_("vtok_ready"), 6)
            for c in range(4):
                store(O["prompt_v"][0, c * P:(c + 1) * P], vtok[:, c, :, 0:DH])
            sp.wait_ge(s_("kvs_ready"), 12)
            store(O["sample_k"].rearrange("b t h d -> (b t) (h d)"), kvs[:, 0, :])
            store(O["sample_v"].rearrange("b t h d -> (b t) (h d)"), kvs[:, 1, :])
            sp.wait_ge(s_("logf_ready"), 2)
            store(O["prompt_logf"][0].rearrange("(c p) h -> p c h", p=P), lft[:, 0:4, :])
            store(O["sample_logf"].rearrange("b t h -> (b t) h"), lfs[:])
            sp.wait_ge(s_("c_ready"), 3)
            load(qh[DH:DH + 1, :, :], lf[:, 2, 0:T], "aug_in")
            load(kh[DH + 1:DH + 2, :, :], lf[:, 0, 0:T], "aug_in")
            weights("win1", cols(I["w_in"][1]))
            sp.wait_ge(panel_done, PH["win1"][2] + 8)
            sp.wait_ge(s_("pages_in"), 16)

            def page_id(n):
                return sp.value_load(pages[0:1, bass.ds(n, 1)], min_val=0, max_val=I["cache_k"].shape[0] - 1)

            def page_loads(cache, b, used=None, count=0):
                for pg in range(PAGES):
                    if used is not None:
                        sp.wait_ge(used, count + pg + 1)
                    load(page[pg][:], cache[bass.ds(page_id(b * PAGES + pg), 1)].rearrange("a t h d -> (a t) (h d)"),
                         f"page_in{pg}")

            page_loads(I["cache_k"], 0)
            with sp.Fori(0, NB - 1) as b:
                page_loads(I["cache_k"], b + 1, s_("k_used"), b * PAGES)
                for pg in range(PAGES):
                    load(logf[:, bass.ds(b, 1), pg, :].rearrange("p a h -> p (a h)"),
                         I["cache_logf"][bass.ds(page_id(b * PAGES + pg), 1)].rearrange("a t h -> (a t) h"), "logf_in")
            for pg in range(PAGES):
                load(logf[:, NB - 1, pg, :], I["cache_logf"][bass.ds(page_id((NB - 1) * PAGES + pg), 1)].rearrange(
                    "a t h -> (a t) h"), "logf_in")
            page_loads(I["cache_v"], 0, s_("k_used"), (NB - 1) * PAGES)
            sp.wait_ge(s_("heads_done"), 1)
            mem_v(1, mb[1])
            mem_k(1, mb[1], 0)
            mem_k(1, mb[1], 1)
            with sp.Fori(0, NB - 1) as b:
                page_loads(I["cache_v"], b + 1, s_("v_used"), b * PAGES)
            for b in range(2, NB):
                mem_k(1, mb[1], b)
            sp.wait_ge(s_("fox_done"), 1)
            weights("wout1", cols(I["w_out"][1]))
            ffn_weights(1)
            for c in range(5):
                sp.wait_ge(s_("ytok_ready"), 2 * (c + 1))
                dst = O["y_prompt"][0, c * P:(c + 1) * P, :] if c < 4 else O["y_sample"].rearrange("b t d -> (b t) d")
                sp.dma_start(dst, ytok[c % 2][0:(P if c < 4 else NB), :]).then_inc(s_(f"ytok_out{c % 2}"), 16)
            sp.wait_ge(s_("stored"), 16 * stores[0])
            sp.wait_ge(s_("crows_out"), 16 * 4)
            for s in range(2):
                sp.wait_ge(s_(f"ktok_out{s}"), 16 * 3)
                sp.wait_ge(s_(f"ytok_out{s}"), 16 * (3 - s))

        @block.gpsimd
        def _(pool):
            own = Own(pool, pool_step)
            own.do(pool.memset(ident[:], 0.0))
            own.do(pool.memset(ones[:], 1.0))
            own.do(pool.memset(meanw[:], 1.0 / D))
            own.do(pool.memset(tri[:], 1.0))
            own.do(pool.memset(causal[:], 0.0))
            own.do(pool.memset(sel[:], 0.0))
            own.tell(pool.memset(lrow[:], 0.0), s_("lrow_zero"), 1)
            own.sync()
            own.do(pool.affine_select(out=ident[:], in_=ident[:], compare_op=ALU.not_equal, fill=1.0, base=0,
                                      pattern=[[-1, P]], channel_multiplier=1))
            own.do(pool.affine_select(out=tri[:], in_=tri[:], compare_op=ALU.is_ge, fill=0.0, base=0,
                                      pattern=[[1, P]], channel_multiplier=-1))
            own.do(pool.affine_select(out=causal[:], in_=causal[:], compare_op=ALU.is_ge, fill=NEG / SCALE, base=0,
                                      pattern=[[-1, P]], channel_multiplier=1))
            own.tell(pool.affine_select(out=sel[:], in_=sel[:], compare_op=ALU.not_equal, fill=1.0, base=0,
                                        pattern=[[-1, NB], [0, P]], channel_multiplier=1), s_("consts"), 1)

            def lo(q, slot, kb):
                pool.wait_ge(hi_made, q + 1)
                pool.tensor_tensor(w_lo[slot][:, 0:kb, :], raw[slot][:, 0:kb, :],
                                   w_hi[slot][:, 0:kb, :].bitcast(F32), ALU.subtract).then_inc(lo_made, 1)

            def k_pass():
                pool.wait_ge(s_("q1_ready"), 1)
                own.do(pool.memset(causal_t[:], 0.0))
                own.sync()
                own.tell(pool.affine_select(out=causal_t[:], in_=causal_t[:], compare_op=ALU.is_ge, fill=NEG / SCALE,
                                            base=0, pattern=[[1, P]], channel_multiplier=-1), s_("causal_t_ready"), 1)
                for n in range(NB * PAGES):
                    b, pg = n // PAGES, n % PAGES
                    if pg == 0:
                        pool.wait_ge(s_("qb_ready"), b + 1)
                    pool.wait_ge(s_(f"page_in{pg}"), 16 * (b + 1))
                    own.tell(pool.tensor_tensor(page[pg][:], page[pg][:], qb[b % 2][:], ALU.mult),
                             s_("k_product"), n + 1)
                own.sync()
                mask = block_diag[0:HEADS, :].rearrange("p (h d) -> p h d", d=DH)
                own.do(pool.memset(mask, 0.0))
                own.sync()
                own.tell(pool.affine_select(out=mask, in_=mask, compare_op=ALU.not_equal, fill=1.0, base=0,
                                            pattern=[[-1, HEADS], [0, DH]], channel_multiplier=1), s_("block_diag"), 1)

            for name, (kb, n, base, _) in PH.items():
                if name == "wout1":
                    k_pass()
                if n <= 2:
                    for i in range(n):
                        lo(base + i, (base + i) % 2, kb)
                    continue
                with pool.Fori(0, n // 2) as it:
                    for half in range(2):
                        lo(it * 2 + (base + half), (base + half) % 2, kb)

        @block.vector
        def _(dve):
            own = Own(dve, dve_step)
            do, tell, sync, mark = own.do, own.tell, own.sync, own.mark
            V = dve
            stat = [0, 0]

            def evac(job, dst, src):
                full(dve, job)
                freed(own, V.tensor_copy(dst, src), job)

            def sum_squares(count, cols):
                for k in range(count):
                    dve.wait_ge(s_("sq_made"), stat[0] + 1)
                    if k == 0:
                        ins = V.tensor_copy(sumsq[:, 0:cols], sq[:, stat[0] % 2, 0:cols])
                    else:
                        sync()
                        ins = V.tensor_tensor(sumsq[:, 0:cols], sumsq[:, 0:cols], sq[:, stat[0] % 2, 0:cols], ALU.add)
                    stat[0] += 1
                    tell(ins, s_("sq_used"), stat[0])

            nstd = [0]

            def reciprocal_std(dst, cols):
                nstd[0] += 1
                dve.wait_ge(s_("root_made"), nstd[0])
                tell(V.reciprocal(dst[:, 0:cols], sd[:, 0:cols]), s_("rstd_ready"), nstd[0])
                sync()

            def split_lo(k, src, g, dst, cols=slice(0, NT), hi=None):
                stat[1] += 1
                dve.wait_ge(s_("xhi_made"), stat[1])
                h = x_hi[:, k, cols].bitcast(F32)
                if g is None:
                    ins = V.tensor_tensor(x_lo[:, k, cols], src, h, ALU.subtract)
                else:
                    ins = V.scalar_tensor_tensor(x_lo[:, k, cols], src, g, h, ALU.mult, ALU.subtract)
                tell(ins, s_("xlo_made"), stat[1])

            dve.wait_ge(s_("lam_in"), 48)
            dve.wait_ge(s_("lrow_zero"), 1)
            do(V.tensor_copy(lrow[64:64 + PAIRS, :].rearrange("j (g p) -> j g p", g=2),
                             dtrow[:].unsqueeze(2).to_broadcast([PAIRS, 2, STATE])))
            mark(s_("lrow_ready"))
            do(V.memset(eps[:], EPS))
            mark(s_("h_made"))
            evac(("rows",), gains[:], bank(("rows",))[:, 0:100])
            for l in range(2):
                for a_ in range(2):
                    evac(("conv", l, a_), convw[:, l, 88 * a_:88 * a_ + 88], bank(("conv", l, a_))[:, 0:88])
            for l in range(2):
                flat = convs[:, l].rearrange("p r f -> p (r f)")
                for a_ in range(2):
                    w = 512 if a_ == 0 else 192
                    evac(("state", l, a_), flat[:, 512 * a_:512 * a_ + w], bank(("state", l, a_))[:, 0:w])
            evac(("lam",), lam[:, 0:96], bank(("lam",))[:, 0:96])
            mark(s_("lam_ready"))
            for a_ in range(4):
                full(dve, ("memT", a_))
                freed(own, V.tensor_copy(memT[:, 2 * a_:2 * a_ + 2, :].rearrange("p k t -> p (k t)"),
                                         bank(("memT", a_))[:, :]), ("memT", a_))
            sync()
            mark(s_("mem_ready"))
            for k in range(KD):
                evac(("xT", k), x[:, k, 0:T], bank(("xT", k))[:, :])
            evac(("xsT",), x[:, :, T:NT], bank(("xsT",))[:, 0:KD * NB].rearrange("p (k b) -> p k b", b=NB))
            sync()
            mark(s_("x_ready"))

            sum_squares(KD, NMEM)
            def sums_ready():
                mark(s_("sumsq_ready"))

            sums_ready()
            reciprocal_std(rstd_mem, NMEM)
            for l in range(2):
                for k in range(KD):
                    split_lo(k, memT[:, k, :], gain("mem", k, l), None, slice(l * NMEM, (l + 1) * NMEM))
            for l in range(2):
                base = PH[f"memkv{l}"][2]
                for m in range(4):
                    q = base + m
                    dve.wait_ge(panel_done, q + 1)
                    src = big[2 * (q % 2)][:, 0:NMEM]
                    dst = mem_kT[:, l, m, :] if m < 2 else sq[:, m - 2, 0:NMEM]
                    if l and m >= 2:
                        full(dve, ("memtok", 0, m))
                    tell(V.tensor_tensor(dst, src, rstd_mem[:], ALU.mult), panel_read, q + 1)
                for m in range(4):
                    full(dve, ("memtok", l, m))
                    freed(own, V.tensor_copy(mem_tok[:, l, :, m * P:(m + 1) * P],
                                             bank(("memtok", l, m))[:, 0:256].rearrange("p (c f) -> p c f", c=2)),
                          ("memtok", l, m))
                    sync()
                    mark(s_("memtok_ready"))

            def pre_norm(name, l):
                for k in range(KD):
                    split_lo(k, x[:, k, :], gain(name, k, l), None)

            sum_squares(KD, NT)
            sums_ready()
            pre_norm("mix_pre", 0)
            reciprocal_std(rstd, NT)

            def read_panel(q, dst_of, mult=True):
                slot = q % 2
                dve.wait_ge(panel_done, q + 1)
                for n, (c0, c1) in enumerate(HALF):
                    dst, src, r = dst_of(n, c0, c1), big[2 * slot + n][:, 0:c1 - c0], rstd[:, c0:c1]
                    if len(dst.shape) == 3:
                        src = src[:, 0:(c1 - c0) // 8 * 8].rearrange("p (k j) -> p k j", j=CHUNK)[:, 0:dst.shape[1], :]
                        r = r.rearrange("p (k j) -> p k j", j=CHUNK)[:, 0:dst.shape[1], :]
                    ins = V.tensor_tensor(dst, src, r, ALU.mult)
                    if n == 0 or len(dst.shape) == 3:
                        do(ins)
                if len(dst.shape) == 3:
                    ins = V.tensor_tensor(dst_of(2, T, NT), big[2 * slot + 1][:, T - HALF[1][0]:NT - HALF[1][0]],
                                          rstd[:, T:NT], ALU.mult)
                tell(ins, panel_read, q + 1)

            def by_chunk(tile):
                return tile[:, 0:T].rearrange("p (j k) -> p k j", j=CHUNK)

            K0 = HALF[0][1] // CHUNK
            for m in range(8):
                q = PH["win0"][2] + m
                if m < KS:
                    pick = {0: by_chunk(y[:, m, :])[:, 0:K0, :], 1: by_chunk(y[:, m, :])[:, K0:NCH, :],
                            2: y[:, m, T:NT]}
                    read_panel(q, lambda n, c0, c1: pick[n])
                else:
                    read_panel(q, lambda n, c0, c1: y[:, m, c0:c1])
                sync()
                mark(s_("z_ready"))

            lr_, li_, dt_ = lam[:, 0:PAIRS], lam[:, 32:32 + PAIRS], lam[:, 64:64 + PAIRS]

            def sl(n):
                return s5s[:, n, :]

            def tt(o, a_, b_, op):
                do(V.tensor_tensor(o, a_, b_, op))
                sync()

            def ts(o, a_, c0, c1, o0, o1):
                do(V.tensor_scalar(o, a_, c0, c1, o0, o1))
                sync()

            LR, X1, TH, MAG, SN, CS, R8, FR, FI, T0, T1, T2, R1, R2, UR, UI = range(16)
            sync()
            ts(sl(LR), lr_, -1e-4, None, ALU.min, ALU.bypass)
            dve.wait_ge(s_("s5_act"), 1)
            tt(sl(X1), sl(LR), dt_, ALU.mult)
            tt(sl(TH), li_, dt_, ALU.mult)
            for dst, shift in ((R1, 0.0), (R2, math.pi / 2)):
                ts(sl(T0), sl(TH), 1.0 / TWO_PI, shift / TWO_PI, ALU.mult, ALU.add)
                ts(sl(T0), sl(T0), ROUND, -ROUND, ALU.add, ALU.add)
                c1 = 6.28125
                c2 = float(np.float32(TWO_PI - c1))
                c3 = TWO_PI - c1 - c2
                ts(sl(T1), sl(T0), -c1, None, ALU.mult, ALU.bypass)
                tt(sl(dst), sl(TH), sl(T1), ALU.add)
                ts(sl(T1), sl(T0), -c2, None, ALU.mult, ALU.bypass)
                tt(sl(dst), sl(dst), sl(T1), ALU.add)
                ts(sl(T1), sl(T0), -c3, None, ALU.mult, ALU.bypass)
                tt(sl(dst), sl(dst), sl(T1), ALU.add)
                if shift:
                    ts(sl(dst), sl(dst), shift, None, ALU.add, ALU.bypass)
                ts(sl(dst), sl(dst), PI_LO, -PI_LO, ALU.min, ALU.max)
            tell(V.tensor_copy(sl(T2), sl(R1)), s_("angles_ready"), 1)
            sync()
            dve.wait_ge(s_("s5_act"), 5)
            AR, AI = pw_r[:, :, 1], pw_i[:, :, 1]
            tt(AR, sl(MAG), sl(CS), ALU.mult)
            tt(AI, sl(MAG), sl(SN), ALU.mult)
            tt(sl(T0), sl(LR), sl(LR), ALU.mult)
            tt(sl(T1), li_, li_, ALU.mult)
            tt(sl(T0), sl(T0), sl(T1), ALU.add)
            do(V.reciprocal(sl(T0), sl(T0)))
            sync()
            ts(sl(T2), AR, -1.0, None, ALU.add, ALU.bypass)
            tt(sl(FR), sl(T2), sl(LR), ALU.mult)
            tt(sl(T1), AI, li_, ALU.mult)
            tt(sl(FR), sl(FR), sl(T1), ALU.add)
            tt(sl(FR), sl(FR), sl(T0), ALU.mult)
            tt(sl(FI), AI, sl(LR), ALU.mult)
            tt(sl(T1), sl(T2), li_, ALU.mult)
            tt(sl(FI), sl(FI), sl(T1), ALU.subtract)
            tt(sl(FI), sl(FI), sl(T0), ALU.mult)

            def cmul(o_r, o_i, a_r, a_i, b_r, b_i, t0, conj=False, neg_i=False):
                tt(o_r, a_r, b_r, ALU.mult)
                tt(t0, a_i, b_i, ALU.mult)
                tt(o_r, o_r, t0, ALU.add if conj else ALU.subtract)
                tt(o_i, a_r, b_i, ALU.mult)
                tt(t0, a_i, b_r, ALU.mult)
                if neg_i:
                    do(V.scalar_tensor_tensor(o_i, o_i, -1.0, t0, ALU.mult, ALU.subtract))
                    sync()
                else:
                    tt(o_i, o_i, t0, ALU.subtract if conj else ALU.add)

            do(V.memset(pw_r[:, :, 0:1], 1.0))
            do(V.memset(pw_i[:, :, 0:1], 0.0))
            sync()
            for m in (1, 2, 4):
                w_r = pw_r[:, :, m:m + 1].to_broadcast([P, PAIRS, m])
                w_i = pw_i[:, :, m:m + 1].to_broadcast([P, PAIRS, m])
                tv = tmp[0][:, 0:PAIRS * m].rearrange("p (j m) -> p j m", m=m)
                cmul(pw_r[:, :, m + 1:2 * m + 1], pw_i[:, :, m + 1:2 * m + 1], w_r, w_i,
                     pw_r[:, :, 1:m + 1], pw_i[:, :, 1:m + 1], tv)
            do(V.tensor_copy(sl(UR), sl(CS)))
            do(V.tensor_copy(sl(UI), sl(SN)))
            sync()

            def square(w_r, w_i, t0, t1):
                tt(t0, w_r, w_r, ALU.mult)
                tt(t1, w_i, w_i, ALU.mult)
                tt(w_i, w_r, w_i, ALU.mult)
                ts(w_i, w_i, 2.0, None, ALU.mult, ALU.bypass)
                tt(w_r, t0, t1, ALU.subtract)

            for _ in range(3):
                square(sl(UR), sl(UI), sl(T0), sl(T1))
            for ri in range(2):
                for half in range(2):
                    evac(("h0", ri, half), h0[:, ri].rearrange("p b j -> p (b j)")[:, 96 * half:96 * half + 96],
                         bank(("h0", ri, half))[:, 0:96])
            do(V.memset(u[:], 0.0))
            do(V.memset(toep[:], 0.0))
            do(V.memset(hp[:, :, :, NB:NB + 1], 0.0))
            sync()
            tell(V.memset(e_i[:, :, 0:1], 0.0), s_("s5_zero"), 1)
            do(V.memset(e_r[:, :, 0:1], 1.0))
            sync()

            for t in range(THIRDS):
                j0 = t * TP
                js = slice(j0, j0 + TP)
                dve.wait_ge(s_("bc_in"), 16 * 6 * (t + 1))
                tv = tmp[0][:, 0:TP * CH].rearrange("p (j c) -> p j c", c=CH)
                f_r = s5s[:, FR, js].unsqueeze(2).to_broadcast([P, TP, CH])
                f_i = s5s[:, FI, js].unsqueeze(2).to_broadcast([P, TP, CH])
                cmul(bb[:, 0], bb[:, 1], f_r, f_i, b_in[:, 0], b_in[:, 1], tv)
                full(dve, ("cT", t))
                for ri in range(2):
                    srcc = bank(("cT", t))[:, 256 * ri:256 * ri + 256].rearrange(
                        "p (j g c) -> p j g c", g=2, c=CH)
                    do(V.tensor_copy(cT[0:64, ri], srcc[0:64, :, 0, :]))
                    ins = V.tensor_copy(cT[64:128, ri], srcc[64:128, :, 1, :])
                    if ri == 0:
                        do(ins)
                freed(own, ins, ("cT", t))
                sync()
                mark(s_("s5_built"))
                n = CHUNK
                ap_r = pw_r[:, js, 0:n].unsqueeze(3).to_broadcast([P, TP, n, CH])
                ap_i = pw_i[:, js, 0:n].unsqueeze(3).to_broadcast([P, TP, n, CH])
                tv = tmp[0][:, 0:TP * n * CH].rearrange("p (j n c) -> p j n c", n=n, c=CH)
                cmul(bp[:, 0].rearrange("p j (n c) -> p j n c", c=CH), bp[:, 1].rearrange("p j (n c) -> p j n c", c=CH),
                     ap_r, ap_i, bb[:, 0].unsqueeze(2).to_broadcast([P, TP, n, CH]),
                     bb[:, 1].unsqueeze(2).to_broadcast([P, TP, n, CH]), tv)
                mark(s_("bp_ready"))
                n = CHUNK + 1
                ap_r = pw_r[:, js, 0:n].unsqueeze(3).to_broadcast([P, TP, n, CH])
                ap_i = pw_i[:, js, 0:n].unsqueeze(3).to_broadcast([P, TP, n, CH])
                tv = tmp[0][:, 0:TP * n * CH].rearrange("p (j n c) -> p j n c", n=n, c=CH)
                cmul(cp[:, 0].rearrange("p j (n c) -> p j n c", c=CH), cp[:, 1].rearrange("p j (n c) -> p j n c", c=CH),
                     ap_r, ap_i, cT[:, 0].unsqueeze(2).to_broadcast([P, TP, n, CH]),
                     cT[:, 1].unsqueeze(2).to_broadcast([P, TP, n, CH]), tv, neg_i=True)
                mark(s_("cp_ready"))
                for a_ in range(TP // 2):
                    evac(("bT", t, a_), bT[:, 2 * a_:2 * a_ + 2].rearrange("p j r n -> p (j r n)"),
                         bank(("bT", t, a_))[:, :])
                sync()
                mark(s_("bT_ready"))
                for a_ in range(TG // 4):
                    if t and a_ == 0:
                        dve.wait_ge(s_("toep_in"), 16 * CHUNK * t)
                    evac(("K", t, a_), kern[:, same_side(a_)[0]:same_side(a_)[-1] + 1:2, :],
                         bank(("K", t, a_))[0:CH, :].rearrange("p (g n) -> p g n", g=4))
                    sync()
                    mark(s_("kern_ready"))
                w_r, w_i, s0, s1 = (s5s[:, n_, js] for n_ in (X1, TH, T0, T1))
                do(V.tensor_copy(w_r, s5s[:, UR, js]))
                do(V.tensor_copy(w_i, s5s[:, UI, js]))
                do(V.tensor_copy(decay[:], s5s[:, R8, js].unsqueeze(2).to_broadcast([P, TP, NCH])))
                sync()
                do(V.memset(decay[:, :, 0:1], 0.0))
                m = 1
                while m < NCH:
                    tv = tmp[0][:, 0:TP * m].rearrange("p (j m) -> p j m", m=m)
                    cmul(e_r[:, :, m:2 * m], e_i[:, :, m:2 * m], w_r.unsqueeze(2).to_broadcast([P, TP, m]),
                         w_i.unsqueeze(2).to_broadcast([P, TP, m]), e_r[:, :, 0:m], e_i[:, :, 0:m], tv)
                    square(w_r, w_i, s0, s1)
                    m *= 2
                for a_ in range((TP + 2) // 3):
                    n = min(3, TP - 3 * a_)
                    full(dve, ("V", t, a_))
                    src = bank(("V", t, a_))[:, 0:n * 2 * (NCH + NB)].rearrange("p (j r k) -> p j r k", r=2, k=NCH + NB)
                    do(V.tensor_copy(v[:, 0, 3 * a_:3 * a_ + n], src[:, :, 0, :]))
                    freed(own, V.tensor_copy(v[:, 1, 3 * a_:3 * a_ + n], src[:, :, 1, :]), ("V", t, a_))
                sync()
                w_ = [tmp[n_][:, 0:TP * NCH].rearrange("p (j k) -> p j k", k=NCH) for n_ in range(3)]
                cmul(w_[0], w_[1], e_r[:], e_i[:], v[:, 0, :, 0:NCH], v[:, 1, :, 0:NCH], w_[2], conj=True)
                flat = [tmp[n_][:, 0:TP * NCH] for n_ in range(2)]
                dflat = decay[:].rearrange("p j k -> p (j k)")
                g_ = tmp[2][:, 0:TP * NCH]
                g2 = tmp[0][:, TP * NCH:2 * TP * NCH]
                do(V.tensor_tensor_scan(g_, dflat, flat[0], 0.0, ALU.mult, ALU.add))
                do(V.tensor_tensor_scan(g2, dflat, flat[1], 0.0, ALU.mult, ALU.add))
                sync()
                g2v = g2.rearrange("p (j k) -> p j k", k=NCH)
                cmul(hp[:, 0, :, NB + 1:], hp[:, 1, :, NB + 1:], e_r[:], e_i[:], w_[2], g2v, w_[1])
                hT = h0[:].rearrange("p r b j -> p r j b")
                for ri in range(2):
                    do(V.tensor_copy(hp[:, ri, :, 0:NB], hT[:, ri, js, :]))
                sync()
                mark(s_("hp_ready"))
                fT = hfin[:].rearrange("p r b j -> p r j b")
                a_r = pw_r[:, js, 1:2].to_broadcast([P, TP, NB])
                a_i = pw_i[:, js, 1:2].to_broadcast([P, TP, NB])
                tv = tmp[0][:, 0:TP * NB].rearrange("p (j b) -> p j b", b=NB)
                cmul(fT[:, 0, js, 1:], fT[:, 1, js, 1:], a_r, a_i, hT[:, 0, js, :], hT[:, 1, js, :], tv)
                for ri in range(2):
                    tt(fT[:, ri, js, 1:], fT[:, ri, js, 1:], v[:, ri, :, NCH:], ALU.add)
                    do(V.tensor_copy(fT[:, ri, js, 0:1], hp[:, ri, :, NB + NCH:]))
                if t:
                    dve.wait_ge(s_("y_out"), 16 * 9 * t)
                for a_ in range(TG // 4):
                    evac(("Y", t, a_), yb[:, same_side(a_)[0]:same_side(a_)[-1] + 1:2, :],
                         bank(("Y", t, a_))[:, 0:4 * (NB + NCH)].rearrange("p (g n) -> p g n", g=4))
                    sync()
                    mark(s_("yb_ready"))
                dve.wait_ge(s_("yz_in"), 16 * (t + 1))
                for m in range(2):
                    k = 2 * t + m
                    do(V.scalar_tensor_tensor(y[:, k, :], y[:, k, :], gain("dskip", k), yz[:, m, :], ALU.mult, ALU.add))
                sync()
                mark(s_("yz_used"))
            mark(s_("hfin_ready"))
            for ri in range(2):
                full(dve, ("fin", ri))
                freed(own, V.tensor_copy(hout[:, ri].rearrange("p a n -> p (a n)"), bank(("fin", ri))[0:108, 0:256]),
                      ("fin", ri))
                sync()
                mark(s_("hout_ready"))
            dve.wait_ge(s_("stored"), 16 * 10)
            dve.wait_ge(s_("gelu_made"), THIRDS)
            mark(s_("x_free"))

            def time_order(tile):
                return tile[:, 0:T].rearrange("p (j k) -> p k j", j=CHUNK)

            for k in range(KS):
                stat[1] += 2
                dve.wait_ge(s_("xhi_made"), stat[1])
                for c, (dst, srcv) in enumerate((
                        (slice(0, T), time_order(y[:, k, :])), (slice(T, NT), y[:, k, T:NT]))):
                    h = x_hi[:, k, dst].bitcast(F32)
                    o = x_lo[:, k, dst]
                    if c == 0:
                        h = h.rearrange("p (k j) -> p k j", j=CHUNK)
                        o = o.rearrange("p (k j) -> p k j", j=CHUNK)
                    tell(V.tensor_tensor(o, srcv, h, ALU.subtract), s_("xlo_made"), stat[1] - 1 + c)
            for m in range(KS):
                q = PH["glu"][2] + m
                dve.wait_ge(panel_done, q + 1)
                do(V.tensor_scalar(gate[:, m, 0:264], big[2 * (q % 2)][:, 0:264], gain("bglu", m), None, ALU.add, ALU.bypass))
                tell(V.tensor_scalar(gate[:, m, 264:NT], big[2 * (q % 2) + 1][:, 0:256], gain("bglu", m), None,
                                     ALU.add, ALU.bypass), panel_read, q + 1)
            sync()
            mark(s_("gate_ready"))
            for m in range(KS):
                dve.wait_ge(s_("sig_made"), m + 1)
                gt = gate[:, m, 0:T].rearrange("p (k j) -> p k j", j=CHUNK)
                do(V.tensor_tensor(gt, gt, time_order(y[:, m, :]), ALU.mult))
                do(V.tensor_tensor(gate[:, m, T:NT], gate[:, m, T:NT], y[:, m, T:NT], ALU.mult))
                sync()
                mark(s_("gated"))
                split_lo(m, gate[:, m, :], None, None)

            def mem_attention(l, m_):
                qm = y[:, 6:8, :]
                m = m_
                if l == 0:
                    for a_ in range(2):
                        evac(("qrow", l, a_), qrow[:, 512 * a_:512 * a_ + 512], bank(("qrow", l, a_))[0:NB, :])
                    sync()
                    mark(s_("qrow_ready"))
                for h in range(MEMH):
                    for a_ in range(2):
                        n = 8 * l + 2 * h + a_
                        full(dve, ("mS", l, h, a_))
                        if n >= 2:
                            prev = ("mT", l, (2 * h + a_ - 2) // 2, a_) if 2 * h + a_ >= 2 else ("mT", 0, 3, a_)
                            full(dve, prev)
                        st = m["st"][:, a_, :]
                        do(V.tensor_reduce(st[:, 0:2], bank(("mS", l, h, a_))[:].rearrange("p (q k) -> p q k", q=2),
                                           AX.X, ALU.max))
                        sync()
                        tell(V.tensor_scalar(st[:, 2:4], st[:, 0:2], -SCALE, None, ALU.mult, ALU.bypass),
                             s_("mneg"), n + 1)
                        dve.wait_ge(s_("mexp"), n + 1)
                        do(V.reciprocal(st[:, 6:8], st[:, 4:6]))
                        sync()
                        for qq in range(2):
                            pp = m["p"][:, a_, qq, :]
                            do(V.tensor_scalar(pp, pp, st[:, 6 + qq:7 + qq], None, ALU.mult, ALU.bypass))
                        sync()
                        mark(s_("mp_ready"))
                    if l and h:
                        pv_out(2 * h - 1)
                    if l:
                        pv_masked(2 * h)
                    for a_ in range(2):
                        if h and a_ == 0:
                            full(dve, ("mO", l, h - 1))
                        evac(("mT", l, h, a_), m["pT"][:, :, 256 * a_:256 * a_ + 256],
                             bank(("mT", l, h, a_))[:].rearrange("p (k q) -> p k q", k=2))
                    sync()
                    mark(s_("mpT_ready"))
                    if l:
                        pv_out(2 * h)
                        pv_masked(2 * h + 1)
                    full(dve, ("mO", l, h))
                    r = slice(DH * (h % 2), DH * (h % 2) + DH)
                    src = bank(("mO", l, h))[r, :]
                    do(V.tensor_copy(x_hi[r, 6 + h // 2, 0:T], src))
                    sync()
                    freed(own, V.tensor_tensor(x_lo[r, 6 + h // 2, 0:T], src,
                                               x_hi[r, 6 + h // 2, 0:T].bitcast(F32), ALU.subtract), ("mO", l, h))
                if l:
                    pv_out(NB - 1)
                    sync()
                    mark(s_("fox_done"))
                for b in range(NB):
                    dve.wait_ge(s_(f"mk_in{b % 2}"), 16 * (4 * l + b // 2 + 1))
                    full(dve, ("mq", l, b))
                    q_b = bank(("mq", l, b))[:, 0:256].unsqueeze(1).to_broadcast([P, 2, 256])
                    ins = V.tensor_tensor(m["prod"][:], m["k"][:, b % 2], q_b, ALU.mult)
                    freed(own, ins, ("mq", l, b))
                    sync()
                    tell(V.tensor_reduce(m["s"][:, b], m["prod"][:].rearrange("p c (h d) -> p c h d", d=DH), AX.X,
                                         ALU.add), s_("mk_used"), NB * l + b + 1)
                    sync()
                sv = m["s"][:].rearrange("p b c h -> p (b c h)")
                do(V.tensor_scalar(sv, sv, SCALE, None, ALU.mult, ALU.bypass))
                sync()
                decode_softmax(m["s"], m["dst"], MEMH, 2, ("mmaxT", l), ("mmax", l), ("mden", l), l)
                full(dve, ("mpv", l))
                pv = bank(("mpv", l))[:, 0:NB * 2 * 2].rearrange("p (b f e) -> p f b e", f=2, e=2)
                for e in range(2):
                    r = slice(DH * e, DH * e + DH)
                    do(V.tensor_copy(x_hi[r, 6:8, T:NT], pv[r, :, :, e]))
                sync()
                for e in range(2):
                    r = slice(DH * e, DH * e + DH)
                    ins = V.tensor_tensor(x_lo[r, 6:8, T:NT], pv[r, :, :, e], x_hi[r, 6:8, T:NT].bitcast(F32),
                                          ALU.subtract)
                    if e == 0:
                        do(ins)
                freed(own, ins, ("mpv", l))
                sync()
                mark(s_("mem_done"))

            ndec = [0]

            def decode_softmax(s, st, H, pgs, jT, jM, jD, l):
                BH = NB * H
                n = ndec[0] = ndec[0] + 1
                m1, mx, dg, sm, inv = (st[:, k_, 0:BH] for k_ in range(5))
                do(V.tensor_reduce(m1.rearrange("p (b h) -> p b h", h=H), s[:].rearrange("p b g h -> p b h g"),
                                   AX.X, ALU.max))
                sync()
                mark(s_("dmax1"))
                full(dve, jT)
                freed(own, V.tensor_reduce(mx[0:BH, 0:1], bank(jT)[0:BH, 0:P], AX.X, ALU.max), jT)
                sync()
                tell(V.tensor_scalar(dg[0:BH, :], ident[0:BH, 0:BH], mx[0:BH, 0:1], None, ALU.mult, ALU.bypass),
                     s_("dmax2"), n)
                full(dve, jM)
                mb_ = bank(jM)[:, 0:BH].rearrange("p (b h) -> p b h", h=H).unsqueeze(2).to_broadcast([P, NB, pgs, H])
                freed(own, V.tensor_tensor(s[:], s[:], mb_, ALU.subtract), jM)
                sync()
                mark(s_("dexp_in"))
                dve.wait_ge(s_("dexp"), n)
                do(V.tensor_reduce(sm.rearrange("p (b h) -> p b h", h=H), s[:].rearrange("p b g h -> p b h g"),
                                   AX.X, ALU.add))
                sync()
                mark(s_("dsum"))
                full(dve, jD)
                freed(own, V.reciprocal(inv, bank(jD)[:, 0:BH]), jD)
                sync()
                iv = inv.rearrange("p (b h) -> p b h", h=H).unsqueeze(2).to_broadcast([P, NB, pgs, H])
                tell(V.tensor_tensor(s[:], s[:], iv, ALU.mult), s_("dp_ready"), n)
                sync()

            mem_attention(0, mb[0])

            npost = [0]

            def post_norm(name, l, nxt, nl):
                sum_squares(KD, NT)
                sums_ready()
                reciprocal_std(rstd, NT)
                for k in range(KD):
                    do(V.scalar_tensor_tensor(y[:, k, :], y[:, k, :], gain(name, k, l), rstd[:], ALU.mult, ALU.mult))
                    sync()
                    npost[0] += 1
                    tell(V.tensor_tensor(x[:, k, :], x[:, k, :], y[:, k, :], ALU.add), s_("x_updated"), npost[0])
                if nxt is not None:
                    pre_norm(nxt, nl)
                    sum_squares(KD, NT)
                    sums_ready()
                    reciprocal_std(rstd, NT)

            def copy_out(ph):
                for m in range(8):
                    q = PH[ph][2] + m
                    dve.wait_ge(panel_done, q + 1)
                    do(V.tensor_copy(y[:, m, 0:264], big[2 * (q % 2)][:, 0:264]))
                    tell(V.tensor_copy(y[:, m, 264:NT], big[2 * (q % 2) + 1][:, 0:256]), panel_read, q + 1)
                sync()
                nproj[0] += 1
                mark(s_("y_full"))

            nproj = [0]

            def ffn(l):
                for f in range(2):
                    _, n, base, _ = PH[f"up{l}{f}"]
                    step0, r = own.n, None
                    K = 10
                    if f == 0:
                        for s in range(2):
                            do(V.memset(uc[s][:, 0:2], 0.0))
                        sync()
                        step0 = own.n
                    done = 22 * l + 11 * f
                    with dve.Fori(0, KH) as it:
                        c = [0]

                        def st(ins):
                            c[0] += 1
                            ins.then_inc(dve_step, 1)

                        def sy():
                            dve.wait_ge(dve_step, it * K + (step0 + c[0]))

                        for half in range(2):
                            q = it * 2 + (base + half)
                            slot = (base + half) % 2
                            fb = it + (f * KH + half * KF)
                            w_ = [convw[:, l, bass.ds(it + (f * KH + half * KF + 44 * tp), 1)] for tp in range(3)]
                            uu, yy = uc[half], yc[half]
                            dve.wait_ge(panel_done, q + 1)
                            st(V.tensor_tensor(uu[:, 2:266], big[2 * slot][:, 0:264], rstd[:, 0:264], ALU.mult))
                            V.tensor_tensor(uu[:, 266:2 + NT], big[2 * slot + 1][:, 0:256], rstd[:, 264:NT],
                                            ALU.mult).then_inc(panel_read, 1)
                            dve.wait_ge(s_("tap_made"), it * 2 + (2 * done + half + 1))
                            st(V.scalar_tensor_tensor(yy[:, 0:T], uu[:, 1:1 + T], w_[1], yy[:, 0:T], ALU.mult, ALU.add))
                            old = convs[:, l, :, bass.ds(it + (f * KH + half * KF), 1)].rearrange(
                                "p (b t) a -> p t (b a)", t=2)
                            st(V.scalar_tensor_tensor(yy[:, T:NT], old[:, 1], w_[1], yy[:, T:NT], ALU.mult, ALU.add))
                            sy()
                            st(V.scalar_tensor_tensor(yy[:, 0:T], uu[:, 0:T], w_[0], yy[:, 0:T], ALU.mult, ALU.add))
                            V.scalar_tensor_tensor(yy[:, T:NT], old[:, 0], w_[0], yy[:, T:NT], ALU.mult,
                                                   ALU.add).then_inc(s_("conv_made"), 1)
                        dve.wait_ge(s_("silu_made"), it + (done + 1))
                        dve.wait_ge(s_("conv_made"), it * 2 + (2 * done + 2))
                        st(V.tensor_tensor(hf[:], sg[:], yc[1][:], ALU.mult))
                        sy()
                        st(V.tensor_copy(h_hi[:, bass.ds(it, 1), :].rearrange("p a t -> p (a t)"), hf[:]))
                        sy()
                        V.tensor_tensor(h_lo[:, bass.ds(it, 1), :].rearrange("p a t -> p (a t)"), hf[:],
                                        h_hi[:, bass.ds(it, 1), :].rearrange("p a t -> p (a t)").bitcast(F32),
                                        ALU.subtract).then_inc(s_("h_made"), 1)
                    own.n = step0 + KH * c[0]
                    assert c[0] == K, c[0]
                    base = PH[f"down{l}{f}"][2]
                    with dve.Fori(0, 4) as it:
                        for half in range(2):
                            slot = (base + half) % 2
                            dve.wait_ge(panel_done, it * 2 + (base + half + 1))
                            for n_, (c0, c1) in enumerate(HALF):
                                dst = y[:, bass.ds(it * 2 + half, 1), c0:c1].rearrange("p a t -> p (a t)")
                                src = big[2 * slot + n_][:, 0:c1 - c0]
                                ins = V.tensor_copy(dst, src) if f == 0 else V.tensor_tensor(dst, dst, src, ALU.add)
                                ins.then_inc(panel_read if n_ else dve_step, 1)
                    own.n += 8
                nproj[0] += 1
                dve.wait_ge(panel_read, base + 8)
                mark(s_("y_full"))
                for a_ in range(KF * 2 // 4):
                    full(dve, ("cout", l, a_))
                    if l and a_ == 0:
                        dve.wait_ge(s_("crows_out"), 32)
                    freed(own, V.tensor_copy(crows[:, 4 * a_:4 * a_ + 4, :].rearrange("r f p -> r (f p)"),
                                             bank(("cout", l, a_))[0:2 + NB, :]), ("cout", l, a_))
                    sync()
                    mark(s_("crows_ready"))

            copy_out("wout0")
            post_norm("mix_post", 0, "ffn_pre", 0)
            ffn(0)
            post_norm("ffn_post", 0, "kv", 0)

            dve.wait_ge(s_("crows_out"), 32)
            do(V.memset(qh[DH:P, :, :], 0.0))
            for m in range(12):
                q = PH["kv"][2] + m
                if m:
                    full(dve, ("kvsamp", m - 1))
                    if m <= 6:
                        dve.wait_ge(s_("kh_made"), m)
                read_panel(q, lambda n, c0, c1: kvT[:, c0:c1])
                sync()
                mark(s_("kvT_ready"))
                if m < 6 and m >= 2:
                    dve.wait_ge(s_(f"ktok_out{m % 2}"), 16 * (m // 2))
                if m < 6:
                    evac(("kvtok", m), ktok[m % 2][:], bank(("kvtok", m))[:].rearrange("p (c f) -> p c f", c=4))
                else:
                    evac(("kvtok", m), vtok[:, :, 2 * (m - 6):2 * (m - 5), 0:DH],
                         bank(("kvtok", m))[:].rearrange("p (c h d) -> p c h d", c=4, h=2))
                if m == 1:
                    do(V.memset(kh[DH:P, :, :], 0.0))
                elif m == 2:
                    do(V.memset(qh[DH:DH + 2, :, :], 1.0))
                elif m == 3:
                    do(V.memset(kh[DH:DH + 2, :, :], 1.0))
                elif m == 4:
                    do(V.memset(kh[96:97, :, :], 1.0))
                elif m == 5:
                    do(V.memset(vtok[:, :, :, DH:DH + 1], 1.0))
                sync()
                mark(s_("ktok_ready" if m < 6 else "vtok_ready"))
                evac(("kvsamp", m), kvs[:, m // 6, (m % 6) * P:(m % 6 + 1) * P], bank(("kvsamp", m))[0:NB, 0:P])
                sync()
                mark(s_("kvs_ready"))
            q = PH["kvf"][2]
            dve.wait_ge(panel_done, q + 1)
            z_, m_, l_ = lf[:, 0, :], lf[:, 1, :], lf[:, 2, :]
            do(V.tensor_tensor(z_[:, 0:264], big[2 * (q % 2)][0:HEADS, 0:264], rstd[0:HEADS, 0:264], ALU.mult))
            tell(V.tensor_tensor(z_[:, 264:NT], big[2 * (q % 2) + 1][0:HEADS, 0:256], rstd[0:HEADS, 264:NT], ALU.mult),
                 panel_read, q + 1)
            sync()
            dve.wait_ge(s_("bf_in"), 16)
            ts(z_, z_, bf[:, 0:1], None, ALU.add, ALU.bypass)
            ts(m_, z_, -1.0, None, ALU.mult, ALU.bypass)
            tell(V.tensor_tensor(m_, m_, z_, ALU.min), s_("nabs_ready"), 1)
            dve.wait_ge(s_("log_made"), 1)
            tell(V.scalar_tensor_tensor(m_, z_, 0.0, l_, ALU.min, ALU.subtract), s_("lf_ready"), 1)
            sync()
            do(V.memset(z_, 1.0))
            sync()
            do(V.tensor_tensor_scan(l_[:, 0:T], z_[:, 0:T], m_[:, 0:T], 0.0, ALU.mult, ALU.add))
            sync()
            do(V.tensor_scalar(lf[:, 0, 0:T], l_[:, 0:T], -1.0 / SCALE, None, ALU.mult, ALU.bypass))
            sync()
            do(V.tensor_scalar(l_[:, 0:T], l_[:, 0:T], 1.0 / SCALE, None, ALU.mult, ALU.bypass))
            sync()
            for n in range(3):
                mark(s_("c_ready"))
            full(dve, ("logf",))
            do(V.tensor_copy(lft[:, 0:4, :], bank(("logf",))[:, 0:48].rearrange("p (c h) -> p c h", h=HEADS)))
            freed(own, V.tensor_copy(lfs[:], bank(("logf",))[0:NB, 48:60]), ("logf",))
            sync()
            for n in range(2):
                mark(s_("logf_ready"))

            pre_norm("mix_pre", 1)
            for m in range(8):
                q = PH["win1"][2] + m
                slot = q % 2
                dve.wait_ge(panel_done, q + 1)
                if m < 6:
                    for n, (c0, c1) in enumerate(HALF):
                        e1 = min(c1, T)
                        for e in range(2):
                            r = slice(DH * e, DH * e + DH)
                            do(V.tensor_tensor(qh[0:DH, 2 * m + e, c0:e1], big[2 * slot + n][r, 0:e1 - c0],
                                               rstd[r, c0:e1], ALU.mult))
                    tell(V.tensor_tensor(qs[:, m, :], big[2 * slot + 1][:, 248:256], rstd[:, T:NT], ALU.mult),
                         panel_read, q + 1)
                else:
                    do(V.tensor_tensor(y[:, m, 0:264], big[2 * slot][:, 0:264], rstd[:, 0:264], ALU.mult))
                    tell(V.tensor_tensor(y[:, m, 264:NT], big[2 * slot + 1][:, 0:256], rstd[:, 264:NT], ALU.mult),
                         panel_read, q + 1)
            sync()
            mark(s_("q1_ready"))

            for a_ in range(2):
                evac(("qrow", 1, a_), qrow[:, 512 * a_:512 * a_ + 512], bank(("qrow", 1, a_))[0:NB, :])
            sync()
            mark(s_("qrow_ready"))
            dve.wait_ge(panel_done, PH["win1"][2] + 8)
            snew, idneg = fst[0:NB, 7, 0:HEADS], fst[0:NB, 7, 16:16 + NB]
            do(V.memset(sc[:], NEG))
            tt(kvq, kvs[:, 0, :], qrow[:, 0:SEQW], ALU.mult)
            do(V.tensor_reduce(snew, kvq.rearrange("p (h d) -> p h d", d=DH), AX.X, ALU.add))
            do(V.tensor_scalar(idneg, ident[0:NB, 0:NB], -NEG, NEG, ALU.mult, ALU.add))
            sync()
            ts(snew, snew, SCALE, None, ALU.mult, ALU.bypass)
            idb = ident[0:NB, 0:NB].unsqueeze(2).to_broadcast([NB, NB, HEADS])
            tt(sc[0:NB, :, PAGES, :], idb, snew.unsqueeze(1).to_broadcast([NB, NB, HEADS]), ALU.mult)
            tt(sc[0:NB, :, PAGES, :], sc[0:NB, :, PAGES, :], idneg.unsqueeze(2).to_broadcast([NB, NB, HEADS]), ALU.add)
            tt(lmask[:], idb, lfs[:].unsqueeze(1).to_broadcast([NB, NB, HEADS]), ALU.mult)

            def past_decay():
                dve.wait_ge(s_("logf_in"), 16 * NB * PAGES)
                do(V.memset(pre[:, :, 0, :], 0.0))
                sync()
                for pg in range(1, PAGES):
                    tt(pre[:, :, pg, :], pre[:, :, pg - 1, :], logf[:, :, pg - 1, :], ALU.add)
                tot = fst[:, 5, 0:BH].rearrange("p (b h) -> p b h", h=HEADS)
                tt(tot, pre[:, :, PAGES - 1, :], logf[:, :, PAGES - 1, :], ALU.add)
                mark(s_("pre_ready"))
                evac(("dtot",), fst[:, 6, 0:BH], bank(("dtot",))[:, 0:BH])
                sync()
                cq = fst[:, 6, 0:BH].rearrange("p (b h) -> p b h", h=HEADS)
                for a_ in range(2):
                    full(dve, ("dc", a_))
                    bs = slice(4 * a_, 4 * a_ + 4)
                    src = bank(("dc", a_))[:, 0:384].rearrange("p (b g h) -> p b g h", b=4, h=HEADS)
                    freed(own, V.tensor_tensor(pre[:, bs], cq[:, bs].unsqueeze(2).to_broadcast([P, 4, PAGES, HEADS]),
                                               src, ALU.subtract), ("dc", a_))

            BH = NB * HEADS
            AQ = ((512, ((0, 512, 3),)), (512, ((0, 384, 2), (384, 512, 0))), (256, ((0, 256, 1),)))
            dve.wait_ge(s_("causal_t_ready"), 1)
            done = 0
            for i in range(STEPS):
                if i < HEADS:
                    s_banks = [bank(("S", i, a_)) for a_ in range(3)]
                    full(dve, ("S", i, 0))
                    do(V.tensor_tensor(s_banks[0][:, 384:512], s_banks[0][:, 384:512], causal[:], ALU.add))
                    full(dve, ("S", i, 1))
                    o = s_banks[1][:, 256:512].rearrange("p (a k) -> p a k", a=2)
                    do(V.tensor_tensor(o, o, causal[:].unsqueeze(1).to_broadcast([P, 2, P]), ALU.add))
                    full(dve, ("S", i, 2))
                    do(V.tensor_tensor(s_banks[2][:, 128:256], s_banks[2][:, 128:256], causal[:], ALU.add))
                    sync()
                    for a_, (_, parts) in enumerate(AQ):
                        for n, (c0, c1, qi) in enumerate(parts):
                            ins = V.tensor_reduce(nmax[i % 2][:, qi:qi + 1], s_banks[a_][:, c0:c1], AX.X, ALU.max)
                            if n < len(parts) - 1:
                                do(ins)
                        freed(own, ins, ("S", i, a_))
                    sync()
                    tell(V.tensor_scalar(nmax[i % 2][:], nmax[i % 2][:], -1.0, None, ALU.mult, ALU.bypass),
                         s_("nmax_ready"), i + 1)
                if i >= 3:
                    h = i - 3
                    r = slice(DH * (h % 2), DH * (h % 2) + DH)
                    full(dve, ("R", h))
                    out = x_out[r, h // 2, 0:T]
                    do(V.tensor_copy(out, bank(("O", h))[0:DH, :]))
                    sync()
                    freed(own, V.tensor_tensor(out, out, bank(("R", h))[r, :], ALU.mult), ("R", h))
                    mark(place(("O", h))[2])
                    do(V.tensor_copy(x_hi[r, h // 2, 0:T], out))
                    sync()
                    do(V.tensor_tensor(x_lo[r, h // 2, 0:T], out, x_hi[r, h // 2, 0:T].bitcast(F32), ALU.subtract))
                if 1 <= i <= HEADS:
                    for a_ in range(3):
                        full(dve, ("T", i - 1, a_))
                        o = bank(("T", i - 1, a_))[:].rearrange("p (a k) -> p a k", a=4)[:, 0:4 if a_ == 1 else 1:3, :]
                        do(V.tensor_tensor(o, o, causal_t[:].unsqueeze(1).to_broadcast([P, 2 if a_ == 1 else 1, P]),
                                           ALU.add))
                        mark(s_("t_masked"))
                if i == DECAY_STEP:
                    past_decay()
                upto = min(NB * PAGES, NB * PAGES * i // (HEADS - 1))
                for n in range(done, upto):
                    dve.wait_ge(s_("k_product"), n + 1)
                    tell(V.tensor_reduce(sc[:, n // PAGES, n % PAGES, :],
                                         page[n % PAGES][:].rearrange("p (h d) -> p h d", d=DH), AX.X, ALU.add),
                         s_("k_used"), n + 1)
                done = upto
                if 2 <= i <= HEADS + 1:
                    full(dve, ("O", i - 2))
                    tell(V.reciprocal(rinv[:], bank(("O", i - 2))[DH:DH + 1, :]), s_("rinv_ready"), i - 1)
            sync()
            mark(s_("heads_done"))
            do(V.scalar_tensor_tensor(sc[:, :, 0:PAGES, :].rearrange("p b g h -> p b (g h)"),
                                      sc[:, :, 0:PAGES, :].rearrange("p b g h -> p b (g h)"), SCALE,
                                      pre[:].rearrange("p b g h -> p b (g h)"), ALU.mult, ALU.add))
            sync()
            decode_softmax(sc, fst, HEADS, PAGES + 1, ("fmaxT",), ("fmax",), ("fden",), 1)
            dve.wait_ge(s_("block_diag"), 1)

            def pv_masked(b):
                dve.wait_ge(s_("pv_done"), b + 1)
                if b:
                    full(dve, ("fpv", b - 1))
                for a_ in range(2):
                    do(V.tensor_tensor(vm[0:HEADS, 384 * a_:384 * a_ + 384], big[2 * (b % 2) + a_][0:HEADS, 0:384],
                                       block_diag[0:HEADS, 384 * a_:384 * a_ + 384], ALU.mult))
                mark(s_("vm_ready"))

            def pv_out(b):
                full(dve, ("fpv", b))
                o = bank(("fpv", b))[:, 0:6].unsqueeze(2)
                do(V.tensor_copy(x_hi[:, 0:6, T + b:T + b + 1], o))
                sync()
                freed(own, V.tensor_tensor(x_lo[:, 0:6, T + b:T + b + 1], o,
                                           x_hi[:, 0:6, T + b:T + b + 1].bitcast(F32), ALU.subtract), ("fpv", b))

            mem_attention(1, mb[1])

            dve.wait_ge(s_("stored"), 16 * 19)
            copy_out("wout1")
            post_norm("mix_post", 1, "ffn_pre", 1)
            ffn(1)
            post_norm("ffn_post", 1, None, 0)
            dve.wait_ge(s_("crows_out"), 64)
            for c in range(5):
                rows_ = P if c < 4 else NB
                if c >= 2:
                    dve.wait_ge(s_(f"ytok_out{c % 2}"), 16 * (c // 2))
                for a_ in range(2):
                    evac(("yT", c, a_), ytok[c % 2][0:rows_, 512 * a_:512 * a_ + 512], bank(("yT", c, a_))[0:rows_, :])
                    sync()
                    mark(s_("ytok_ready"))

        @block.scalar
        def _(act):
            own = Own(act, act_step)
            do, tell, sync, mark = own.do, own.tell, own.sync, own.mark
            A = act
            stat = [0, 0, 0]

            def hi(kb, half_c, it=None):
                slot = half_c % 2
                if it is None:
                    q, loads = half_c, half_c // 2 + 1
                else:
                    q, loads = it * 2 + half_c, it + (half_c // 2 + 1)
                act.wait_ge(raw_loaded[slot], loads * 16)
                if it is not None or q >= 2:
                    act.wait_ge(panel_done, q - 1)
                A.activation(w_hi[slot][:, 0:kb, :], raw[slot][:, 0:kb, :], ACT.Copy).then_inc(hi_made, 1)

            def run(name, work=None, ahead=True, started=True):
                kb, n, base, nxt = PH[name]
                work = work or (lambda it, half: None)
                if not started:
                    hi(kb, base)
                    hi(kb, base + 1)
                pairs = n // 2
                if pairs > 2:
                    with act.Fori(0, pairs - 1) as it:
                        for half in range(2):
                            hi(kb, base + half + 2, it)
                            work(it, half)
                for i in range(n - 2 if pairs > 2 else 0, n):
                    if i + 2 < n:
                        hi(kb, base + i + 2)
                    elif ahead:
                        hi(PH[nxt][0], base + i + 2)
                    work(i // 2, i % 2)

            def squares(count, src, cols, ready):
                for k in range(count):
                    ready(k)
                    n = stat[0]
                    if n >= 2:
                        act.wait_ge(s_("sq_used"), n - 1)
                    stat[0] += 1
                    tell(A.activation(sq[:, n % 2, 0:cols], src(k), ACT.Square), s_("sq_made"), n + 1)

            def root(jobs):
                if stat[2]:
                    act.wait_ge(s_("rstd_ready"), stat[2])
                for job, c0, c1 in jobs:
                    full(act, job)
                    freed(own, A.activation(sd[:, c0:c1], bank(job)[:, 0:c1 - c0], ACT.Sqrt, bias=eps[:, 0:1]), job)
                stat[2] += 1
                mark(s_("root_made"))

            def root_x(name):
                root([(("ms", name, n), c0, c1) for n, (c0, c1) in enumerate(HALF)])

            def split_hi(k, src, g=None, cols=slice(0, NT)):
                stat[1] += 1
                o = x_hi[:, k, cols]
                if len(src.shape) == 3:
                    o = o.rearrange("p (k j) -> p k j", j=CHUNK)
                ins = A.activation(o, src, ACT.Copy, scale=1.0 if g is None else g)
                tell(ins, s_("xhi_made"), stat[1])

            hi(KD, 0)
            hi(KD, 1)
            act.wait_ge(s_("mem_ready"), 1)
            squares(KD, lambda k: memT[:, k, :], NMEM, lambda k: None)
            for l in range(2):
                for k in range(KD):
                    split_hi(k, memT[:, k, :], gain("mem", k, l), slice(l * NMEM, (l + 1) * NMEM))
            root([(("ms_mem",), 0, NMEM)])
            run("memkv0")
            run("memkv1")
            act.wait_ge(s_("x_ready"), 1)
            squares(KD, lambda k: x[:, k, :], NT, lambda k: None)
            act.wait_ge(panel_done, 8)
            for k in range(KD):
                split_hi(k, x[:, k, :], gain("mix_pre", k, 0))
            root_x("x0")
            run("win0", ahead=False)

            act.wait_ge(s_("lam_ready"), 1)
            tell(A.activation(lam[:, 64:64 + PAIRS], lam[:, 64:64 + PAIRS], ACT.Exp), s_("s5_act"), 1)
            act.wait_ge(s_("angles_ready"), 1)
            for n, (dst, src, fn, sca) in enumerate((
                    (3, 1, ACT.Exp, 1.0), (6, 1, ACT.Exp, 8.0), (4, 12, ACT.Sin, 1.0), (5, 13, ACT.Sin, 1.0))):
                tell(A.activation(s5s[:, dst, :], s5s[:, src, :], fn, scale=sca), s_("s5_act"), n + 2)
            for t in range(THIRDS):
                act.wait_ge(s_("yz_used"), t + 1)
                for m in range(2):
                    k = 2 * t + m
                    do(A.activation(y[:, k, :], y[:, k, :], ACT.Gelu_apprx_tanh))
                mark(s_("gelu_made"))
            act.wait_ge(s_("x_free"), 1)
            for k in range(KS):
                split_hi(k, y[:, k, 0:T].rearrange("p (j k) -> p k j", j=CHUNK), None, slice(0, T))
                split_hi(k, y[:, k, T:NT], None, slice(T, NT))
            run("glu", ahead=False, started=False)
            act.wait_ge(s_("gate_ready"), 1)
            for m in range(KS):
                tell(A.activation(gate[:, m, :], gate[:, m, :], ACT.Sigmoid), s_("sig_made"), m + 1)
            for m in range(KS):
                act.wait_ge(s_("gated"), m + 1)
                split_hi(m, gate[:, m, :])

            def mem_attention(l, m):
                for h in range(MEMH):
                    for a_ in range(2):
                        n = 8 * l + 2 * h + a_
                        act.wait_ge(s_("mneg"), n + 1)
                        for qq in range(2):
                            st = m["st"][:, a_, :]
                            ins = A.activation(m["p"][:, a_, qq, :], bank(("mS", l, h, a_))[:, 256 * qq:256 * qq + 256],
                                               ACT.Exp, bias=st[:, 2 + qq:3 + qq], scale=SCALE,
                                               accum_out=st[:, 4 + qq:5 + qq])
                            if qq:
                                freed(own, ins, ("mS", l, h, a_))
                            else:
                                do(ins)
                        mark(s_("mexp"))
                act.wait_ge(s_("dexp_in"), 1 + 2 * l)
                tell(A.activation(m["s"][:], m["s"][:], ACT.Exp), s_("dexp"), 1 + 2 * l)

            mem_attention(0, mb[0])
            ny = [0]

            def post(name, post_name, l, nxt, nl):
                ny[0] += 1
                act.wait_ge(s_("y_full"), ny[0])
                squares(KD, lambda k: y[:, k, :], NT, lambda k: None)
                root_x(f"{post_name}{l}")
                if nxt is not None:
                    for k in range(KD):
                        act.wait_ge(s_("x_updated"), 8 * (ny[0] - 1) + k + 1)
                        split_hi(k, x[:, k, :], gain(nxt, k, nl))
                    squares(KD, lambda k: x[:, k, :], NT, lambda k: None)
                    root_x(name)

            def ffn(l):
                for f in range(2):
                    base = PH[f"up{l}{f}"][2]
                    done = 22 * l + 11 * f

                    def work(it, half):
                        fb = it + (f * KH + half * KF)
                        uu, yy = uc[half], yc[half]
                        act.wait_ge(panel_read, it * 2 + (base + half + 1))
                        A.activation(newconv[:, bass.ds(fb, 1), :].rearrange("p a t -> p (a t)"),
                                     uu[:, T:T + 2 + NB], ACT.Copy).then_inc(act_step, 1)
                        act.wait_ge(s_("h_made"), it + (done + 1))
                        A.activation(yy[:], uu[:, 2:2 + NT], ACT.Identity,
                                     bias=convw[:, l, bass.ds(it + (f * KH + half * KF + 132), 1)],
                                     scale=convw[:, l, bass.ds(it + (f * KH + half * KF + 88), 1)]
                                     ).then_inc(s_("tap_made"), 1)
                        if half == 1:
                            act.wait_ge(s_("conv_made"), it * 2 + (2 * done + 1))
                            A.activation(sg[:], yc[0][:], ACT.Silu).then_inc(s_("silu_made"), 1)

                    run(f"up{l}{f}", work)
                    run(f"down{l}{f}", ahead=(f == 0))
                    own.n += 22

            run("wout0", started=False)
            post("f0", "o", 0, "ffn_pre", 0)
            ffn(0)
            post("x1", "d", 0, "kv", 0)

            def kv_work(m):
                act.wait_ge(s_("kvT_ready"), m + 1)
                if m < 6:
                    do(A.activation(kh[0:DH, 2 * m, :], kvT[0:DH, 0:T], ACT.Copy))
                    tell(A.activation(kh[0:DH, 2 * m + 1, :], kvT[DH:P, 0:T], ACT.Copy), s_("kh_made"), m + 1)

            kb, n, base, _ = PH["kv"]
            hi(kb, base)
            hi(kb, base + 1)
            for m in range(n):
                if m + 2 <= n:
                    hi(KD, base + m + 2)
                kv_work(m)
            act.wait_ge(s_("nabs_ready"), 1)
            do(A.activation(lf[:, 2, :], lf[:, 1, :], ACT.Exp))
            sync()
            tell(A.activation(lf[:, 2, :], lf[:, 2, :], ACT.Ln, bias=1.0), s_("log_made"), 1)
            act.wait_ge(panel_done, PH["kvf"][2] + 1)
            for k in range(KD):
                split_hi(k, x[:, k, :], gain("mix_pre", k, 1))
            run("win1", ahead=False, started=False)
            for s in range(2):
                act.wait_ge(s_(f"ktok_out{s}"), 48)
            act.wait_ge(s_("stored"), 16 * 19)
            act.wait_ge(s_("aug_in"), 32)
            for i in range(STEPS):
                if 1 <= i <= HEADS:
                    h, c = i - 1, 0
                    if h >= 2:
                        full(act, ("O", h - 2))
                    for a_ in range(3):
                        w = 256 if a_ == 2 else 512
                        act.wait_ge(s_("t_masked"), 3 * h + a_ + 1)
                        ins = A.activation(PT[h % 2][:, c:c + w], bank(("T", h, a_))[:, 0:w], ACT.Exp, scale=SCALE)
                        freed(own, ins, ("T", h, a_))
                        c += w
                    mark(s_("pt_ready"))
                for b in range(NB):
                    if q_step(b) == i:
                        if b >= 2:
                            act.wait_ge(s_("k_product"), PAGES * (b - 1))
                        for a_ in range(2):
                            full(act, ("q", b, a_))
                            freed(own, A.activation(qb[b % 2][:, 384 * a_:384 * a_ + 384],
                                                    bank(("q", b, a_))[:, 0:384], ACT.Copy), ("q", b, a_))
                        mark(s_("qb_ready"))
                if i < HEADS:
                    full(act, ("M", i))
                    freed(own, A.activation(qh[96:97, i, :], bank(("M", i))[0:1, :], ACT.Copy), ("M", i))
                    mark(s_("qrow_max"))
            act.wait_ge(s_("dexp_in"), 2)
            tell(A.activation(sc[:], sc[:], ACT.Exp), s_("dexp"), 2)
            mem_attention(1, mb[1])
            run("wout1", started=False)
            post("f1", "o", 1, "ffn_pre", 1)
            ffn(1)
            post("", "d", 1, None, 0)

        @block.tensor
        def _(pe):
            def kv_turn(m):
                pe.wait_ge(s_("kvT_ready"), m + 1)
                o = take(("kvtok", m))
                for c in range(4):
                    ins = turn(o[:, c * P:c * P + P], kvT[:, c * P:c * P + P], P)
                give(ins, ("kvtok", m))
                give(turn(take(("kvsamp", m))[0:NB, 0:P], kvT[:, T:NT], P), ("kvsamp", m))

            order = {True: 0, False: 0}

            def take(job):
                ring, (o, _, free_, before) = job in J, place(job)
                assert (J if ring else FJ)[job] == order[ring], job
                order[ring] += 1
                if before:
                    pe.wait_ge(free_, before)
                return o

            def give(ins, job):
                ins.then_inc(place(job)[1], 1)

            def all_read(frees, jobs):
                for n, free_ in enumerate(frees):
                    pe.wait_ge(free_, (jobs - n + len(frees) - 1) // len(frees))

            def product(q, slot, kb, rhs, cols, wait_k=None, free=True):
                pe.wait_ge(lo_made, q + 1)
                if free:
                    pe.wait_ge(panel_read, q - 1)
                for k in range(kb):
                    if wait_k is not None:
                        wait_k(k)
                    xh, xl = rhs(k)
                    for n_, (w, r) in enumerate(((w_hi, xh), (w_hi, xl), (w_lo, xh))):
                        for b_, (c0, c1) in enumerate(cols):
                            ins = pe.matmul(big[2 * slot + b_][:, 0:c1 - c0], w[slot][:, k, :], r[:, c0:c1],
                                            start=(k == 0 and n_ == 0), stop=(k == kb - 1 and n_ == 2))
                ins.then_inc(panel_done, 1)

            xs_ = lambda k: (x_hi[:, k, :], x_lo[:, k, :])

            def phase(name, rhs=xs_, cols=HALF, wait_k=None):
                kb, n, base, _ = PH[name]
                peel = 2 if wait_k is not None else 0
                if base < 2 or n <= 2:
                    peel = n
                for i in range(peel):
                    product(base + i, (base + i) % 2, kb, rhs, cols, wait_k if i == 0 else None, base + i >= 2)
                if n > peel:
                    with pe.Fori(0, (n - peel) // 2) as it:
                        for half in range(2):
                            c = base + peel + half
                            product(it * 2 + c, c % 2, kb, rhs, cols)

            nsplit = [0]

            def x_split(k):
                pe.wait_ge(s_("xlo_made"), nsplit[0] + k + 1)

            nsums = [0]

            def stats(jobs):
                nsums[0] += 1
                pe.wait_ge(s_("sumsq_ready"), nsums[0])
                for job, c0, c1 in jobs:
                    o = take(job)
                    give(pe.matmul(o[:, 0:c1 - c0], meanw[:], sumsq[:, c0:c1], start=True, stop=True), job)

            def stats_x(name):
                stats([(("ms", name, n), c0, c1) for n, (c0, c1) in enumerate(HALF)])

            def turn(o, src, n):
                return pe.transpose(o, src, ident[0:n, 0:n])

            pe.wait_ge(s_("consts"), 1)
            pe.wait_ge(s_("rows_in"), 16 * 8)
            give(turn(take(("rows",))[:, 0:100], rows[:], 100), ("rows",))
            pe.wait_ge(s_("conv_in"), 16 * 10)
            for l in range(2):
                for a_ in range(2):
                    job = ("conv", l, a_)
                    give(turn(take(job)[:, 0:88], crow[:, 2 * l + a_, :], 88), job)
            for l in range(2):
                for a_ in range(2):
                    job = ("state", l, a_)
                    o = take(job)
                    for n in range(4 if a_ == 0 else 2):
                        r = 4 * a_ + n
                        m = P if r < 5 else 64
                        ins = turn(o[:, n * P:n * P + m], srow[0:m, l, r, :], m)
                    give(ins, job)
            pe.wait_ge(s_("lrow_ready"), 1)
            pe.wait_ge(s_("lam_in"), 48)
            give(turn(take(("lam",))[:, 0:96], lrow[0:96, :], 96), ("lam",))
            pe.wait_ge(s_("mem_in"), 16)
            for a_ in range(4):
                o = take(("memT", a_))
                for n in range(4):
                    k, c = 2 * a_ + n // 2, n % 2
                    ins = turn(o[:, n * P:n * P + P], mem_in[:, c, k * P:k * P + P], P)
                give(ins, ("memT", a_))
            pe.wait_ge(s_("x_in"), 32)
            for k in range(KD):
                o = take(("xT", k))
                for c in range(4):
                    ins = turn(o[:, c * P:c * P + P], x_tok[:, c, k * P:k * P + P], P)
                give(ins, ("xT", k))
            o = take(("xsT",))
            for k in range(KD):
                ins = turn(o[:, k * NB:k * NB + NB], xs_tok[:, k * P:k * P + P], NB)
            give(ins, ("xsT",))

            stats([(("ms_mem",), 0, NMEM)])
            pe.wait_ge(s_("xlo_made"), 2 * KD)
            nsplit[0] += 2 * KD
            for l in range(2):
                phase(f"memkv{l}", cols=((l * NMEM, (l + 1) * NMEM),))
                for m in range(4):
                    job = ("memtok", l, m)
                    o = take(job)
                    q = PH[f"memkv{l}"][2] + m
                    pe.wait_ge(panel_read, q + 1)
                    src = mem_kT[:, l, m, :] if m < 2 else sq[:, m - 2, 0:NMEM]
                    for c in range(2):
                        ins = turn(o[:, c * P:c * P + P], src[:, c * P:c * P + P], P)
                    give(ins, job)
            stats_x("x0")
            phase("win0", wait_k=x_split)
            nsplit[0] += KD

            pe.wait_ge(s_("h0_in"), 64)
            for ri in range(2):
                for half in range(2):
                    job = ("h0", ri, half)
                    give(turn(take(job)[:, 0:96], hrow[:, ri, half, :], 96), job)
            for t in range(THIRDS):
                pe.wait_ge(s_("bc_in"), 16 * 6 * (t + 1))
                job = ("cT", t)
                o = take(job)
                for ri in range(2):
                    for m in range(2):
                        ins = turn(o[:, 256 * ri + P * m:256 * ri + P * m + P],
                                   c_in[:, ri, m].rearrange("p d n -> p (d n)"), P)
                give(ins, job)
                pe.wait_ge(s_("bp_ready"), t + 1)
                for a_ in range(TP // 2):
                    job = ("bT", t, a_)
                    o = take(job)
                    for n in range(4):
                        ins = turn(o[:, n * P:n * P + P], bp[:, n % 2, 2 * a_ + n // 2, :], P)
                    give(ins, job)
                pe.wait_ge(s_("cp_ready"), t + 1)
                for a_ in range(TG // 4):
                    job = ("K", t, a_)
                    o = take(job)
                    for n, g in enumerate(same_side(a_)):
                        r = slice(STATE * (g % 2), STATE * (g % 2) + STATE)
                        for ri in range(2):
                            ins = pe.matmul(o[0:CH, n * P:n * P + P], bb[r, ri, g // 2, :], cp[r, ri, g // 2, 0:P],
                                            start=(ri == 0), stop=(ri == 1))
                    give(ins, job)
                pe.wait_ge(s_("u_in"), 16 * 10 * (t + 1))
                pe.wait_ge(s_("bT_ready"), t + 1)
                for a_ in range((TP + 2) // 3):
                    job = ("V", t, a_)
                    o = take(job)
                    W = NCH + NB
                    for n in range(min(3, TP - 3 * a_)):
                        j = 3 * a_ + n
                        for ri in range(2):
                            for e in range(2):
                                r = slice(STATE * e, STATE * e + STATE)
                                ins = pe.matmul(o[r, (2 * n + ri) * W:(2 * n + ri + 1) * W], bT[:, j, ri, r],
                                                u[:, 2 * j + e, NB:], start=True, stop=True)
                    give(ins, job)
                pe.wait_ge(s_("toep_in"), 16 * CHUNK * (t + 1))
                pe.wait_ge(s_("hp_ready"), t + 1)
                for a_ in range(TG // 4):
                    job = ("Y", t, a_)
                    o = take(job)
                    for n, g in enumerate(same_side(a_)):
                        r = slice(STATE * (g % 2), STATE * (g % 2) + STATE)
                        oo = o[:, n * W:(n + 1) * W]
                        pe.matmul(oo, cp[r, 0, g // 2, CH:], hp[r, 0, g // 2, 0:W], start=True, stop=False)
                        pe.matmul(oo, cp[r, 1, g // 2, CH:], hp[r, 1, g // 2, 0:W], start=False, stop=False)
                        ins = pe.matmul(oo, toep[:, g, :], u[:, g, 0:W], start=False, stop=True)
                    give(ins, job)
            pe.wait_ge(s_("hfin_ready"), 1)
            for ri in range(2):
                job = ("fin", ri)
                o = take(job)
                for a_ in range(2):
                    ins = turn(o[0:108, a_ * P:a_ * P + P],
                               hfin[:, ri].rearrange("p b j -> p (b j)")[:, 108 * a_:108 * a_ + 108], P)
                give(ins, job)
            pe.wait_ge(s_("xlo_made"), nsplit[0] + 2 * KS)
            nsplit[0] += 2 * KS
            phase("glu")

            ndec = [0]

            def decode_max(jT, jM, jD, st, BH):
                ndec[0] += 1
                pe.wait_ge(s_("dmax1"), ndec[0])
                give(turn(take(jT)[0:BH, 0:P], st[:, 0, 0:BH], P), jT)
                pe.wait_ge(s_("dmax2"), ndec[0])
                give(pe.matmul(take(jM)[:, 0:BH], ones[0:BH, :], st[0:BH, 2, 0:BH], start=True, stop=True), jM)
                pe.wait_ge(s_("dsum"), ndec[0])
                give(pe.matmul(take(jD)[:, 0:BH], ones[:], st[:, 3, 0:BH], start=True, stop=True), jD)
                pe.wait_ge(s_("dp_ready"), ndec[0])

            def q_rows(l):
                for a_ in range(2):
                    job = ("qrow", l, a_)
                    o = take(job)
                    for n in range(4):
                        k = 4 * a_ + n
                        src = y[:, k, T:NT] if (k >= 6 or l == 0) else qs[:, k, :]
                        ins = turn(o[0:NB, n * P:n * P + P], src, P)
                    give(ins, job)

            def mem_attention(l, m):
                if l == 0:
                    q_rows(l)
                for h in range(MEMH):
                    r = slice(DH * (h % 2), DH * (h % 2) + DH)
                    for a_ in range(2):
                        job = ("mS", l, h, a_)
                        o = take(job)
                        for qq in range(2):
                            c = (2 * a_ + qq) * P
                            ins = pe.matmul(o[:, 256 * qq:256 * qq + 256], y[r, 6 + h // 2, c:c + P],
                                            mem_kT[r, l, h // 2, :], start=True, stop=True)
                        give(ins, job)
                    if l and h:
                        pv_sum(2 * h - 1)
                    if l:
                        pv(2 * h)
                    for a_ in range(2):
                        pe.wait_ge(s_("mp_ready"), 8 * l + 2 * h + a_ + 1)
                        job = ("mT", l, h, a_)
                        o = take(job)
                        for kc in range(2):
                            for qq in range(2):
                                ins = turn(o[:, (2 * kc + qq) * P:(2 * kc + qq + 1) * P],
                                           m["p"][:, a_, qq, kc * P:kc * P + P], P)
                        give(ins, job)
                    if l:
                        pv_sum(2 * h)
                        pv(2 * h + 1)
                    pe.wait_ge(s_("mpT_ready"), 4 * l + h + 1)
                    job = ("mO", l, h)
                    o = take(job)
                    for kc in range(2):
                        ins = pe.matmul(o[r, :], mem_tok[:, l, kc, 256 + h * DH:256 + h * DH + DH], m["pT"][:, kc, :],
                                        start=(kc == 0), stop=(kc == 1))
                    give(ins, job)
                if l:
                    pv_sum(NB - 1)
                pe.wait_ge(s_("qrow_ready"), l + 1)
                for b in range(NB):
                    job = ("mq", l, b)
                    give(pe.matmul(take(job)[:, 0:256], sel[:, b, :], qrow[:, SEQW:D], start=True, stop=True), job)
                decode_max(("mmaxT", l), ("mmax", l), ("mden", l), m["dst"], NB * MEMH)
                pe.wait_ge(s_("mv_in"), 16 * (l + 1))
                job = ("mpv", l)
                o = take(job)
                for b in range(NB):
                    for f in range(2):
                        for c in range(2):
                            cc = (2 * b + f) * 2
                            ins = pe.matmul(o[:, cc:cc + 2], m["v"][:, b, c, f * P:f * P + P],
                                            m["s"][:, b, c, 2 * f:2 * f + 2], start=(c == 0), stop=(c == 1))
                give(ins, job)

            mem_attention(0, mb[0])
            nsplit[0] += KS
            pe.wait_ge(s_("xlo_made"), nsplit[0])
            pe.wait_ge(s_("mem_done"), 1)
            phase("wout0")

            def ffn(l):
                for f in range(2):
                    phase(f"up{l}{f}", wait_k=x_split if f == 0 else None)
                    if f == 0:
                        nsplit[0] += KD
                    pe.wait_ge(s_("h_made"), 1 + 22 * l + 11 * (f + 1))
                    phase(f"down{l}{f}", rhs=lambda k: (h_hi[:, k, :], h_lo[:, k, :]))
                pe.wait_ge(s_("tap_made"), 44 * (l + 1))
                for a_ in range(KF * 2 // 4):
                    job = ("cout", l, a_)
                    o = take(job)
                    for n in range(4):
                        ins = turn(o[0:2 + NB, n * P:n * P + P], newconv[:, 4 * a_ + n, :], P)
                    give(ins, job)

            stats_x("o0")
            stats_x("f0")
            ffn(0)
            stats_x("d0")
            stats_x("x1")

            kb, n, base, _ = PH["kv"]
            for m in range(n):
                product(base + m, (base + m) % 2, kb, xs_, HALF, x_split if m == 0 else None)
                if m:
                    kv_turn(m - 1)
            nsplit[0] += KD
            kv_turn(11)
            q = PH["kvf"][2]
            pe.wait_ge(lo_made, q + 1)
            pe.wait_ge(panel_read, q - 1)
            for k in range(KD):
                for n_, (w, r_) in enumerate(((w_hi, x_hi), (w_hi, x_lo), (w_lo, x_hi))):
                    for b_, (c0, c1) in enumerate(HALF):
                        ins = pe.matmul(big[2 * (q % 2) + b_][:, 0:c1 - c0], w[q % 2][:, k, :], r_[:, k, c0:c1],
                                        start=(k == 0 and n_ == 0), stop=(k == KD - 1 and n_ == 2))
            ins.then_inc(panel_done, 1)
            pe.wait_ge(s_("lf_ready"), 1)
            job = ("logf",)
            o = take(job)
            for c in range(4):
                turn(o[:, 12 * c:12 * c + 12], lf[:, 1, c * P:c * P + P], HEADS)
            give(turn(o[0:NB, 48:60], lf[:, 1, T:NT], HEADS), job)
            phase("win1", wait_k=x_split)
            nsplit[0] += KD

            pe.wait_ge(s_("aug_in"), 32)
            pe.wait_ge(s_("q1_ready"), 1)
            pe.wait_ge(s_("kh_made"), 6)
            pe.wait_ge(s_("vtok_ready"), 6)
            q_rows(1)
            pe.wait_ge(panel_read, PH["win1"][2] + 8)
            all_read(misc_free, J[("fmaxT",)])
            BH = NB * HEADS
            AQ = (((3, 0, 512),), ((2, 0, 384), (0, 384, 128)), ((1, 0, 256),))
            AK = (((0, 0, 512),), ((1, 0, 384), (3, 384, 128)), ((2, 0, 256),))
            PT_AT = (0, 512, 1024, 896)
            for i in range(STEPS):
                if i < HEADS:
                    for a_ in range(3):
                        o = take(("S", i, a_))
                        for qi, c, n in AQ[a_]:
                            ins = pe.matmul(o[:, c:c + n], qh[0:DH + 2, i, qi * P:qi * P + P], kh[0:DH + 2, i, 0:n],
                                            start=True, stop=True)
                        give(ins, ("S", i, a_))
                if i >= 3:
                    h = i - 3
                    o = take(("R", h))
                    pe.wait_ge(s_("rinv_ready"), h + 1)
                    r = slice(DH * (h % 2), DH * (h % 2) + DH)
                    give(pe.matmul(o[r, :], ones[0:1, 0:DH], rinv[:], start=True, stop=True), ("R", h))
                if 1 <= i <= HEADS:
                    h = i - 1
                    pe.wait_ge(s_("qrow_max"), i)
                    for a_ in range(3):
                        o = take(("T", h, a_))
                        for kc, c, n in AK[a_]:
                            ins = pe.matmul(o[:, c:c + n], kh[0:97, h, kc * P:kc * P + P], qh[0:97, h, T - n:T],
                                            start=True, stop=True)
                        give(ins, ("T", h, a_))
                for b in range(NB):
                    if q_step(b) == i:
                        pe.wait_ge(s_("qrow_ready"), 2)
                        for a_ in range(2):
                            o = take(("q", b, a_))
                            give(pe.matmul(o[:, 0:384], sel[:, b, :], qrow[:, 384 * a_:384 * a_ + 384], start=True,
                                           stop=True), ("q", b, a_))
                if i == DECAY_STEP:
                    pe.wait_ge(s_("pre_ready"), 1)
                    o = take(("dtot",))
                    pe.matmul(o[:, 0:BH], ones[:], fst[:, 5, 0:BH], start=True, stop=False)
                    give(pe.matmul(o[:, 0:BH], ones[0:NB, :], lmask[:].rearrange("r b h -> r (b h)"), start=False,
                                   stop=True), ("dtot",))
                    for a_ in range(2):
                        o = take(("dc", a_))
                        bs = slice(4 * a_, 4 * a_ + 4)
                        pe.matmul(o[:, 0:384], tri[:], logf[:, bs].rearrange("p b g h -> p (b g h)"), start=True,
                                  stop=False)
                        give(pe.matmul(o[:, 0:384], ones[:], pre[:, bs].rearrange("p b g h -> p (b g h)"),
                                       start=False, stop=True), ("dc", a_))
                if i < HEADS:
                    o = take(("M", i))
                    pe.wait_ge(s_("nmax_ready"), i + 1)
                    for qi in range(4):
                        ins = pe.matmul(o[0:1, qi * P:qi * P + P], nmax[i % 2][:, qi:qi + 1], ident[:], start=True,
                                        stop=True)
                    give(ins, ("M", i))
                if 2 <= i <= HEADS + 1:
                    h = i - 2
                    o = take(("O", h))
                    pe.wait_ge(s_("pt_ready"), h + 1)
                    for kc in range(4):
                        n = T - kc * P
                        ins = pe.matmul(o[0:DH + 1, T - n:T], vtok[:, kc, h, :], PT[h % 2][:, PT_AT[kc]:PT_AT[kc] + n],
                                        start=(kc == 0), stop=(kc == 3))
                    give(ins, ("O", h))
            all_read(fox_free, len(FJ))

            def pv(b):
                if b >= 2:
                    pe.wait_ge(s_("vm_ready"), b - 1)
                o = [big[2 * (b % 2) + a_] for a_ in range(2)]
                for pg in range(PAGES):
                    pe.wait_ge(s_(f"page_in{pg}"), 16 * (NB + b + 1))
                    for a_ in range(2):
                        ins = pe.matmul(o[a_][0:HEADS, 0:384], sc[:, b, pg, :], page[pg][:, 384 * a_:384 * a_ + 384],
                                        start=(pg == 0), stop=False)
                    ins.then_inc(s_("v_used"), 1)
                for a_ in range(2):
                    ins = pe.matmul(o[a_][0:HEADS, 0:384], sc[0:NB, b, PAGES, :], kvs[:, 1, 384 * a_:384 * a_ + 384],
                                    start=False, stop=True)
                ins.then_inc(s_("pv_done"), 1)

            def pv_sum(b):
                o = take(("fpv", b))
                pe.wait_ge(s_("vm_ready"), b + 1)
                for f in range(6):
                    ins = pe.matmul(o[:, f:f + 1], vm[0:HEADS, f * P:f * P + P], ones[0:HEADS, 0:1], start=True,
                                    stop=True)
                give(ins, ("fpv", b))

            decode_max(("fmaxT",), ("fmax",), ("fden",), fst, BH)
            mem_attention(1, mb[1])
            pe.wait_ge(s_("fox_done"), 1)
            pe.wait_ge(s_("mem_done"), 2)
            phase("wout1")
            stats_x("o1")
            stats_x("f1")
            ffn(1)
            stats_x("d1")
            pe.wait_ge(s_("x_updated"), 32)
            for c in range(5):
                for a_ in range(2):
                    job = ("yT", c, a_)
                    o = take(job)
                    for n in range(4):
                        k = 4 * a_ + n
                        if c < 4:
                            ins = turn(o[:, n * P:n * P + P], x[:, k, c * P:c * P + P], P)
                        else:
                            ins = turn(o[0:NB, n * P:n * P + P], x[:, k, T:NT], P)
                    give(ins, job)


OUTS = [
    ("y_prompt", (1, T, D)), ("y_sample", (NB, 1, D)),
    ("prompt_ssm_re", (1, 1, GROUPS, STATE)), ("prompt_ssm_im", (1, 1, GROUPS, STATE)),
    ("prompt_k", (1, T, HEADS, DH)), ("prompt_v", (1, T, HEADS, DH)), ("prompt_logf", (1, T, HEADS)),
    ("prompt_mem_k", (2, 1, NMEM, MEMH, DH)), ("prompt_mem_v", (2, 1, NMEM, MEMH, DH)),
    ("prompt_ffn_conv", (2, 1, 2, 2 * DFF)),
    ("sample_ssm_re", (1, NB, GROUPS, STATE)), ("sample_ssm_im", (1, NB, GROUPS, STATE)),
    ("sample_k", (NB, 1, HEADS, DH)), ("sample_v", (NB, 1, HEADS, DH)), ("sample_logf", (NB, 1, HEADS)),
    ("sample_ffn_conv", (2, NB, 2, 2 * DFF)),
]


def kernel(**inputs):
    from concourse import bacc
    from concourse.bass_utils import run_bass_kernel_spmd

    nc = bacc.Bacc("TRN2", target_bir_lowering=False, num_devices=1)
    arrays, ins, outs = {}, {}, {}
    for name, a in inputs.items():
        a = np.ascontiguousarray(a)
        arrays[f"in_{name}"] = a
        ins[name] = nc.dram_tensor(f"in_{name}", a.shape, mybir.dt.from_np(a.dtype), kind="ExternalInput").ap()
    for name, shape in OUTS:
        outs[name] = nc.dram_tensor(f"out_{name}", shape, F32, kind="ExternalOutput").ap()
    program(nc, ins, outs)
    r = run_bass_kernel_spmd(nc, [arrays], core_ids=[0])
    return tuple(r.results[0][f"out_{name}"] for name, _ in OUTS)
```

```python
import math
from contextlib import ExitStack

import numpy as np

import concourse.bass as bass
from concourse import mybir

F32 = mybir.dt.float32
F32R = mybir.dt.float32r
I32 = mybir.dt.int32
ALU = mybir.AluOpType
ACT = mybir.ActivationFunctionType
AX = mybir.AxisListType

P = 128
T = 512
NB = 8
NT = T + NB
HALF = ((0, 264), (264, NT))
D = 1024
KD = D // P
DFF = 2816
KF = DFF // P
KH = KF // 2
SEQW = 768
KS = SEQW // P
HEADS = 12
MEMH = 4
DH = 64
NMEM = 256
PAST = 1024
PAGE = 128
PAGES = PAST // PAGE
GROUPS, STATE, CH = 48, 64, 16
PAIRS = GROUPS // 2
CHUNK = 8
NCH = T // CHUNK
THIRDS = 3
TP = PAIRS // THIRDS
TG = GROUPS // THIRDS
EPS = 1e-6
NEG = -1e30
SCALE = DH ** -0.5
TWO_PI = 2 * math.pi
ROUND = 12582912.0
PI_LO = 3.1415925


class Own:

    def __init__(self, eng, step):
        self.eng, self.step, self.n, self.last = eng, step, 0, None

    def do(self, ins):
        self.n += 1
        ins.then_inc(self.step, 1)
        self.last = (self.step, self.n)

    def tell(self, ins, sem, value):
        ins.then_inc(sem, 1)
        self.last = (sem, value)

    def mark(self, sem):
        self.sync()
        self.eng.sem_inc(sem, 1)

    def sync(self):
        self.eng.wait_ge(*self.last)


def phases():
    out = [("memkv0", KD, 4), ("memkv1", KD, 4), ("win0", KD, 8), ("glu", KS, 6), ("wout0", KD, 8)]
    for l in range(2):
        if l:
            out += [("kv", KD, 12), ("kvf", KD, 1), ("win1", KD, 8), ("wout1", KD, 8)]
        for f in range(2):
            out += [(f"up{l}{f}", KD, 2 * KH), (f"down{l}{f}", KH, 8)]
    table, base = {}, 0
    for n, (name, kb, panels) in enumerate(out):
        nxt = out[n + 1][0] if n + 1 < len(out) else None
        table[name] = (kb, panels, base, nxt)
        base += panels
    return table, base


def same_side(a):
    return [8 * (a // 2) + 2 * n + a % 2 for n in range(4)]


def samples_of(l, h):
    return range(2 * h, 2 * h + 2) if l else range(max(0, 3 * h - 3), min(NB, 3 * h))


def misc_jobs():
    jobs = [("rows",)] + [("memT", a) for a in range(4)] + [("ms_mem",)]
    jobs += [("memtok", 0, m) for m in range(4)] + [("lam",)]
    jobs += [("conv", l, a) for l in range(2) for a in range(2)]
    jobs += [("state", l, a) for l in range(2) for a in range(2)]
    jobs += [("xT", k) for k in range(KD)] + [("xsT",)] + [("memtok", 1, m) for m in range(4)]
    jobs += [("cT", 0), ("ms", "x0", 0), ("ms", "x0", 1)]
    jobs += [("h0", ri, a) for ri in range(2) for a in range(2)]
    for t in range(THIRDS):
        jobs += [*[("bT", t, a) for a in range(TP // 2)], *[("V", t, a) for a in range((TP + 2) // 3)]]
        jobs += [("Y", t - 1, a) for a in range(TG // 4) if t]
        jobs += [("K", t, a) for a in range(TG // 4)] + [("cT", t + 1)] * (t + 1 < THIRDS)
    jobs += [("Y", THIRDS - 1, a) for a in range(TG // 4)]
    jobs += [("fin", ri) for ri in range(2)]
    for l in range(2):
        if l:
            jobs += [x for m in range(12) for x in (("kvtok", m), ("kvsamp", m))]
            jobs += [("logf",)]
        jobs += [("qrow", l, a) for a in range(2) if l or a]
        for h in range(MEMH):
            jobs += [("mS", l, h, 0), ("mS", l, h, 1)] + [("mq", l, b) for b in samples_of(l, h)]
            jobs += [("fpv", 2 * h - 1)] if l and h else []
            jobs += [("mT", l, h, 0), ("mT", l, h, 1)]
            jobs += [("fpv", 2 * h)] if l else []
            jobs += [("mO", l, h)]
        jobs += [("fpv", NB - 1)] if l else []
        jobs += [("mmaxT", l), ("mmax", l), ("mden", l), ("mpv", l)]
        jobs += [("ms", f"o{l}", 0), ("ms", f"o{l}", 1), ("ms", f"f{l}", 0), ("ms", f"f{l}", 1)]
        jobs += [("cout", l, a) for a in range(KF * 2 // 4)]
        jobs += [("ms", f"d{l}", 0), ("ms", f"d{l}", 1)]
        if l == 0:
            jobs += [("ms", "x1", 0), ("ms", "x1", 1)]
    jobs += [("yT", c, a) for a in range(2) for c in range(5)]
    return {name: j for j, name in enumerate(jobs)}


def conv_rows(m):
    return range(2 * m, min(2 * m + 2, 2 * KF // 4))


STEPS = HEADS + 3
DECAY_STEP = HEADS - 1
SOFTMAX_STEP = HEADS


def q_step(b):
    return 3 * b // 2


def fox_jobs():
    jobs = []
    for i in range(STEPS):
        jobs += [("S", i, a) for a in range(3)] if i < HEADS else []
        jobs += [("R", i - 3)] if i >= 3 else []
        jobs += [("T", i - 1, a) for a in range(3)] if 1 <= i <= HEADS else []
        jobs += [("q", b, a) for b in range(NB) if q_step(b) == i for a in range(2)]
        jobs += [("dtot",), ("dc", 0), ("dc", 1)] if i == DECAY_STEP else []
        jobs += [("M", i)] if i < HEADS else []
        jobs += [("O", i - 2)] if 2 <= i <= HEADS + 1 else []
        jobs += [("fmaxT",), ("fmax",), ("fden",)] if i == SOFTMAX_STEP else []
    return {name: j for j, name in enumerate(jobs)}


def program(nc, I, O):
    PH, PANELS = phases()
    J, FJ = misc_jobs(), fox_jobs()
    ctx = ExitStack()
    with ctx:
        def sb(name, shape, dt=F32):
            return ctx.enter_context(nc.sbuf_tensor(name, shape, dt))

        ident = sb("ident", [P, P])
        ones = sb("ones", [P, P])
        meanw = sb("meanw", [P, P])
        tri = sb("tri", [P, P])
        causal = sb("causal", [P, P])
        sel = sb("sel", [NB, NB, P])
        gains = sb("gains", [P, 100])
        convw = sb("convw", [P, 2, 4 * 2 * KF])
        convs = sb("convs", [P, 2, 2 * NB, 2 * KF])
        newconv = sb("newconv", [P, 2 * KF, 2 + NB])
        stats_at = nc.sbuf_base
        rstd = sb("rstd", [P, NT])
        sd = sb("sd", [P, NT])
        sumsq = sb("sumsq", [P, NT])
        sq = sb("sq", [P, 2, NT])
        stats_end = nc.sbuf_base
        rstd_mem = sb("rstd_mem", [P, NMEM])
        x = sb("x", [P, KD, NT])
        y_at = nc.sbuf_base
        y = sb("y", [P, KD, NT])
        weights_at = nc.sbuf_base
        raw = [sb(f"raw{s}", [P, KH, P]) for s in range(2)]
        w_hi = [sb(f"w_hi{s}", [P, KH, P], F32R) for s in range(2)]
        w_lo = [sb(f"w_lo{s}", [P, KH, P], F32R) for s in range(2)]
        weights_end = nc.sbuf_base
        mem_kT = sb("mem_kT", [P, 2, 2, NMEM])
        mem_tok = sb("mem_tok", [P, 2, 2, 512])
        qrow = sb("qrow", [NB, D])
        bf = sb("bf", [HEADS, 1])
        eps = sb("eps", [P, 1])
        root_warm = sb("root_warm", [P, 1])
        qs = sb("qs", [P, 6, NB])
        pages = sb("pages", [1, NB * PAGES], I32)

        class Arena:

            def __init__(self, at, top):
                self.at, self.top = at, top

            def __call__(self, name, shape, dt=F32):
                size = (int(np.prod(shape[1:])) * 4 + 31) // 32 * 32
                assert self.at + size <= self.top, (name, self.at + size - self.top)
                t = nc.alloc_sbuf_tensor_at(name, shape, dt, offset=self.at)
                self.at += size
                return t

        nc_base = nc.sbuf_base
        start = (nc.sbuf_base + 31) // 32 * 32
        top = nc.sbuf_usable_end // 32 * 32
        split = Arena(start, top)
        x_hi = split("x_hi", [P, KD, NT], F32R)
        x_lo = split("x_lo", [P, KD, NT], F32R)
        free = split.at
        split = Arena(start, free)
        kvq = split("kvq", [P, KD, NT])[0:NB].rearrange("p a b -> p (a b)")[:, 0:SEQW]
        x_out = split("x_out", [P, KD, NT])

        early = top - 5824
        a = Arena(free, early)
        x_tok = a("x_tok", [P, 4, D])
        xs_tok = a("xs_tok", [NB, D])
        mem_in = a("mem_in", [P, 2, D])
        memT = a("memT", [P, KD, NMEM])
        lrow = a("lrow", [P, P])
        dtrow = a("dtrow", [PAIRS, 2])

        a = Arena(y_at, y_at + 4 * KD * NT)
        rows = a("rows", [100, P])
        crow = a("crow", [88, 4, P])
        srow = a("srow", [P, 2, 6, P])

        e = Arena(early, top)
        lam = e("lam", [P, P])
        hrow = e("hrow", [96, 2, 2, P])
        s5s = e("s5s", [P, 16, PAIRS])
        pw_r = e("pw_r", [P, PAIRS, CHUNK + 1])
        pw_i = e("pw_i", [P, PAIRS, CHUNK + 1])
        a = Arena(free, early)
        b_in = a("b_in", [P, 2, TP, CH])
        c_in = a("c_in", [P, 2, 2, 2, STATE])
        cT = a("cT", [P, 2, TP, CH])
        bb = [a("bb0", [P, 2, TP, CH])]
        bp = a("bp", [P, 2, TP, CHUNK * CH])
        cp = [a("cp0", [P, 2, TP, (CHUNK + 1) * CH])]
        e_r = a("e_r", [P, PAIRS, NCH])
        e_i = a("e_i", [P, PAIRS, NCH])
        e_tmp = a("e_tmp", [P, PAIRS * NCH // 2])
        decay = a("decay", [P, PAIRS, NCH])
        tmp = [a(f"tmp{n}", [P, TP * (CHUNK + 1) * CH]) for n in range(3)]
        hfin = a("hfin", [P, 2, 1 + NB, PAIRS])
        hout = a("hout", [108, 2, 2, P])
        a = Arena(start, free)
        toep = a("toep", [P, TG, P])
        u = [a("u0", [P, TG, NCH + 2 * NB])]
        v = a("v", [P, 2, TP, NCH + NB])
        hp = [a("hp0", [P, 2, TP, NB + 1 + NCH])]
        yb = a("yb", [P, TG, NB + NCH])
        yz = a("yz", [P, 2, NT])
        h0 = a("h0", [P, 2, NB, PAIRS])
        a = Arena(stats_at, stats_end)
        u.append(a("u1", [P, TG, NCH + 2 * NB]))
        hp.append(a("hp1", [P, 2, TP, NB + 1 + NCH]))
        a = Arena(weights_at, weights_end)
        bb.append(a("bb1", [P, 2, TP, CH]))
        cp.append(a("cp1", [P, 2, TP, (CHUNK + 1) * CH]))
        kern = a("kern", [CH, TG, P])
        bT = a("bT", [P, TP, 2, P])
        cp_tmp = a("cp_tmp", [P, TP * (CHUNK + 1) * CH])
        a = Arena(free, top)
        gate = a("gate", [P, KS, NT])

        def mem_buffers(a, l):
            return dict(
                p=a(f"mp{l}", [P, 2, 2, NMEM]), pT=a(f"mpT{l}", [P, 2, T]), st=a(f"mst{l}", [P, 2, 8]),
                k=a(f"mk{l}", [P, 2, 2, NMEM]), v=a(f"mv{l}", [P, NB, 2, NMEM]), prod=a(f"mprod{l}", [P, 2, NMEM]),
                s=a(f"ms{l}", [P, NB, 2, MEMH]), dst=a(f"mdst{l}", [P, 8, NB * MEMH]))

        mb = [mem_buffers(a, 0)]

        a = Arena(free, top)
        h_hi = a("h_hi", [P, KH, NT], F32R)
        h_lo = a("h_lo", [P, KH, NT], F32R)
        uc = [a(f"uc{s}", [P, 2 + NT]) for s in range(2)]
        yc = [a(f"yc{s}", [P, NT]) for s in range(2)]
        hf = a("hf", [P, NT])
        sg = a("sg", [P, NT])
        crows = yc
        a = Arena(free, top)
        ytok = [a(f"ytok{c}", [P, D]) for c in range(5)]

        a = Arena(free, top)
        qh = a("qh", [P, HEADS, T])
        kh = a("kh", [P, HEADS, T])
        after_heads = a.at
        vtok = y[:, 0:6, :].rearrange("p a b -> p (a b)").rearrange("p (c h d) -> p c h d", c=4, h=HEADS)
        kvs = a("kvs", [NB, 2, SEQW])
        lfs = a("lfs", [NB, HEADS])
        keep = a.at
        kvT = a("kvT", [P, NT])
        ktok = [a(f"ktok{s}", [P, 4, P]) for s in range(2)]
        lf = a("lf", [HEADS, 3, NT])
        lft = a("lft", [P, 4, HEADS])
        a = Arena(keep, top)
        PT = [a(f"PT{s}", [P, 1280]) for s in range(2)]
        nmax = [a(f"nmax{s}", [P, 4]) for s in range(2)]
        rinv = a("rinv", [1, T])
        lmask = a("lmask", [NB, NB, HEADS])
        mba = Arena(free, after_heads)
        mb.append(mem_buffers(mba, 1))
        a = Arena(weights_at, weights_end)
        page = [a(f"page{n}", [P, SEQW]) for n in range(PAGES)]
        qb = [a(f"qb{n}", [P, SEQW]) for n in range(2)]
        logf = a("logf", [P, NB, PAGES, HEADS])
        a = Arena(stats_at, stats_end)
        sc = a("sc", [P, NB, PAGES + 1, HEADS])
        pre = a("pre", [P, NB, PAGES, HEADS])
        fst = a("fst", [P, 8, NB * HEADS])
        causal_t = a("causal_t", [P, P])
        block_diag, vm = qb[1], qb[0]

        z_dram = nc.dram_tensor("z_scratch", [SEQW, NT], F32, kind="Internal").ap()
        y_dram = nc.dram_tensor("y_scratch", [SEQW, NT], F32, kind="Internal").ap()

        assert nc.sbuf_base == nc_base

        big = [ctx.enter_context(nc.psum_tensor(f"big{n}", [P, 512], F32)) for n in range(4)]
        misc = [ctx.enter_context(nc.psum_tensor(f"misc{n}", [P, 512], F32)) for n in range(4)]

        def sem(name):
            return ctx.enter_context(nc.semaphore(name))

        raw_loaded = [sem(f"raw_loaded{s}") for s in range(2)]
        hi_made, lo_made = sem("hi_made"), sem("lo_made")
        panel_done, panel_read = sem("panel_done"), sem("panel_read")
        misc_full = [sem(f"misc_full{n}") for n in range(4)]
        misc_free = [sem(f"misc_free{n}") for n in range(4)]
        act_step, dve_step, pool_step = sem("act_step"), sem("dve_step"), sem("pool_step")
        S = {}

        def s_(name):
            if name not in S:
                S[name] = sem(name)
            return S[name]

        fox = big + misc
        fox_full = [sem(f"fox_full{n}") for n in range(8)]
        fox_free = [sem(f"fox_free{n}") for n in range(8)]

        def place(job):
            if job in J:
                j = J[job]
                return misc[j % 4], misc_full[j % 4], misc_free[j % 4], j // 4
            j = FJ[job]
            return fox[j % 8], fox_full[j % 8], fox_free[j % 8], j // 8

        def bank(job):
            return place(job)[0]

        def full(eng, job):
            _, made, _, before = place(job)
            eng.wait_ge(made, before + 1)

        def freed(own, ins, job):
            _, _, free_, before = place(job)
            own.tell(ins, free_, before + 1)

        OFF = dict(mix_pre=0, mix_post=16, ffn_pre=32, ffn_post=48, mem=64, kv=80, dskip=88, bglu=94)

        def gain(name, k, l=0):
            c = OFF[name] + (l * KD if name not in ("kv", "dskip", "bglu") else 0) + k
            return gains[:, c:c + 1]

        block = ctx.enter_context(nc.Block())

        @block.sync
        def _(sp):
            stores = [0]

            def load(dst, src, sm, **kw):
                sp.dma_start(dst, src, **kw).then_inc(s_(sm), 16)

            def store(dst, src, **kw):
                sp.dma_start(dst, src, **kw).then_inc(s_("stored"), 16)
                stores[0] += 1

            def weights(name, src, after=None, start=0, stop=None):
                kb, n, base, _ = PH[name]

                def one(i, q, half):
                    slot = (base + half) % 2
                    if not isinstance(q, int) or q >= 2:
                        sp.wait_ge(lo_made, q - 1)
                    view = src(i)
                    sp.dma_start(raw[slot][:, 0:kb, 0:view.shape[2]], view).then_inc(raw_loaded[slot], 16)

                if n <= 2 or start or stop or after is not None:
                    for i in range(start, stop or n):
                        one(i, base + i, i % 2)
                        if after is not None:
                            after(i)
                else:
                    with sp.Fori(0, n // 2) as it:
                        for half in range(2):
                            one(it * 2 + half, it * 2 + (base + half), half)

            def cols(w, rows=None):
                w = w if rows is None else w[rows[0]:rows[1], :]
                v3 = w.rearrange("(k p) n -> p k n", p=P)
                return lambda i: v3[:, :, bass.ds(i * P, P)]

            for n, nm in enumerate(("norm_mix_pre", "norm_mix_post", "norm_ffn_pre", "norm_ffn_post", "mem_norm")):
                load(rows[16 * n:16 * n + 16, :], I[nm].rearrange("l (k p) -> (l k) p", p=P), "rows_in")
            load(rows[80:88, :], I["kv_norm"].rearrange("(k p) -> k p", p=P), "rows_in")
            load(rows[88:94, :], I["d_skip"].rearrange("l (k p) -> (l k) p", p=P), "rows_in")
            load(rows[94:100, :], I["b_glu"].rearrange("l (k p) -> (l k) p", p=P), "rows_in")
            load(mem_in[:], I["mem_prompt"].rearrange("b (c p) d -> p (b c) d", p=P), "mem_in")
            weights("memkv0", cols(I["w_mem_kv"][0]), stop=2)
            load(x_tok[:], I["x_prompt"].rearrange("b (c p) d -> p (b c) d", p=P), "x_in")
            load(xs_tok[:], I["x_sample"].rearrange("b t d -> (b t) d"), "x_in")
            for l in range(2):
                taps = I["conv_w"][l].rearrange("t (f p) -> (t f) p", p=P)
                load(crow[:, 2 * l, :], taps[0:88, :], "conv_in")
                load(crow[0:44, 2 * l + 1, :], taps[88:132, :], "conv_in")
                load(crow[44:88, 2 * l + 1, :], I["conv_b"][l].rearrange("(f p) -> f p", p=P), "conv_in")
                st = I["state_ffn_conv"][l].rearrange("b t (f p) -> (b t f) p", p=P)
                load(srow[:, l, 0:5, :], st[0:640, :].rearrange("(r q) p -> q r p", q=P), "conv_in")
                load(srow[0:64, l, 5, :], st[640:704, :], "conv_in")
            sp.wait_ge(s_("lrow_zero"), 1)
            load(lrow[0:24, :], I["lam_re"][0].rearrange("(j g) p -> j (g p)", g=2), "lam_in")
            load(lrow[32:56, :], I["lam_im"][0].rearrange("(j g) p -> j (g p)", g=2), "lam_in")
            load(dtrow[:], I["log_dt"][0].rearrange("(j g) -> j g", g=2), "lam_in")
            load(pages[:], I["page_table"].rearrange("(a b) p -> a (b p)", a=1), "pages_in")
            load(bf[:], I["b_f"].rearrange("(h a) -> h a", a=1), "bf_in")
            for ri, nm in enumerate(("state_ssm_re", "state_ssm_im")):
                st = I[nm][0].rearrange("b (j g) p -> (b j) (g p)", g=2)
                for half in range(2):
                    load(hrow[:, ri, half, :], st[96 * half:96 * half + 96, :], "h0_in")

            weights("memkv0", cols(I["w_mem_kv"][0]), start=2)
            weights("memkv1", cols(I["w_mem_kv"][1]))
            def bc_load(t):
                g = slice(t * TG, t * TG + TG)
                for ri, nm in enumerate(("b_re", "b_im")):
                    load(b_in[:, ri], I[nm][0, g].rearrange("(j g) p c -> (g p) j c", g=2), "bc_in")
                for ri, nm in enumerate(("c_re", "c_im")):
                    for dup in range(2):
                        load(c_in[:, ri, :, dup, :], I[nm][0, g].rearrange("(t g) c p -> (g c) t p", g=8), "bc_in")

            sp.wait_ge(s_("x_ready"), 1)
            bc_load(0)
            weights("win0", cols(I["w_in"][0]))
            for l in range(2):
                sp.wait_ge(s_("memtok_ready"), 4 * (l + 1))
                for nm, c in (("prompt_mem_k", 0), ("prompt_mem_v", 256)):
                    store(O[nm][l, 0].rearrange("(c p) h d -> p c (h d)", p=P), mem_tok[:, l, :, c:c + 256])

            zs3 = z_dram.rearrange("(g c) n -> c g n", c=CH)
            ys3 = y_dram.rearrange("(g c) n -> c g n", c=CH)
            sp.wait_ge(s_("z_ready"), KS)
            for m in range(KS):
                sp.dma_start(z_dram[m * P:(m + 1) * P, :], y[:, m, :]).then_inc(s_("z_out"), 16)
            def u_load(t):
                g = slice(t * TG, t * TG + TG)
                for tau in range(CHUNK):
                    j = CHUNK - 1 - tau
                    load(u[t % 2][CH * tau:CH * tau + CH, :, NB:NB + NCH], zs3[:, g, j * NCH:(j + 1) * NCH], "u_in")
                load(u[t % 2][P - CH:P, :, 0:NB], zs3[:, g, T:NT], "u_in")
                load(u[t % 2][0:CH, :, NB + NCH:], zs3[:, g, T:NT], "u_in")

            sp.wait_ge(s_("z_out"), 16 * KS)
            sp.wait_ge(s_("s5_zero"), 1)
            u_load(0)
            sp.wait_ge(s_("u1_zero"), 1)
            u_load(1)

            def y_shuffle(t):
                g = slice(t * TG, t * TG + TG)
                sp.wait_ge(s_("yb_ready"), 4 * (t + 1))
                for i in range(CHUNK):
                    sp.dma_start(ys3[:, g, i * NCH:(i + 1) * NCH],
                                 yb[CH * i:CH * i + CH, :, NB:]).then_inc(s_("y_out"), 16)
                sp.dma_start(ys3[:, g, T:NT], yb[0:CH, :, 0:NB]).then_inc(s_("y_out"), 16)
                sp.wait_ge(s_("y_out"), 16 * 9 * (t + 1))
                if t:
                    sp.wait_ge(s_("yz_used"), t)
                load(yz[:], y_dram[t * TG * CH:(t + 1) * TG * CH, :].rearrange("(m p) n -> p m n", p=P), "yz_in")

            for t in range(THIRDS):
                if t + 1 < THIRDS:
                    sp.wait_ge(s_("s5_built"), t + 1)
                    bc_load(t + 1)
                if t:
                    full(sp, ("Y", t - 1, 3))
                    if t + 1 < THIRDS:
                        u_load(t + 1)
                    y_shuffle(t - 1)
                sp.wait_ge(s_("s5_zero"), 2)
                sp.wait_ge(s_("kern_ready"), 4 * (t + 1))
                for tau in range(CHUNK):
                    load(toep[CH * tau:CH * tau + CH, :, (CHUNK - 1 - tau) * CH:P],
                         kern[:, :, 0:(tau + 1) * CH], "toep_in")
            y_shuffle(THIRDS - 1)
            sp.wait_ge(s_("hout_ready"), 2)
            for ri, (pn, sn) in enumerate((("prompt_ssm_re", "sample_ssm_re"), ("prompt_ssm_im", "sample_ssm_im"))):
                store(O[pn][0, 0].rearrange("(j g) p -> j (g p)", g=2), hout[0:24, ri, 0, :])
                so = O[sn][0].rearrange("b (j g) p -> (b j) (g p)", g=2)
                store(so[0:84, :], hout[24:108, ri, 0, :])
                store(so[84:192, :], hout[:, ri, 1, :])
            def mem_v(l, m):
                load(m["v"][:].rearrange("p b c n -> p (b c) n"),
                     I["cache_mem_v"][l].rearrange("b (c p) h d -> p (b c) (h d)", p=P), "mv_in")

            def mem_k(l, m, b):
                if b >= 2:
                    sp.wait_ge(s_("mk_used"), NB * l + b - 1)
                load(m["k"][:, b % 2], I["cache_mem_k"][l, b].rearrange("(c p) h d -> p c (h d)", p=P),
                     f"mk_in{b % 2}")

            mem_v(0, mb[0])
            mem_k(0, mb[0], 0)
            mem_k(0, mb[0], 1)
            weights("glu", cols(I["w_glu"][0]))
            weights("wout0", cols(I["w_out"][0]), stop=2)
            for b in range(2, NB):
                mem_k(0, mb[0], b)
            weights("wout0", cols(I["w_out"][0]), start=2)

            def conv_out(l, m):
                for a_ in conv_rows(m) if m >= 0 else ():
                    sp.wait_ge(s_("crows_ready"), 11 * l + a_ + 1)
                    c = slice(4 * P * a_, 4 * P * (a_ + 1))
                    for dst, r in ((O["prompt_ffn_conv"][l, 0][:, c], slice(0, 2)),
                                   (O["sample_ffn_conv"][l, :, 1, c], slice(2, 2 + NB))):
                        sp.dma_start(dst, crows[a_ % 2][r, 0:4 * P]).then_inc(s_(f"crows_out{a_ % 2}"), 16)

            def ffn_weights(l):
                for f in range(2):
                    wu = I["w_up"][l].rearrange("(k p) n -> p k n", p=P)

                    def up(i, wu=wu, f=f):
                        it, half = i
                        return wu[:, :, bass.ds(it * P + (f * KH + half * KF) * P, P)]

                    kb, n, base, _ = PH[f"up{l}{f}"]
                    with sp.Fori(0, KH) as it:
                        for half in range(2):
                            slot = (base + half) % 2
                            sp.wait_ge(lo_made, it * 2 + (base + half - 1))
                            sp.dma_start(raw[slot][:, 0:KD, :], up((it, half))).then_inc(raw_loaded[slot], 16)
                    weights(f"down{l}{f}", cols(I["w_down"][l], (f * KH * P, (f + 1) * KH * P)),
                            (lambda i: conv_out(l, i - 4)) if f else None)
                for m in range(4, 8):
                    conv_out(l, m)
                store(O["sample_ffn_conv"][l, :, 0, :], I["state_ffn_conv"][l, :, 1, :])

            ffn_weights(0)

            def store_k(i):
                m = i - 4
                if 0 <= m < 6:
                    sp.wait_ge(s_("ktok_ready"), m + 1)
                    sp.dma_start(O["prompt_k"][0].rearrange("(c p) h d -> p c (h d)", p=P)[:, :, m * P:(m + 1) * P],
                                 ktok[m % 2][:]).then_inc(s_(f"ktok_out{m % 2}"), 16)

            weights("kv", cols(I["w_kv"]), store_k)
            wf = I["w_kv"].rearrange("(k p) n -> p k n", p=P)
            weights("kvf", lambda i: wf[:, :, 2 * SEQW:2 * SEQW + HEADS])
            weights("win1", cols(I["w_in"][1]))
            sp.wait_ge(s_("vtok_ready"), 6)
            for c in range(4):
                store(O["prompt_v"][0, c * P:(c + 1) * P], vtok[:, c, :, 0:DH])
            sp.wait_ge(s_("kvs_ready"), 12)
            store(O["sample_k"].rearrange("b t h d -> (b t) (h d)"), kvs[:, 0, :])
            store(O["sample_v"].rearrange("b t h d -> (b t) (h d)"), kvs[:, 1, :])
            sp.wait_ge(s_("logf_ready"), 2)
            store(O["prompt_logf"][0].rearrange("(c p) h -> p c h", p=P), lft[:, 0:4, :])
            store(O["sample_logf"].rearrange("b t h -> (b t) h"), lfs[:])
            sp.wait_ge(s_("c_ready"), 3)
            load(qh[DH:DH + 1, :, :], lf[:, 2, 0:T], "aug_in")
            load(kh[DH + 1:DH + 2, :, :], lf[:, 0, 0:T], "aug_in")
            sp.wait_ge(panel_done, PH["win1"][2] + 8)
            sp.wait_ge(s_("pages_in"), 16)

            def page_id(n):
                return sp.value_load(pages[0:1, bass.ds(n, 1)], min_val=0, max_val=I["cache_k"].shape[0] - 1)

            def page_loads(cache, b, used=None, count=0):
                for pg in range(PAGES):
                    if used is not None:
                        sp.wait_ge(used, count + pg + 1)
                    load(page[pg][:], cache[bass.ds(page_id(b * PAGES + pg), 1)].rearrange("a t h d -> (a t) (h d)"),
                         f"page_in{pg}")

            page_loads(I["cache_k"], 0)
            for pg in range(PAGES):
                load(logf[:, NB - 1, pg, :], I["cache_logf"][bass.ds(page_id((NB - 1) * PAGES + pg), 1)].rearrange(
                    "a t h -> (a t) h"), "logf_in")
            with sp.Fori(0, NB - 1) as b:
                for pg in range(PAGES):
                    load(logf[:, bass.ds(b, 1), pg, :].rearrange("p a h -> p (a h)"),
                         I["cache_logf"][bass.ds(page_id(b * PAGES + pg), 1)].rearrange("a t h -> (a t) h"), "logf_in")
                page_loads(I["cache_k"], b + 1, s_("k_used"), b * PAGES)
            page_loads(I["cache_v"], 0, s_("k_used"), (NB - 1) * PAGES)
            sp.wait_ge(s_("heads_done"), 1)
            mem_v(1, mb[1])
            mem_k(1, mb[1], 0)
            mem_k(1, mb[1], 1)
            with sp.Fori(0, NB // 2 - 1) as i:
                for half in range(2):
                    page_loads(I["cache_v"], i * 2 + (half + 1), s_("v_used"), i * (2 * PAGES) + half * PAGES)
                    sp.wait_ge(s_("mk_used"), i * 2 + (NB + half + 1))
                    load(mb[1]["k"][:, half], I["cache_mem_k"][1, bass.ds(i * 2 + (half + 2), 1)].rearrange(
                        "b (c p) h d -> p (b c) (h d)", p=P), f"mk_in{half}")
            page_loads(I["cache_v"], NB - 1, s_("v_used"), (NB - 2) * PAGES)
            sp.wait_ge(s_("fox_done"), 1)
            weights("wout1", cols(I["w_out"][1]))
            ffn_weights(1)
            for a_ in range(2):
                for c in range(5):
                    sp.wait_ge(s_("ytok_ready"), 5 * a_ + c + 1)
                    dst = O["y_prompt"][0, c * P:(c + 1) * P, :] if c < 4 else O["y_sample"].rearrange("b t d -> (b t) d")
                    store(dst[:, 512 * a_:512 * a_ + 512], ytok[c][0:(P if c < 4 else NB), 512 * a_:512 * a_ + 512])
            sp.wait_ge(s_("stored"), 16 * stores[0])
            for s in range(2):
                sp.wait_ge(s_(f"ktok_out{s}"), 16 * 3)
                sp.wait_ge(s_(f"crows_out{s}"), 16 * 2 * (12 - 2 * s))

        @block.gpsimd
        def _(pool):
            own = Own(pool, pool_step)
            own.do(pool.memset(ident[:], 0.0))
            own.do(pool.memset(ones[:], 1.0))
            own.do(pool.memset(meanw[:], 1.0 / D))
            own.do(pool.memset(tri[:], 1.0))
            own.do(pool.memset(causal[:], 0.0))
            own.do(pool.memset(sel[:], 0.0))
            own.tell(pool.memset(lrow[:], 0.0), s_("lrow_zero"), 1)
            own.sync()
            own.do(pool.affine_select(out=ident[:], in_=ident[:], compare_op=ALU.not_equal, fill=1.0, base=0,
                                      pattern=[[-1, P]], channel_multiplier=1))
            own.do(pool.affine_select(out=tri[:], in_=tri[:], compare_op=ALU.is_ge, fill=0.0, base=0,
                                      pattern=[[1, P]], channel_multiplier=-1))
            own.do(pool.affine_select(out=causal[:], in_=causal[:], compare_op=ALU.is_ge, fill=NEG / SCALE, base=0,
                                      pattern=[[-1, P]], channel_multiplier=1))
            own.tell(pool.affine_select(out=sel[:], in_=sel[:], compare_op=ALU.not_equal, fill=1.0, base=0,
                                        pattern=[[-1, NB], [0, P]], channel_multiplier=1), s_("consts"), 1)

            def lo(q, slot, kb):
                pool.wait_ge(hi_made, q + 1)
                pool.tensor_tensor(w_lo[slot][:, 0:kb, :], raw[slot][:, 0:kb, :],
                                   w_hi[slot][:, 0:kb, :].bitcast(F32), ALU.subtract).then_inc(lo_made, 1)

            def ptt(o, a_, b_, op):
                own.do(pool.tensor_tensor(o, a_, b_, op))
                own.sync()

            def phase_table(lo_of):
                w_r, w_i, s0, s1 = (s5s[:, n, :] for n in (1, 2, 12, 13))

                def doubling(m, js=slice(0, PAIRS)):
                    n = js.stop - js.start
                    tv = e_tmp[:, 0:n * m].rearrange("p (j m) -> p j m", m=m)
                    b_r, b_i = (w[:, js].unsqueeze(2).to_broadcast([P, n, m]) for w in (w_r, w_i))
                    f_r, f_i, o_r, o_i = e_r[:, js, 0:m], e_i[:, js, 0:m], e_r[:, js, m:2 * m], e_i[:, js, m:2 * m]
                    ptt(o_r, b_r, f_r, ALU.mult)
                    ptt(tv, b_i, f_i, ALU.mult)
                    ptt(o_r, o_r, tv, ALU.subtract)
                    ptt(o_i, b_r, f_i, ALU.mult)
                    ptt(tv, b_i, f_r, ALU.mult)
                    ptt(o_i, o_i, tv, ALU.add)

                def square():
                    ptt(s0, w_r, w_r, ALU.mult)
                    ptt(s1, w_i, w_i, ALU.mult)
                    ptt(w_i, w_r, w_i, ALU.mult)
                    ptt(w_i, w_i, w_i, ALU.add)
                    ptt(w_r, s0, s1, ALU.subtract)

                lo_of(0)
                lo_of(1)
                lo_of(2)
                pool.wait_ge(s_("s5_params"), 1)
                own.do(pool.memset(decay[:, :, 0:1], 0.0))
                own.do(pool.memset(e_r[:, :, 0:1], 1.0))
                own.do(pool.memset(e_i[:, :, 0:1], 0.0))
                own.do(pool.tensor_copy(w_r, s5s[:, 14, :]))
                own.do(pool.tensor_copy(w_i, s5s[:, 15, :]))
                own.sync()
                doubling(1)
                square()
                doubling(2)
                lo_of(3)
                square()
                doubling(4)
                square()
                doubling(8)
                lo_of(4)
                square()
                doubling(16)
                square()
                for t in range(THIRDS):
                    lo_of(5 + t)
                    doubling(32, slice(t * TP, t * TP + TP))
                    own.eng.sem_inc(s_("table_ready"), 1)

            def s5_beside():
                pool.wait_ge(s_("z_ready"), 8)
                own.tell(pool.memset(u[1][:], 0.0), s_("u1_zero"), 1)

                def add_z(t):
                    pool.wait_ge(s_("z_scaled"), 1)
                    pool.wait_ge(s_("yz_in"), 16 * (t + 1))
                    own.do(pool.tensor_tensor(y[:, 2 * t:2 * t + 2, :], y[:, 2 * t:2 * t + 2, :], yz[:], ALU.add))
                    own.mark(s_("yz_used"))

                for t in range(THIRDS):
                    if t:
                        add_z(t - 1)
                    if t + 1 < THIRDS:
                        pool.wait_ge(s_("s5_built"), t + 2)
                        if t >= 1:
                            full(pool, ("Y", t - 1, 3))
                        js, n = slice((t + 1) * TP, (t + 2) * TP), CHUNK + 1
                        o = cp[(t + 1) % 2][:, 0].rearrange("p j (n c) -> p j n c", c=CH)
                        tv = cp_tmp[:].rearrange("p (j n c) -> p j n c", n=n, c=CH)
                        a_r, a_i = (w[:, js, 0:n].unsqueeze(3).to_broadcast([P, TP, n, CH]) for w in (pw_r, pw_i))
                        c_r, c_i = (cT[:, ri].unsqueeze(2).to_broadcast([P, TP, n, CH]) for ri in range(2))
                        ptt(o, a_r, c_r, ALU.mult)
                        ptt(tv, a_i, c_i, ALU.mult)
                        ptt(o, o, tv, ALU.subtract)
                        pool.sem_inc(s_("cp_re_ready"), 1)
                add_z(THIRDS - 1)

            def residual(n):
                for k in range(KD):
                    pool.wait_ge(s_("y_scaled"), KD * n + k + 1)
                    own.tell(pool.tensor_tensor(x[:, k, :], x[:, k, :], y[:, k, :], ALU.add),
                             s_("x_updated"), KD * n + k + 1)

            def k_pass():
                pool.wait_ge(s_("q1_ready"), 1)
                own.do(pool.memset(causal_t[:], 0.0))
                own.sync()
                own.tell(pool.affine_select(out=causal_t[:], in_=causal_t[:], compare_op=ALU.is_ge, fill=NEG / SCALE,
                                            base=0, pattern=[[1, P]], channel_multiplier=-1), s_("causal_t_ready"), 1)
                for n in range(NB * PAGES):
                    b, pg = n // PAGES, n % PAGES
                    if pg == 0:
                        pool.wait_ge(s_("qb_ready"), b + 1)
                    pool.wait_ge(s_(f"page_in{pg}"), 16 * (b + 1))
                    own.tell(pool.tensor_tensor(page[pg][:], page[pg][:], qb[b % 2][:], ALU.mult),
                             s_("k_product"), n + 1)
                own.sync()
                mask = block_diag[0:HEADS, :].rearrange("p (h d) -> p h d", d=DH)
                own.do(pool.memset(mask, 0.0))
                own.sync()
                own.tell(pool.affine_select(out=mask, in_=mask, compare_op=ALU.not_equal, fill=1.0, base=0,
                                            pattern=[[-1, HEADS], [0, DH]], channel_multiplier=1), s_("block_diag"), 1)

            for name, (kb, n, base, _) in PH.items():
                if name == "wout1":
                    k_pass()
                if name == "win0":
                    phase_table(lambda i: lo(base + i, (base + i) % 2, kb))
                    s5_beside()
                    continue
                first = 2 if name in ("up00", "kv", "up10") or n <= 2 else 0
                for i in range(min(first, n)):
                    lo(base + i, (base + i) % 2, kb)
                if name in ("up00", "kv", "up10"):
                    residual(("up00", "kv", "up10").index(name))
                if n > first:
                    with pool.Fori(0, (n - first) // 2) as it:
                        for half in range(2):
                            lo(it * 2 + (base + first + half), (base + half) % 2, kb)
            residual(3)


        @block.vector
        def _(dve):
            own = Own(dve, dve_step)
            do, tell, sync, mark = own.do, own.tell, own.sync, own.mark
            V = dve
            stat = [0, 0]

            def evac(job, dst, src):
                full(dve, job)
                freed(own, V.tensor_copy(dst, src), job)

            def sum_step(m, src, made, used):
                stat[0] += 1
                dve.wait_ge(s_(made), stat[0])
                if m == 0:
                    ins = V.tensor_copy(sumsq[:], src)
                else:
                    dve.wait_ge(s_(used), stat[0] - 1)
                    ins = V.tensor_tensor(sumsq[:], sumsq[:], src, ALU.add)
                tell(ins, s_(used), stat[0])

            def sum_squares(count, cols):
                for k in range(count):
                    dve.wait_ge(s_("sq_made"), stat[0] + 1)
                    if k == 0:
                        ins = V.tensor_copy(sumsq[:, 0:cols], sq[:, stat[0] % 2, 0:cols])
                    else:
                        sync()
                        ins = V.tensor_tensor(sumsq[:, 0:cols], sumsq[:, 0:cols], sq[:, stat[0] % 2, 0:cols], ALU.add)
                    stat[0] += 1
                    tell(ins, s_("sq_used"), stat[0])

            nstd = [0]

            def reciprocal_std(dst, cols):
                nstd[0] += 1
                dve.wait_ge(s_("root_made"), nstd[0])
                tell(V.reciprocal(dst[:, 0:cols], sd[:, 0:cols]), s_("rstd_ready"), nstd[0])
                sync()

            def split_lo(k, src, g, cols=slice(0, NT)):
                stat[1] += 1
                dve.wait_ge(s_("xhi_made"), stat[1])
                h = x_hi[:, k, cols].bitcast(F32)
                if g is None:
                    ins = V.tensor_tensor(x_lo[:, k, cols], src, h, ALU.subtract)
                else:
                    ins = V.scalar_tensor_tensor(x_lo[:, k, cols], src, g, h, ALU.mult, ALU.subtract)
                tell(ins, s_("xlo_made"), stat[1])

            lr_, li_, dt_ = lam[:, 0:PAIRS], lam[:, 32:32 + PAIRS], lam[:, 64:64 + PAIRS]

            def sl(n):
                return s5s[:, n, :]

            def tt(o, a_, b_, op):
                do(V.tensor_tensor(o, a_, b_, op))
                sync()

            def ts(o, a_, c0, c1, o0, o1):
                do(V.tensor_scalar(o, a_, c0, c1, o0, o1))
                sync()

            LR, X1, TH, MAG, SN, CS, R8, FR, FI, T0, T1, T2, R1, R2, UR, UI = range(16)

            def cmul(o_r, o_i, a_r, a_i, b_r, b_i, t0, conj=False, neg_i=False):
                tt(o_r, a_r, b_r, ALU.mult)
                tt(t0, a_i, b_i, ALU.mult)
                tt(o_r, o_r, t0, ALU.add if conj else ALU.subtract)
                tt(o_i, a_r, b_i, ALU.mult)
                tt(t0, a_i, b_r, ALU.mult)
                if neg_i:
                    do(V.scalar_tensor_tensor(o_i, o_i, -1.0, t0, ALU.mult, ALU.subtract))
                    sync()
                else:
                    tt(o_i, o_i, t0, ALU.subtract if conj else ALU.add)

            def square(w_r, w_i, t0, t1):
                tt(t0, w_r, w_r, ALU.mult)
                tt(t1, w_i, w_i, ALU.mult)
                tt(w_i, w_r, w_i, ALU.mult)
                ts(w_i, w_i, 2.0, None, ALU.mult, ALU.bypass)
                tt(w_r, t0, t1, ALU.subtract)

            def s5_angles():
                sync()
                ts(sl(LR), lr_, -1e-4, None, ALU.min, ALU.bypass)
                dve.wait_ge(s_("s5_act"), 1)
                tt(sl(X1), sl(LR), dt_, ALU.mult)
                tt(sl(TH), li_, dt_, ALU.mult)
                for dst, shift in ((R1, 0.0), (R2, math.pi / 2)):
                    ts(sl(T0), sl(TH), 1.0 / TWO_PI, shift / TWO_PI, ALU.mult, ALU.add)
                    ts(sl(T0), sl(T0), ROUND, -ROUND, ALU.add, ALU.add)
                    c1 = 6.28125
                    c2 = float(np.float32(TWO_PI - c1))
                    c3 = TWO_PI - c1 - c2
                    ts(sl(T1), sl(T0), -c1, None, ALU.mult, ALU.bypass)
                    tt(sl(dst), sl(TH), sl(T1), ALU.add)
                    ts(sl(T1), sl(T0), -c2, None, ALU.mult, ALU.bypass)
                    tt(sl(dst), sl(dst), sl(T1), ALU.add)
                    ts(sl(T1), sl(T0), -c3, None, ALU.mult, ALU.bypass)
                    tt(sl(dst), sl(dst), sl(T1), ALU.add)
                    if shift:
                        ts(sl(dst), sl(dst), shift, None, ALU.add, ALU.bypass)
                    ts(sl(dst), sl(dst), PI_LO, -PI_LO, ALU.min, ALU.max)
                tell(V.tensor_copy(sl(T2), sl(R1)), s_("angles_ready"), 1)
                sync()

            def s5_unit():
                dve.wait_ge(s_("s5_act"), 5)
                do(V.tensor_copy(sl(UR), sl(CS)))
                do(V.tensor_copy(sl(UI), sl(SN)))
                sync()

                for _ in range(3):
                    square(sl(UR), sl(UI), sl(T0), sl(T1))
                mark(s_("s5_params"))

            def s5_factor():
                AR, AI = pw_r[:, :, 1], pw_i[:, :, 1]
                tt(AR, sl(MAG), sl(CS), ALU.mult)
                tt(AI, sl(MAG), sl(SN), ALU.mult)
                tt(sl(T0), sl(LR), sl(LR), ALU.mult)
                tt(sl(T1), li_, li_, ALU.mult)
                tt(sl(T0), sl(T0), sl(T1), ALU.add)
                do(V.reciprocal(sl(T0), sl(T0)))
                sync()
                ts(sl(T2), AR, -1.0, None, ALU.add, ALU.bypass)
                tt(sl(FR), sl(T2), sl(LR), ALU.mult)
                tt(sl(T1), AI, li_, ALU.mult)
                tt(sl(FR), sl(FR), sl(T1), ALU.add)
                tt(sl(FR), sl(FR), sl(T0), ALU.mult)
                tt(sl(FI), AI, sl(LR), ALU.mult)
                tt(sl(T1), sl(T2), li_, ALU.mult)
                tt(sl(FI), sl(FI), sl(T1), ALU.subtract)
                tt(sl(FI), sl(FI), sl(T0), ALU.mult)

            def s5_powers():
                do(V.memset(pw_r[:, :, 0:1], 1.0))
                do(V.memset(pw_i[:, :, 0:1], 0.0))
                sync()
                for m in (1, 2, 4):
                    w_r = pw_r[:, :, m:m + 1].to_broadcast([P, PAIRS, m])
                    w_i = pw_i[:, :, m:m + 1].to_broadcast([P, PAIRS, m])
                    tv = tmp[0][:, 0:PAIRS * m].rearrange("p (j m) -> p j m", m=m)
                    cmul(pw_r[:, :, m + 1:2 * m + 1], pw_i[:, :, m + 1:2 * m + 1], w_r, w_i,
                         pw_r[:, :, 1:m + 1], pw_i[:, :, 1:m + 1], tv)

            def s5_b(t):
                js = slice(t * TP, t * TP + TP)
                dve.wait_ge(s_("bc_in"), 16 * 6 * (t + 1))
                tv = tmp[0][:, 0:TP * CH].rearrange("p (j c) -> p j c", c=CH)
                f_r = s5s[:, FR, js].unsqueeze(2).to_broadcast([P, TP, CH])
                f_i = s5s[:, FI, js].unsqueeze(2).to_broadcast([P, TP, CH])
                cmul(bb[t % 2][:, 0], bb[t % 2][:, 1], f_r, f_i, b_in[:, 0], b_in[:, 1], tv)

            def s5_c(t):
                full(dve, ("cT", t))
                for ri in range(2):
                    srcc = bank(("cT", t))[:, 256 * ri:256 * ri + 256].rearrange(
                        "p (j g c) -> p j g c", g=2, c=CH)
                    do(V.tensor_copy(cT[0:64, ri], srcc[0:64, :, 0, :]))
                    ins = V.tensor_copy(cT[64:128, ri], srcc[64:128, :, 1, :])
                    if ri == 0:
                        do(ins)
                freed(own, ins, ("cT", t))
                sync()
                mark(s_("s5_built"))

            def s5_product(t, out, parts, n, w):
                js = slice(t * TP, t * TP + TP)
                a_r, a_i = (pw[:, js, 0:n].unsqueeze(3).to_broadcast([P, TP, n, CH]) for pw in (pw_r, pw_i))
                w_r, w_i = (w[:, ri].unsqueeze(2).to_broadcast([P, TP, n, CH]) for ri in range(2))
                tv = tmp[0][:, 0:TP * n * CH].rearrange("p (j n c) -> p j n c", n=n, c=CH)
                for ri in parts:
                    o = out[:, ri].rearrange("p j (n c) -> p j n c", c=CH)
                    if ri == 0:
                        tt(o, a_r, w_r, ALU.mult)
                        tt(tv, a_i, w_i, ALU.mult)
                        tt(o, o, tv, ALU.subtract)
                        continue
                    tt(o, a_r, w_i, ALU.mult)
                    tt(tv, a_i, w_r, ALU.mult)
                    if w is cT:
                        do(V.scalar_tensor_tensor(o, o, -1.0, tv, ALU.mult, ALU.subtract))
                        sync()
                    else:
                        tt(o, o, tv, ALU.add)

            def beside_win0(m):
                if m == 0:
                    s5_unit()
                elif m == 1:
                    s5_factor()
                elif m == 2:
                    s5_powers()
                elif m == 3:
                    s5_b(0)
                    s5_c(0)
                elif m == 4:
                    s5_product(0, bp, (0, 1), CHUNK, bb[0])
                    mark(s_("bp_ready"))
                elif m in (5, 6):
                    s5_product(0, cp[0], (m - 5,), CHUNK + 1, cT)
                    if m == 6:
                        mark(s_("cp_ready"))

            def gate_of(m):
                dve.wait_ge(s_("sig_made"), m + 1)
                gt = gate[:, m, 0:T].rearrange("p (k j) -> p k j", j=CHUNK)
                do(V.tensor_tensor(gt, gt, time_order(y[:, m, :]), ALU.mult))
                do(V.tensor_tensor(gate[:, m, T:NT], gate[:, m, T:NT], y[:, m, T:NT], ALU.mult))
                sync()
                mark(s_("gated"))
                split_lo(m, gate[:, m, :], None)

            def mem_q():
                evac(("qrow", 0, 1), qrow[:, SEQW:D], bank(("qrow", 0, 1))[0:NB, 256:512])
                sync()
                mark(s_("qrow_ready"))

            def mem_sample(l, m, b):
                dve.wait_ge(s_(f"mk_in{b % 2}"), 16 * (4 * l + b // 2 + 1))
                full(dve, ("mq", l, b))
                q_b = bank(("mq", l, b))[:, 0:256].unsqueeze(1).to_broadcast([P, 2, 256])
                ins = V.tensor_tensor(m["prod"][:], m["k"][:, b % 2], q_b, ALU.mult)
                freed(own, ins, ("mq", l, b))
                sync()
                tell(V.tensor_reduce(m["s"][:, b], m["prod"][:].rearrange("p c (h d) -> p c h d", d=DH), AX.X,
                                     ALU.add), s_("mk_used"), NB * l + b + 1)
                sync()

            def mem_head(l, m, h):
                for a_ in range(2):
                    n = 8 * l + 2 * h + a_
                    full(dve, ("mS", l, h, a_))
                    if n >= 2:
                        prev = ("mT", l, (2 * h + a_ - 2) // 2, a_) if 2 * h + a_ >= 2 else ("mT", 0, 3, a_)
                        full(dve, prev)
                    st = m["st"][:, a_, :]
                    do(V.tensor_reduce(st[:, 0:2], bank(("mS", l, h, a_))[:].rearrange("p (q k) -> p q k", q=2),
                                       AX.X, ALU.max))
                    sync()
                    tell(V.tensor_scalar(st[:, 2:4], st[:, 0:2], -SCALE, None, ALU.mult, ALU.bypass),
                         s_("mneg"), n + 1)
                for b in samples_of(l, h):
                    mem_sample(l, m, b)
                for a_ in range(2):
                    n, st = 8 * l + 2 * h + a_, m["st"][:, a_, :]
                    if l == 0 and h:
                        gate_of(2 * (h - 1) + a_)
                    dve.wait_ge(s_("mexp"), n + 1)
                    do(V.reciprocal(st[:, 6:8], st[:, 4:6]))
                    sync()
                    for qq in range(2):
                        pp = m["p"][:, a_, qq, :]
                        do(V.tensor_scalar(pp, pp, st[:, 6 + qq:7 + qq], None, ALU.mult, ALU.bypass))
                    sync()
                    mark(s_("mp_ready"))
                if l and h:
                    pv_out(2 * h - 1)
                if l:
                    pv_masked(2 * h)
                for a_ in range(2):
                    if h and a_ == 0:
                        full(dve, ("mO", l, h - 1))
                    evac(("mT", l, h, a_), m["pT"][:, :, 256 * a_:256 * a_ + 256],
                         bank(("mT", l, h, a_))[:].rearrange("p (k q) -> p k q", k=2))
                sync()
                mark(s_("mpT_ready"))
                if l:
                    pv_out(2 * h)
                    pv_masked(2 * h + 1)
                full(dve, ("mO", l, h))
                r = slice(DH * (h % 2), DH * (h % 2) + DH)
                src = bank(("mO", l, h))[r, :]
                if l == 0 and h == 0:
                    dve.wait_ge(s_("yz_used"), THIRDS)
                do(V.tensor_copy(x_hi[r, 6 + h // 2, 0:T], src))
                sync()
                freed(own, V.tensor_tensor(x_lo[r, 6 + h // 2, 0:T], src,
                                           x_hi[r, 6 + h // 2, 0:T].bitcast(F32), ALU.subtract), ("mO", l, h))

            def mem_samples(l, m):
                if l:
                    pv_out(NB - 1)
                    sync()
                    mark(s_("fox_done"))
                sv = m["s"][:].rearrange("p b c h -> p (b c h)")
                do(V.tensor_scalar(sv, sv, SCALE, None, ALU.mult, ALU.bypass))
                sync()
                decode_softmax(m["s"], m["dst"], MEMH, 2, ("mmaxT", l), ("mmax", l), ("mden", l), l)
                full(dve, ("mpv", l))
                pv = bank(("mpv", l))[:, 0:NB * 2 * 2].rearrange("p (b f e) -> p f b e", f=2, e=2)
                for e in range(2):
                    r = slice(DH * e, DH * e + DH)
                    do(V.tensor_copy(x_hi[r, 6:8, T:NT], pv[r, :, :, e]))
                sync()
                for e in range(2):
                    r = slice(DH * e, DH * e + DH)
                    ins = V.tensor_tensor(x_lo[r, 6:8, T:NT], pv[r, :, :, e], x_hi[r, 6:8, T:NT].bitcast(F32),
                                          ALU.subtract)
                    if e == 0:
                        do(ins)
                freed(own, ins, ("mpv", l))
                sync()
                mark(s_("mem_done"))

            ndec = [0]

            def decode_softmax(s, st, H, pgs, jT, jM, jD, l):
                BH = NB * H
                n = ndec[0] = ndec[0] + 1
                m1, mx, dg, sm, inv = (st[:, k_, 0:BH] for k_ in range(5))
                do(V.tensor_reduce(m1.rearrange("p (b h) -> p b h", h=H), s[:].rearrange("p b g h -> p b h g"),
                                   AX.X, ALU.max))
                sync()
                mark(s_("dmax1"))
                full(dve, jT)
                freed(own, V.tensor_reduce(mx[0:BH, 0:1], bank(jT)[0:BH, 0:P], AX.X, ALU.max), jT)
                sync()
                tell(V.tensor_scalar(dg[0:BH, :], ident[0:BH, 0:BH], mx[0:BH, 0:1], None, ALU.mult, ALU.bypass),
                     s_("dmax2"), n)
                full(dve, jM)
                mb_ = bank(jM)[:, 0:BH].rearrange("p (b h) -> p b h", h=H).unsqueeze(2).to_broadcast([P, NB, pgs, H])
                freed(own, V.tensor_tensor(s[:], s[:], mb_, ALU.subtract), jM)
                sync()
                mark(s_("dexp_in"))
                dve.wait_ge(s_("dexp"), n)
                do(V.tensor_reduce(sm.rearrange("p (b h) -> p b h", h=H), s[:].rearrange("p b g h -> p b h g"),
                                   AX.X, ALU.add))
                sync()
                mark(s_("dsum"))
                full(dve, jD)
                freed(own, V.reciprocal(inv, bank(jD)[:, 0:BH]), jD)
                sync()
                iv = inv.rearrange("p (b h) -> p b h", h=H).unsqueeze(2).to_broadcast([P, NB, pgs, H])
                tell(V.tensor_tensor(s[:], s[:], iv, ALU.mult), s_("dp_ready"), n)
                sync()

            def sums_ready():
                mark(s_("sumsq_ready"))

            do(V.memset(eps[:], EPS))
            mark(s_("h_made"))
            evac(("rows",), gains[:], bank(("rows",))[:, 0:100])
            for a_ in range(4):
                full(dve, ("memT", a_))
                freed(own, V.tensor_copy(memT[:, 2 * a_:2 * a_ + 2, :].rearrange("p k t -> p (k t)"),
                                         bank(("memT", a_))[:, :]), ("memT", a_))
            sync()
            mark(s_("mem_ready"))

            def small_inputs():
                dve.wait_ge(s_("lam_in"), 48)
                dve.wait_ge(s_("lrow_zero"), 1)
                do(V.tensor_copy(lrow[64:64 + PAIRS, :].rearrange("j (g p) -> j g p", g=2),
                                 dtrow[:].unsqueeze(2).to_broadcast([PAIRS, 2, STATE])))
                mark(s_("lrow_ready"))
                evac(("lam",), lam[:, 0:96], bank(("lam",))[:, 0:96])
                mark(s_("lam_ready"))
                for l in range(2):
                    for a_ in range(2):
                        evac(("conv", l, a_), convw[:, l, 88 * a_:88 * a_ + 88], bank(("conv", l, a_))[:, 0:88])
                for l in range(2):
                    flat = convs[:, l].rearrange("p r f -> p (r f)")
                    for a_ in range(2):
                        w = 512 if a_ == 0 else 192
                        evac(("state", l, a_), flat[:, 512 * a_:512 * a_ + w], bank(("state", l, a_))[:, 0:w])
                for k in range(KD):
                    evac(("xT", k), x[:, k, 0:T], bank(("xT", k))[:, :])
                evac(("xsT",), x[:, :, T:NT], bank(("xsT",))[:, 0:KD * NB].rearrange("p (k b) -> p k b", b=NB))
                sync()
                mark(s_("x_ready"))

            for l in range(2):
                for k in range(KD):
                    split_lo(k, memT[:, k, :], gain("mem", k, l), slice(l * NMEM, (l + 1) * NMEM))
                if l == 0:
                    sum_squares(KD, NMEM)
                    sums_ready()
                    reciprocal_std(rstd_mem, NMEM)
            for l in range(2):
                base = PH[f"memkv{l}"][2]
                for m in range(4):
                    q = base + m
                    dve.wait_ge(panel_done, q + 1)
                    src = big[2 * (q % 2)][:, 0:NMEM]
                    dst = mem_kT[:, l, m, :] if m < 2 else sq[:, m - 2, 0:NMEM]
                    if l and m >= 2:
                        full(dve, ("memtok", 0, m))
                    tell(V.tensor_tensor(dst, src, rstd_mem[:], ALU.mult), panel_read, q + 1)
                for m in range(4):
                    full(dve, ("memtok", l, m))
                    freed(own, V.tensor_copy(mem_tok[:, l, :, m * P:(m + 1) * P],
                                             bank(("memtok", l, m))[:, 0:256].rearrange("p (c f) -> p c f", c=2)),
                          ("memtok", l, m))
                    sync()
                    mark(s_("memtok_ready"))
                if l == 0:
                    small_inputs()
                    s5_angles()

            def pre_norm(name, l):
                for k in range(KD):
                    split_lo(k, x[:, k, :], gain(name, k, l))

            sum_squares(KD, NT)
            sums_ready()
            pre_norm("mix_pre", 0)
            reciprocal_std(rstd, NT)

            def read_panel(q, dst_of, mult=True):
                slot = q % 2
                dve.wait_ge(panel_done, q + 1)
                for n, (c0, c1) in enumerate(HALF):
                    dst, src, r = dst_of(n, c0, c1), big[2 * slot + n][:, 0:c1 - c0], rstd[:, c0:c1]
                    if len(dst.shape) == 3:
                        src = src[:, 0:(c1 - c0) // 8 * 8].rearrange("p (k j) -> p k j", j=CHUNK)[:, 0:dst.shape[1], :]
                        r = r.rearrange("p (k j) -> p k j", j=CHUNK)[:, 0:dst.shape[1], :]
                    ins = V.tensor_tensor(dst, src, r, ALU.mult)
                    if n == 0 or len(dst.shape) == 3:
                        do(ins)
                if len(dst.shape) == 3:
                    ins = V.tensor_tensor(dst_of(2, T, NT), big[2 * slot + 1][:, T - HALF[1][0]:NT - HALF[1][0]],
                                          rstd[:, T:NT], ALU.mult)
                tell(ins, panel_read, q + 1)

            def by_chunk(tile):
                return tile[:, 0:T].rearrange("p (j k) -> p k j", j=CHUNK)

            K0 = HALF[0][1] // CHUNK
            for m in range(8):
                q = PH["win0"][2] + m
                if m < KS:
                    pick = {0: by_chunk(y[:, m, :])[:, 0:K0, :], 1: by_chunk(y[:, m, :])[:, K0:NCH, :],
                            2: y[:, m, T:NT]}
                    read_panel(q, lambda n, c0, c1: pick[n])
                else:
                    read_panel(q, lambda n, c0, c1: y[:, m, c0:c1])
                sync()
                mark(s_("z_ready"))
                beside_win0(m)

            do(V.memset(u[0][:], 0.0))
            mark(s_("s5_zero"))
            do(V.memset(toep[:], 0.0))
            mark(s_("s5_zero"))
            for ri in range(2):
                for half in range(2):
                    evac(("h0", ri, half), h0[:, ri].rearrange("p b j -> p (b j)")[:, 96 * half:96 * half + 96],
                         bank(("h0", ri, half))[:, 0:96])
            for hp_ in hp:
                do(V.memset(hp_[:, :, :, NB:NB + 1], 0.0))
            sync()

            for t in range(THIRDS):
                j0 = t * TP
                js = slice(j0, j0 + TP)
                for a_ in range((TP + 2) // 3):
                    n = min(3, TP - 3 * a_)
                    full(dve, ("V", t, a_))
                    src = bank(("V", t, a_))[:, 0:n * 2 * (NCH + NB)].rearrange("p (j r k) -> p j r k", r=2, k=NCH + NB)
                    do(V.tensor_copy(v[:, 0, 3 * a_:3 * a_ + n], src[:, :, 0, :]))
                    freed(own, V.tensor_copy(v[:, 1, 3 * a_:3 * a_ + n], src[:, :, 1, :]), ("V", t, a_))
                sync()
                dve.wait_ge(s_("table_ready"), t + 1)
                dve.wait_ge(s_("decay_ready"), 1)
                w_ = [tmp[n_][:, 0:TP * NCH].rearrange("p (j k) -> p j k", k=NCH) for n_ in range(3)]
                cmul(w_[0], w_[1], e_r[:, js], e_i[:, js], v[:, 0, :, 0:NCH], v[:, 1, :, 0:NCH], w_[2], conj=True)
                flat = [tmp[n_][:, 0:TP * NCH] for n_ in range(2)]
                dflat = decay[:, js].rearrange("p j k -> p (j k)")
                g_ = tmp[2][:, 0:TP * NCH]
                g2 = tmp[0][:, TP * NCH:2 * TP * NCH]
                do(V.tensor_tensor_scan(g_, dflat, flat[0], 0.0, ALU.mult, ALU.add))
                do(V.tensor_tensor_scan(g2, dflat, flat[1], 0.0, ALU.mult, ALU.add))
                sync()
                g2v = g2.rearrange("p (j k) -> p j k", k=NCH)
                if t >= 2:
                    full(dve, ("Y", t - 2, 3))
                hp_ = hp[t % 2]
                cmul(hp_[:, 0, :, NB + 1:], hp_[:, 1, :, NB + 1:], e_r[:, js], e_i[:, js], w_[2], g2v, w_[1])
                hT = h0[:].rearrange("p r b j -> p r j b")
                for ri in range(2):
                    do(V.tensor_copy(hp_[:, ri, :, 0:NB], hT[:, ri, js, :]))
                sync()
                mark(s_("hp_ready"))
                fT = hfin[:].rearrange("p r b j -> p r j b")
                a_r = pw_r[:, js, 1:2].to_broadcast([P, TP, NB])
                a_i = pw_i[:, js, 1:2].to_broadcast([P, TP, NB])
                tv = tmp[0][:, 0:TP * NB].rearrange("p (j b) -> p j b", b=NB)
                cmul(fT[:, 0, js, 1:], fT[:, 1, js, 1:], a_r, a_i, hT[:, 0, js, :], hT[:, 1, js, :], tv)
                for ri in range(2):
                    tt(fT[:, ri, js, 1:], fT[:, ri, js, 1:], v[:, ri, :, NCH:], ALU.add)
                    do(V.tensor_copy(fT[:, ri, js, 0:1], hp_[:, ri, :, NB + NCH:]))
                if t + 1 < THIRDS:
                    s5_b(t + 1)
                    full(dve, ("bT", t, 3))
                    s5_product(t + 1, bp, (0, 1), CHUNK, bb[(t + 1) % 2])
                    mark(s_("bp_ready"))
                    s5_c(t + 1)
                    if t:
                        full(dve, ("Y", t - 1, 3))
                    s5_product(t + 1, cp[(t + 1) % 2], (1,), CHUNK + 1, cT)
                    mark(s_("cp_ready"))
            mark(s_("hfin_ready"))
            for ri in range(2):
                full(dve, ("fin", ri))
                freed(own, V.tensor_copy(hout[:, ri].rearrange("p a n -> p (a n)"), bank(("fin", ri))[0:108, 0:256]),
                      ("fin", ri))
                sync()
                mark(s_("hout_ready"))
            mem_q()
            mem_head(0, mb[0], 0)
            dve.wait_ge(s_("stored"), 16 * 10)
            dve.wait_ge(s_("gelu_made"), THIRDS)
            mark(s_("x_free"))

            def time_order(tile):
                return tile[:, 0:T].rearrange("p (j k) -> p k j", j=CHUNK)

            for k in range(KS):
                stat[1] += 2
                dve.wait_ge(s_("xhi_made"), stat[1])
                for c, (dst, srcv) in enumerate((
                        (slice(0, T), time_order(y[:, k, :])), (slice(T, NT), y[:, k, T:NT]))):
                    h = x_hi[:, k, dst].bitcast(F32)
                    o = x_lo[:, k, dst]
                    if c == 0:
                        h = h.rearrange("p (k j) -> p k j", j=CHUNK)
                        o = o.rearrange("p (k j) -> p k j", j=CHUNK)
                    tell(V.tensor_tensor(o, srcv, h, ALU.subtract), s_("xlo_made"), stat[1] - 1 + c)
            for m in range(KS):
                q = PH["glu"][2] + m
                dve.wait_ge(panel_done, q + 1)
                do(V.tensor_scalar(gate[:, m, 0:264], big[2 * (q % 2)][:, 0:264], gain("bglu", m), None, ALU.add, ALU.bypass))
                tell(V.tensor_scalar(gate[:, m, 264:NT], big[2 * (q % 2) + 1][:, 0:256], gain("bglu", m), None,
                                     ALU.add, ALU.bypass), panel_read, q + 1)
            sync()
            mark(s_("gate_ready"))
            for h in range(1, MEMH):
                mem_head(0, mb[0], h)
            mem_samples(0, mb[0])

            npost = [0]

            def post_norm(name, l, nxt, nl):
                sums_ready()
                reciprocal_std(rstd, NT)
                lag = 3
                for k in range(KD + lag):
                    if k < KD:
                        npost[0] += 1
                        tell(V.scalar_tensor_tensor(y[:, k, :], y[:, k, :], gain(name, k, l), rstd[:], ALU.mult,
                                                    ALU.mult), s_("y_scaled"), npost[0])
                    if nxt is not None and k >= lag:
                        split_lo(k - lag, x[:, k - lag, :], gain(nxt, k - lag, nl))
                if nxt is not None:
                    sync()
                    for k in range(KD):
                        sum_step(k, y[:, k, :], "sq_made", "sq_used")
                    sync()
                    sums_ready()
                    reciprocal_std(rstd, NT)

            def copy_out(ph, add=None, conv=None):
                for m in range(8):
                    q = PH[ph][2] + m
                    dve.wait_ge(panel_done, q + 1)
                    for n_, (c0, c1) in enumerate(HALF):
                        dst, src = y[:, m, c0:c1], big[2 * (q % 2) + n_][:, 0:c1 - c0]
                        ins = V.tensor_tensor(dst, dst, src, add) if add else V.tensor_copy(dst, src)
                        if n_:
                            tell(ins, panel_read, q + 1)
                        else:
                            do(ins)
                    for a_ in conv_rows(m) if conv is not None else ():
                        full(dve, ("cout", conv, a_))
                        if 11 * conv + a_ >= 2:
                            before = (a_ // 2 + (conv * (6 - a_ % 2)))
                            dve.wait_ge(s_(f"crows_out{a_ % 2}"), 32 * before)
                        freed(own, V.tensor_copy(crows[a_ % 2][0:2 + NB, 0:4 * P], bank(("cout", conv, a_))[0:2 + NB, :]),
                              ("cout", conv, a_))
                        mark(s_("crows_ready"))
                    sum_step(m, sq[:, stat[0] % 2, :], "sq_made", "sq_used")
                sync()

            def ffn(l):
                for f in range(2):
                    _, n, base, _ = PH[f"up{l}{f}"]
                    step0, r = own.n, None
                    K = 10
                    if f == 0:
                        for s in range(2):
                            do(V.memset(uc[s][:, 0:2], 0.0))
                        sync()
                        step0 = own.n
                    done = 22 * l + 11 * f
                    with dve.Fori(0, KH) as it:
                        c = [0]

                        def st(ins):
                            c[0] += 1
                            ins.then_inc(dve_step, 1)

                        def sy():
                            dve.wait_ge(dve_step, it * K + (step0 + c[0]))

                        for half in range(2):
                            q = it * 2 + (base + half)
                            slot = (base + half) % 2
                            fb = it + (f * KH + half * KF)
                            w_ = [convw[:, l, bass.ds(it + (f * KH + half * KF + 44 * tp), 1)] for tp in range(3)]
                            uu, yy = uc[half], yc[half]
                            dve.wait_ge(panel_done, q + 1)
                            st(V.tensor_tensor(uu[:, 2:266], big[2 * slot][:, 0:264], rstd[:, 0:264], ALU.mult))
                            V.tensor_tensor(uu[:, 266:2 + NT], big[2 * slot + 1][:, 0:256], rstd[:, 264:NT],
                                            ALU.mult).then_inc(panel_read, 1)
                            dve.wait_ge(s_("tap_made"), it * 2 + (2 * done + half + 1))
                            st(V.scalar_tensor_tensor(yy[:, 0:T], uu[:, 1:1 + T], w_[1], yy[:, 0:T], ALU.mult, ALU.add))
                            old = convs[:, l, :, bass.ds(it + (f * KH + half * KF), 1)].rearrange(
                                "p (b t) a -> p t (b a)", t=2)
                            st(V.scalar_tensor_tensor(yy[:, T:NT], old[:, 1], w_[1], yy[:, T:NT], ALU.mult, ALU.add))
                            sy()
                            st(V.scalar_tensor_tensor(yy[:, 0:T], uu[:, 0:T], w_[0], yy[:, 0:T], ALU.mult, ALU.add))
                            V.scalar_tensor_tensor(yy[:, T:NT], old[:, 0], w_[0], yy[:, T:NT], ALU.mult,
                                                   ALU.add).then_inc(s_("conv_made"), 1)
                        dve.wait_ge(s_("silu_made"), it + (done + 1))
                        dve.wait_ge(s_("conv_made"), it * 2 + (2 * done + 2))
                        st(V.tensor_tensor(hf[:], sg[:], yc[1][:], ALU.mult))
                        sy()
                        st(V.tensor_copy(h_hi[:, bass.ds(it, 1), :].rearrange("p a t -> p (a t)"), hf[:]))
                        sy()
                        V.tensor_tensor(h_lo[:, bass.ds(it, 1), :].rearrange("p a t -> p (a t)"), hf[:],
                                        h_hi[:, bass.ds(it, 1), :].rearrange("p a t -> p (a t)").bitcast(F32),
                                        ALU.subtract).then_inc(s_("h_made"), 1)
                    own.n = step0 + KH * c[0]
                    assert c[0] == K, c[0]
                    if f == 0:
                        base = PH[f"down{l}{f}"][2]
                        with dve.Fori(0, 4) as it:
                            for half in range(2):
                                slot = (base + half) % 2
                                dve.wait_ge(panel_done, it * 2 + (base + half + 1))
                                for n_, (c0, c1) in enumerate(HALF):
                                    dst = y[:, bass.ds(it * 2 + half, 1), c0:c1].rearrange("p a t -> p (a t)")
                                    V.tensor_copy(dst, big[2 * slot + n_][:, 0:c1 - c0]).then_inc(
                                        panel_read if n_ else dve_step, 1)
                        own.n += 8
                    else:
                        copy_out(f"down{l}1", ALU.add, l)

            copy_out("wout0")
            post_norm("mix_post", 0, "ffn_pre", 0)
            ffn(0)
            post_norm("ffn_post", 0, "kv", 0)

            for s in range(2):
                dve.wait_ge(s_(f"crows_out{s}"), 32 * (6 - s))
            do(V.memset(qh[DH:P, :, :], 0.0))
            for m in range(12):
                q = PH["kv"][2] + m
                if m:
                    full(dve, ("kvsamp", m - 1))
                    if m <= 6:
                        dve.wait_ge(s_("kh_made"), m)
                read_panel(q, lambda n, c0, c1: kvT[:, c0:c1])
                sync()
                mark(s_("kvT_ready"))
                if m < 6 and m >= 2:
                    dve.wait_ge(s_(f"ktok_out{m % 2}"), 16 * (m // 2))
                if m < 6:
                    evac(("kvtok", m), ktok[m % 2][:], bank(("kvtok", m))[:].rearrange("p (c f) -> p c f", c=4))
                else:
                    evac(("kvtok", m), vtok[:, :, 2 * (m - 6):2 * (m - 5), 0:DH],
                         bank(("kvtok", m))[:].rearrange("p (c h d) -> p c h d", c=4, h=2))
                if m == 1:
                    do(V.memset(kh[DH:P, :, :], 0.0))
                elif m == 2:
                    do(V.memset(qh[DH:DH + 2, :, :], 1.0))
                elif m == 3:
                    do(V.memset(kh[DH:DH + 2, :, :], 1.0))
                elif m == 4:
                    do(V.memset(kh[96:97, :, :], 1.0))
                elif m == 5:
                    do(V.memset(vtok[:, :, :, DH:DH + 1], 1.0))
                sync()
                mark(s_("ktok_ready" if m < 6 else "vtok_ready"))
                evac(("kvsamp", m), kvs[:, m // 6, (m % 6) * P:(m % 6 + 1) * P], bank(("kvsamp", m))[0:NB, 0:P])
                sync()
                mark(s_("kvs_ready"))
            q = PH["kvf"][2]
            dve.wait_ge(panel_done, q + 1)
            z_, m_, l_ = lf[:, 0, :], lf[:, 1, :], lf[:, 2, :]
            do(V.tensor_tensor(z_[:, 0:264], big[2 * (q % 2)][0:HEADS, 0:264], rstd[0:HEADS, 0:264], ALU.mult))
            tell(V.tensor_tensor(z_[:, 264:NT], big[2 * (q % 2) + 1][0:HEADS, 0:256], rstd[0:HEADS, 264:NT], ALU.mult),
                 panel_read, q + 1)
            sync()
            pre_norm("mix_pre", 1)
            dve.wait_ge(s_("bf_in"), 16)
            ts(z_, z_, bf[:, 0:1], None, ALU.add, ALU.bypass)
            ts(m_, z_, -1.0, None, ALU.mult, ALU.bypass)
            tell(V.tensor_tensor(m_, m_, z_, ALU.min), s_("nabs_ready"), 1)
            dve.wait_ge(s_("log_made"), 1)
            tell(V.scalar_tensor_tensor(m_, z_, 0.0, l_, ALU.min, ALU.subtract), s_("lf_ready"), 1)
            sync()
            do(V.memset(z_, 1.0))
            sync()
            do(V.tensor_tensor_scan(l_[:, 0:T], z_[:, 0:T], m_[:, 0:T], 0.0, ALU.mult, ALU.add))
            sync()
            do(V.tensor_scalar(lf[:, 0, 0:T], l_[:, 0:T], -1.0 / SCALE, None, ALU.mult, ALU.bypass))
            sync()
            do(V.tensor_scalar(l_[:, 0:T], l_[:, 0:T], 1.0 / SCALE, None, ALU.mult, ALU.bypass))
            sync()
            for n in range(3):
                mark(s_("c_ready"))
            full(dve, ("logf",))
            do(V.tensor_copy(lft[:, 0:4, :], bank(("logf",))[:, 0:48].rearrange("p (c h) -> p c h", h=HEADS)))
            freed(own, V.tensor_copy(lfs[:], bank(("logf",))[0:NB, 48:60]), ("logf",))
            sync()
            for n in range(2):
                mark(s_("logf_ready"))

            for m in range(8):
                q = PH["win1"][2] + m
                slot = q % 2
                dve.wait_ge(panel_done, q + 1)
                if m < 6:
                    for n, (c0, c1) in enumerate(HALF):
                        e1 = min(c1, T)
                        for e in range(2):
                            r = slice(DH * e, DH * e + DH)
                            do(V.tensor_tensor(qh[0:DH, 2 * m + e, c0:e1], big[2 * slot + n][r, 0:e1 - c0],
                                               rstd[r, c0:e1], ALU.mult))
                    tell(V.tensor_tensor(qs[:, m, :], big[2 * slot + 1][:, 248:256], rstd[:, T:NT], ALU.mult),
                         panel_read, q + 1)
                else:
                    do(V.tensor_tensor(y[:, m, 0:264], big[2 * slot][:, 0:264], rstd[:, 0:264], ALU.mult))
                    tell(V.tensor_tensor(y[:, m, 264:NT], big[2 * slot + 1][:, 0:256], rstd[:, 264:NT], ALU.mult),
                         panel_read, q + 1)
            sync()
            mark(s_("q1_ready"))

            for a_ in range(2):
                evac(("qrow", 1, a_), qrow[:, 512 * a_:512 * a_ + 512], bank(("qrow", 1, a_))[0:NB, :])
            sync()
            mark(s_("qrow_ready"))
            dve.wait_ge(panel_done, PH["win1"][2] + 8)
            snew, idneg = fst[0:NB, 7, 0:HEADS], fst[0:NB, 7, 16:16 + NB]
            do(V.memset(sc[:], NEG))
            tt(kvq, kvs[:, 0, :], qrow[:, 0:SEQW], ALU.mult)
            do(V.tensor_reduce(snew, kvq.rearrange("p (h d) -> p h d", d=DH), AX.X, ALU.add))
            do(V.tensor_scalar(idneg, ident[0:NB, 0:NB], -NEG, NEG, ALU.mult, ALU.add))
            sync()
            ts(snew, snew, SCALE, None, ALU.mult, ALU.bypass)
            idb = ident[0:NB, 0:NB].unsqueeze(2).to_broadcast([NB, NB, HEADS])
            tt(sc[0:NB, :, PAGES, :], idb, snew.unsqueeze(1).to_broadcast([NB, NB, HEADS]), ALU.mult)
            tt(sc[0:NB, :, PAGES, :], sc[0:NB, :, PAGES, :], idneg.unsqueeze(2).to_broadcast([NB, NB, HEADS]), ALU.add)
            tt(lmask[:], idb, lfs[:].unsqueeze(1).to_broadcast([NB, NB, HEADS]), ALU.mult)

            def past_decay():
                dve.wait_ge(s_("logf_in"), 16 * NB * PAGES)
                do(V.memset(pre[:, :, 0, :], 0.0))
                sync()
                for pg in range(1, PAGES):
                    tt(pre[:, :, pg, :], pre[:, :, pg - 1, :], logf[:, :, pg - 1, :], ALU.add)
                tot = fst[:, 5, 0:BH].rearrange("p (b h) -> p b h", h=HEADS)
                tt(tot, pre[:, :, PAGES - 1, :], logf[:, :, PAGES - 1, :], ALU.add)
                mark(s_("pre_ready"))
                evac(("dtot",), fst[:, 6, 0:BH], bank(("dtot",))[:, 0:BH])
                sync()
                cq = fst[:, 6, 0:BH].rearrange("p (b h) -> p b h", h=HEADS)
                for a_ in range(2):
                    full(dve, ("dc", a_))
                    bs = slice(4 * a_, 4 * a_ + 4)
                    src = bank(("dc", a_))[:, 0:384].rearrange("p (b g h) -> p b g h", b=4, h=HEADS)
                    freed(own, V.tensor_tensor(pre[:, bs], cq[:, bs].unsqueeze(2).to_broadcast([P, 4, PAGES, HEADS]),
                                               src, ALU.subtract), ("dc", a_))

            BH = NB * HEADS
            AQ = ((512, ((0, 512, 3),)), (512, ((0, 384, 2), (384, 512, 0))), (256, ((0, 256, 1),)))
            dve.wait_ge(s_("causal_t_ready"), 1)
            done = 0
            for i in range(STEPS):
                if i < HEADS:
                    s_banks = [bank(("S", i, a_)) for a_ in range(3)]
                    full(dve, ("S", i, 0))
                    do(V.tensor_tensor(s_banks[0][:, 384:512], s_banks[0][:, 384:512], causal[:], ALU.add))
                    full(dve, ("S", i, 1))
                    o = s_banks[1][:, 256:512].rearrange("p (a k) -> p a k", a=2)
                    do(V.tensor_tensor(o, o, causal[:].unsqueeze(1).to_broadcast([P, 2, P]), ALU.add))
                    full(dve, ("S", i, 2))
                    do(V.tensor_tensor(s_banks[2][:, 128:256], s_banks[2][:, 128:256], causal[:], ALU.add))
                    sync()
                    for a_, (_, parts) in enumerate(AQ):
                        for n, (c0, c1, qi) in enumerate(parts):
                            ins = V.tensor_reduce(nmax[i % 2][:, qi:qi + 1], s_banks[a_][:, c0:c1], AX.X, ALU.max)
                            if n < len(parts) - 1:
                                do(ins)
                        freed(own, ins, ("S", i, a_))
                    sync()
                    tell(V.tensor_scalar(nmax[i % 2][:], nmax[i % 2][:], -1.0, None, ALU.mult, ALU.bypass),
                         s_("nmax_ready"), i + 1)
                if i >= 3:
                    h = h_out = i - 3
                    r = r_out = slice(DH * (h % 2), DH * (h % 2) + DH)
                    full(dve, ("R", h))
                    out = x_out[r, h // 2, 0:T]
                    dve.wait_ge(s_("o_copied"), h + 1)
                    freed(own, V.tensor_tensor(out, out, bank(("R", h))[r, :], ALU.mult), ("R", h))
                    mark(s_("o_scaled"))
                if 1 <= i <= HEADS:
                    for a_ in range(3):
                        full(dve, ("T", i - 1, a_))
                        o = bank(("T", i - 1, a_))[:].rearrange("p (a k) -> p a k", a=4)[:, 0:4 if a_ == 1 else 1:3, :]
                        do(V.tensor_tensor(o, o, causal_t[:].unsqueeze(1).to_broadcast([P, 2 if a_ == 1 else 1, P]),
                                           ALU.add))
                        mark(s_("t_masked"))
                if i >= 3:
                    dve.wait_ge(s_("o_rounded"), h_out + 1)
                    do(V.tensor_tensor(x_lo[r_out, h_out // 2, 0:T], out, x_hi[r_out, h_out // 2, 0:T].bitcast(F32),
                                       ALU.subtract))
                if i == DECAY_STEP:
                    past_decay()
                upto = min(NB * PAGES, NB * PAGES * i // (HEADS - 1))
                for n in range(done, upto):
                    dve.wait_ge(s_("k_product"), n + 1)
                    tell(V.tensor_reduce(sc[:, n // PAGES, n % PAGES, :],
                                         page[n % PAGES][:].rearrange("p (h d) -> p h d", d=DH), AX.X, ALU.add),
                         s_("k_used"), n + 1)
                done = upto
                if 2 <= i <= HEADS + 1:
                    full(dve, ("O", i - 2))
                    tell(V.reciprocal(rinv[:], bank(("O", i - 2))[DH:DH + 1, :]), s_("rinv_ready"), i - 1)
                if i == SOFTMAX_STEP:
                    sync()
                    do(V.scalar_tensor_tensor(sc[:, :, 0:PAGES, :].rearrange("p b g h -> p b (g h)"),
                                              sc[:, :, 0:PAGES, :].rearrange("p b g h -> p b (g h)"), SCALE,
                                              pre[:].rearrange("p b g h -> p b (g h)"), ALU.mult, ALU.add))
                    sync()
                    decode_softmax(sc, fst, HEADS, PAGES + 1, ("fmaxT",), ("fmax",), ("fden",), 1)
            sync()
            mark(s_("heads_done"))
            dve.wait_ge(s_("block_diag"), 1)

            def pv_masked(b):
                dve.wait_ge(s_("pv_done"), b + 1)
                if b:
                    full(dve, ("fpv", b - 1))
                for a_ in range(2):
                    do(V.tensor_tensor(vm[0:HEADS, 384 * a_:384 * a_ + 384], big[2 * (b % 2) + a_][0:HEADS, 0:384],
                                       block_diag[0:HEADS, 384 * a_:384 * a_ + 384], ALU.mult))
                mark(s_("vm_ready"))

            def pv_out(b):
                full(dve, ("fpv", b))
                o = bank(("fpv", b))[:, 0:6].unsqueeze(2)
                do(V.tensor_copy(x_hi[:, 0:6, T + b:T + b + 1], o))
                sync()
                freed(own, V.tensor_tensor(x_lo[:, 0:6, T + b:T + b + 1], o,
                                           x_hi[:, 0:6, T + b:T + b + 1].bitcast(F32), ALU.subtract), ("fpv", b))

            for h in range(MEMH):
                mem_head(1, mb[1], h)
            mem_samples(1, mb[1])

            dve.wait_ge(s_("stored"), 16 * 19)
            copy_out("wout1")
            post_norm("mix_post", 1, "ffn_pre", 1)
            ffn(1)
            post_norm("ffn_post", 1, None, 0)

        @block.scalar
        def _(act):
            own = Own(act, act_step)
            do, tell, sync, mark = own.do, own.tell, own.sync, own.mark
            A = act
            stat = [0, 0, 0]

            def hi(kb, half_c, it=None):
                slot = half_c % 2
                if it is None:
                    q, loads = half_c, half_c // 2 + 1
                else:
                    q, loads = it * 2 + half_c, it + (half_c // 2 + 1)
                act.wait_ge(raw_loaded[slot], loads * 16)
                if it is not None or q >= 2:
                    act.wait_ge(panel_done, q - 1)
                A.activation(w_hi[slot][:, 0:kb, :], raw[slot][:, 0:kb, :], ACT.Copy).then_inc(hi_made, 1)

            def run(name, work=None, ahead=True, started=True):
                kb, n, base, nxt = PH[name]
                work = work or (lambda it, half: None)
                if not started:
                    hi(kb, base)
                    hi(kb, base + 1)
                pairs = n // 2
                if pairs > 2:
                    with act.Fori(0, pairs - 1) as it:
                        for half in range(2):
                            hi(kb, base + half + 2, it)
                            work(it, half)
                for i in range(n - 2 if pairs > 2 else 0, n):
                    if i + 2 < n:
                        hi(kb, base + i + 2)
                    elif ahead:
                        hi(PH[nxt][0], base + i + 2)
                    work(i // 2, i % 2)

            def squares(count, src, cols, ready):
                for k in range(count):
                    ready(k)
                    n = stat[0]
                    if n >= 2:
                        act.wait_ge(s_("sq_used"), n - 1)
                    stat[0] += 1
                    tell(A.activation(sq[:, n % 2, 0:cols], src(k), ACT.Square), s_("sq_made"), n + 1)

            def root(jobs):
                if stat[2]:
                    act.wait_ge(s_("rstd_ready"), stat[2])
                do(A.activation(root_warm[:], eps[:], ACT.Sqrt))
                for job, c0, c1 in jobs:
                    full(act, job)
                    freed(own, A.activation(sd[:, c0:c1], bank(job)[:, 0:c1 - c0], ACT.Sqrt, bias=eps[:, 0:1]), job)
                stat[2] += 1
                mark(s_("root_made"))

            def root_x(name):
                root([(("ms", name, n), c0, c1) for n, (c0, c1) in enumerate(HALF)])

            def split_hi(k, src, g=None, cols=slice(0, NT)):
                stat[1] += 1
                o = x_hi[:, k, cols]
                if len(src.shape) == 3:
                    o = o.rearrange("p (k j) -> p k j", j=CHUNK)
                ins = A.activation(o, src, ACT.Copy, scale=1.0 if g is None else g)
                tell(ins, s_("xhi_made"), stat[1])

            hi(KD, 0)
            hi(KD, 1)
            act.wait_ge(s_("mem_ready"), 1)
            for l in range(2):
                for k in range(KD):
                    split_hi(k, memT[:, k, :], gain("mem", k, l), slice(l * NMEM, (l + 1) * NMEM))
                if l == 0:
                    squares(KD, lambda k: memT[:, k, :], NMEM, lambda k: None)
                    root([(("ms_mem",), 0, NMEM)])
            run("memkv0")
            act.wait_ge(s_("lam_ready"), 1)
            tell(A.activation(lam[:, 64:64 + PAIRS], lam[:, 64:64 + PAIRS], ACT.Exp), s_("s5_act"), 1)
            run("memkv1")
            act.wait_ge(s_("angles_ready"), 1)
            for n, (dst, src, fn, sca) in enumerate((
                    (3, 1, ACT.Exp, 1.0), (6, 1, ACT.Exp, 8.0), (4, 12, ACT.Sin, 1.0), (5, 13, ACT.Sin, 1.0))):
                tell(A.activation(s5s[:, dst, :], s5s[:, src, :], fn, scale=sca), s_("s5_act"), n + 2)
            act.wait_ge(s_("x_ready"), 1)
            full(act, ("memtok", 1, 3))
            squares(KD, lambda k: x[:, k, :], NT, lambda k: None)
            act.wait_ge(panel_done, 8)
            for k in range(KD):
                split_hi(k, x[:, k, :], gain("mix_pre", k, 0))
            root_x("x0")
            run("win0", ahead=False)

            def mem_head(l, m, h):
                for a_ in range(2):
                    n = 8 * l + 2 * h + a_
                    act.wait_ge(s_("mneg"), n + 1)
                    for qq in range(2):
                        st = m["st"][:, a_, :]
                        ins = A.activation(m["p"][:, a_, qq, :], bank(("mS", l, h, a_))[:, 256 * qq:256 * qq + 256],
                                           ACT.Exp, bias=st[:, 2 + qq:3 + qq], scale=SCALE,
                                           accum_out=st[:, 4 + qq:5 + qq])
                        if qq:
                            freed(own, ins, ("mS", l, h, a_))
                        else:
                            do(ins)
                    mark(s_("mexp"))
                    if l == 0 and h:
                        g = 2 * (h - 1) + a_
                        act.wait_ge(s_("gated"), g + 1)
                        split_hi(g, gate[:, g, :])

            def mem_samples(l, m):
                act.wait_ge(s_("dexp_in"), 1 + 2 * l)
                tell(A.activation(m["s"][:], m["s"][:], ACT.Exp), s_("dexp"), 1 + 2 * l)

            def z_and_decay():
                act.wait_ge(s_("z_out"), 16 * KS)
                for k in range(KS):
                    do(A.activation(y[:, k, :], y[:, k, :], ACT.Copy, scale=gain("dskip", k)))
                mark(s_("z_scaled"))
                act.wait_ge(s_("s5_params"), 1)
                tell(A.activation(decay[:, :, 1:], s5s[:, 6, :].unsqueeze(2).to_broadcast([P, PAIRS, NCH - 1]), ACT.Copy),
                     s_("decay_ready"), 1)

            def read_bank(job, dst, src):
                full(act, job)
                freed(own, A.activation(dst, src, ACT.Copy), job)

            def read_y(t):
                if t:
                    act.wait_ge(s_("y_out"), 16 * 9 * t)
                for a_ in range(TG // 4):
                    read_bank(("Y", t, a_), yb[:, same_side(a_)[0]:same_side(a_)[-1] + 1:2, :],
                              bank(("Y", t, a_))[:, 0:4 * (NB + NCH)].rearrange("p (g n) -> p g n", g=4))
                    mark(s_("yb_ready"))

            def gelu(t):
                act.wait_ge(s_("yz_used"), t + 1)
                for m in range(2):
                    k = 2 * t + m
                    do(A.activation(y[:, k, :], y[:, k, :], ACT.Gelu_apprx_tanh))
                mark(s_("gelu_made"))

            for t in range(THIRDS):
                if t:
                    full(act, ("V", t - 1, 2))
                for a_ in range(TP // 2):
                    read_bank(("bT", t, a_), bT[:, 2 * a_:2 * a_ + 2].rearrange("p j r n -> p (j r n)"),
                              bank(("bT", t, a_))[:, :])
                mark(s_("bT_ready"))
                if t == 0:
                    z_and_decay()
                if t:
                    read_y(t - 1)
                for a_ in range(TG // 4):
                    if t and a_ == 0:
                        act.wait_ge(s_("toep_in"), 16 * CHUNK * t)
                    read_bank(("K", t, a_), kern[:, same_side(a_)[0]:same_side(a_)[-1] + 1:2, :],
                              bank(("K", t, a_))[0:CH, :].rearrange("p (g n) -> p g n", g=4))
                    mark(s_("kern_ready"))
                if t:
                    gelu(t - 1)
            read_y(THIRDS - 1)
            mem_head(0, mb[0], 0)
            gelu(THIRDS - 1)
            act.wait_ge(s_("x_free"), 1)
            for k in range(KS):
                split_hi(k, y[:, k, 0:T].rearrange("p (j k) -> p k j", j=CHUNK), None, slice(0, T))
                split_hi(k, y[:, k, T:NT], None, slice(T, NT))
            run("glu", started=False)
            act.wait_ge(s_("gate_ready"), 1)
            for m in range(KS):
                tell(A.activation(gate[:, m, :], gate[:, m, :], ACT.Sigmoid), s_("sig_made"), m + 1)
            for h in range(1, MEMH):
                mem_head(0, mb[0], h)
            mem_samples(0, mb[0])
            ny = [0]

            def y_squares(name):
                base, n0 = PH[name][2], stat[0]

                def work(it, half):
                    act.wait_ge(panel_read, it * 2 + (base + half + 1))
                    act.wait_ge(s_("sq_used"), it * 2 + (n0 + half - 1))
                    A.activation(sq[:, half, :], y[:, bass.ds(it * 2 + half, 1), :].rearrange("p a t -> p (a t)"),
                                 ACT.Square).then_inc(s_("sq_made"), 1)

                return work

            def post(name, post_name, l, nxt, nl):
                ny[0] += 1
                stat[0] += KD
                root_x(f"{post_name}{l}")
                if nxt is not None:
                    for k in range(KD):
                        act.wait_ge(s_("x_updated"), 8 * (ny[0] - 1) + k + 1)
                        split_hi(k, x[:, k, :], gain(nxt, k, nl))
                        stat[0] += 1
                        tell(A.activation(y[:, k, :], x[:, k, :], ACT.Square), s_("sq_made"), stat[0])
                    root_x(name)

            def ffn(l):
                for f in range(2):
                    base = PH[f"up{l}{f}"][2]
                    done = 22 * l + 11 * f

                    def work(it, half):
                        fb = it + (f * KH + half * KF)
                        uu, yy = uc[half], yc[half]
                        act.wait_ge(panel_read, it * 2 + (base + half + 1))
                        A.activation(newconv[:, bass.ds(fb, 1), :].rearrange("p a t -> p (a t)"),
                                     uu[:, T:T + 2 + NB], ACT.Copy).then_inc(act_step, 1)
                        act.wait_ge(s_("h_made"), it + (done + 1))
                        A.activation(yy[:], uu[:, 2:2 + NT], ACT.Identity,
                                     bias=convw[:, l, bass.ds(it + (f * KH + half * KF + 132), 1)],
                                     scale=convw[:, l, bass.ds(it + (f * KH + half * KF + 88), 1)]
                                     ).then_inc(s_("tap_made"), 1)
                        if half == 1:
                            act.wait_ge(s_("conv_made"), it * 2 + (2 * done + 1))
                            A.activation(sg[:], yc[0][:], ACT.Silu).then_inc(s_("silu_made"), 1)

                    run(f"up{l}{f}", work)
                    run(f"down{l}{f}", y_squares(f"down{l}{f}") if f else None,
                        ahead=(l, f) != (1, 1))
                    own.n += 22

            run("wout0", y_squares("wout0"))
            post("f0", "o", 0, "ffn_pre", 0)
            ffn(0)
            post("x1", "d", 0, "kv", 0)

            def kv_work(m):
                act.wait_ge(s_("kvT_ready"), m + 1)
                if m < 6:
                    do(A.activation(kh[0:DH, 2 * m, :], kvT[0:DH, 0:T], ACT.Copy))
                    tell(A.activation(kh[0:DH, 2 * m + 1, :], kvT[DH:P, 0:T], ACT.Copy), s_("kh_made"), m + 1)

            kb, n, base, _ = PH["kv"]
            for m in range(n):
                if m + 2 <= n:
                    hi(KD, base + m + 2)
                kv_work(m)
            hi(KD, PH["win1"][2])
            hi(KD, PH["win1"][2] + 1)
            act.wait_ge(panel_done, PH["kvf"][2] + 1)
            for k in range(KD):
                split_hi(k, x[:, k, :], gain("mix_pre", k, 1))
            act.wait_ge(s_("nabs_ready"), 1)
            do(A.activation(lf[:, 2, :], lf[:, 1, :], ACT.Exp))
            sync()
            tell(A.activation(lf[:, 2, :], lf[:, 2, :], ACT.Ln, bias=1.0), s_("log_made"), 1)
            run("win1", ahead=False)
            for s in range(2):
                act.wait_ge(s_(f"ktok_out{s}"), 48)
            act.wait_ge(s_("stored"), 16 * 19)
            act.wait_ge(s_("aug_in"), 32)
            act.wait_ge(panel_done, PH["win1"][2] + 8)
            for i in range(STEPS):
                if i >= 3:
                    h = i - 3
                    r = slice(DH * (h % 2), DH * (h % 2) + DH)
                    act.wait_ge(s_("o_scaled"), h + 1)
                    tell(A.activation(x_hi[r, h // 2, 0:T], x_out[r, h // 2, 0:T], ACT.Copy), s_("o_rounded"), h + 1)
                if 1 <= i <= HEADS:
                    h, c = i - 1, 0
                    if h >= 2:
                        full(act, ("O", h - 2))
                    for a_ in range(3):
                        w = 256 if a_ == 2 else 512
                        act.wait_ge(s_("t_masked"), 3 * h + a_ + 1)
                        ins = A.activation(PT[h % 2][:, c:c + w], bank(("T", h, a_))[:, 0:w], ACT.Exp, scale=SCALE)
                        freed(own, ins, ("T", h, a_))
                        c += w
                    mark(s_("pt_ready"))
                for b in range(NB):
                    if q_step(b) == i:
                        if b >= 2:
                            act.wait_ge(s_("k_product"), PAGES * (b - 1))
                        for a_ in range(2):
                            full(act, ("q", b, a_))
                            freed(own, A.activation(qb[b % 2][:, 384 * a_:384 * a_ + 384],
                                                    bank(("q", b, a_))[:, 0:384], ACT.Copy), ("q", b, a_))
                        mark(s_("qb_ready"))
                if i < HEADS:
                    full(act, ("M", i))
                    freed(own, A.activation(qh[96:97, i, :], bank(("M", i))[0:1, :], ACT.Copy), ("M", i))
                    mark(s_("qrow_max"))
                if 2 <= i <= HEADS + 1:
                    h = i - 2
                    r = slice(DH * (h % 2), DH * (h % 2) + DH)
                    act.wait_ge(s_("rinv_ready"), h + 1)
                    freed(own, A.activation(x_out[r, h // 2, 0:T], bank(("O", h))[0:DH, :], ACT.Copy), ("O", h))
                    mark(s_("o_copied"))
                if i == SOFTMAX_STEP:
                    act.wait_ge(s_("dexp_in"), 2)
                    tell(A.activation(sc[:], sc[:], ACT.Exp), s_("dexp"), 2)
            for h in range(MEMH):
                mem_head(1, mb[1], h)
            mem_samples(1, mb[1])
            run("wout1", y_squares("wout1"), started=False)
            post("f1", "o", 1, "ffn_pre", 1)
            ffn(1)
            post("", "d", 1, None, 0)
            for a_ in range(2):
                for c in range(5):
                    n = P if c < 4 else NB
                    full(act, ("yT", c, a_))
                    freed(own, A.activation(ytok[c][0:n, 512 * a_:512 * a_ + 512], bank(("yT", c, a_))[0:n, :], ACT.Copy),
                          ("yT", c, a_))
                    mark(s_("ytok_ready"))

        @block.tensor
        def _(pe):
            def kv_turn(m):
                pe.wait_ge(s_("kvT_ready"), m + 1)
                o = take(("kvtok", m))
                for c in range(4):
                    ins = turn(o[:, c * P:c * P + P], kvT[:, c * P:c * P + P], P)
                give(ins, ("kvtok", m))
                give(turn(take(("kvsamp", m))[0:NB, 0:P], kvT[:, T:NT], P), ("kvsamp", m))

            order = {True: 0, False: 0}

            def take(job):
                ring, (o, _, free_, before) = job in J, place(job)
                assert (J if ring else FJ)[job] == order[ring], job
                order[ring] += 1
                if before:
                    pe.wait_ge(free_, before)
                return o

            def give(ins, job):
                ins.then_inc(place(job)[1], 1)

            def all_read(frees, jobs):
                for n, free_ in enumerate(frees):
                    pe.wait_ge(free_, (jobs - n + len(frees) - 1) // len(frees))

            def product(q, slot, kb, rhs, cols, wait_k=None, free=True):
                pe.wait_ge(lo_made, q + 1)
                if free:
                    pe.wait_ge(panel_read, q - 1)
                for k in range(kb):
                    if wait_k is not None:
                        wait_k(k)
                    xh, xl = rhs(k)
                    for n_, (w, r) in enumerate(((w_hi, xh), (w_hi, xl), (w_lo, xh))):
                        for b_, (c0, c1) in enumerate(cols):
                            ins = pe.matmul(big[2 * slot + b_][:, 0:c1 - c0], w[slot][:, k, :], r[:, c0:c1],
                                            start=(k == 0 and n_ == 0), stop=(k == kb - 1 and n_ == 2))
                ins.then_inc(panel_done, 1)

            xs_ = lambda k: (x_hi[:, k, :], x_lo[:, k, :])

            def phase(name, rhs=xs_, cols=HALF, wait_k=None, then=None):
                kb, n, base, _ = PH[name]
                peel = 2 if wait_k is not None else 0
                if base < 2 or n <= 2:
                    peel = n
                for i in range(peel):
                    product(base + i, (base + i) % 2, kb, rhs, cols, wait_k if i == 0 else None, base + i >= 2)
                if then is not None:
                    then()
                if n > peel:
                    with pe.Fori(0, (n - peel) // 2) as it:
                        for half in range(2):
                            c = base + peel + half
                            product(it * 2 + c, c % 2, kb, rhs, cols)

            nsplit = [0]

            def x_split(k):
                pe.wait_ge(s_("xlo_made"), nsplit[0] + k + 1)

            nsums = [0]

            def stats(jobs):
                nsums[0] += 1
                pe.wait_ge(s_("sumsq_ready"), nsums[0])
                for job, c0, c1 in jobs:
                    o = take(job)
                    give(pe.matmul(o[:, 0:c1 - c0], meanw[:], sumsq[:, c0:c1], start=True, stop=True), job)

            def stats_x(name):
                stats([(("ms", name, n), c0, c1) for n, (c0, c1) in enumerate(HALF)])

            def turn(o, src, n):
                return pe.transpose(o, src, ident[0:n, 0:n])

            pe.wait_ge(s_("consts"), 1)
            pe.wait_ge(s_("rows_in"), 16 * 8)
            give(turn(take(("rows",))[:, 0:100], rows[:], 100), ("rows",))
            pe.wait_ge(s_("mem_in"), 16)
            for a_ in range(4):
                o = take(("memT", a_))
                for n in range(4):
                    k, c = 2 * a_ + n // 2, n % 2
                    ins = turn(o[:, n * P:n * P + P], mem_in[:, c, k * P:k * P + P], P)
                give(ins, ("memT", a_))
            stats([(("ms_mem",), 0, NMEM)])

            def small_inputs():
                pe.wait_ge(s_("lrow_ready"), 1)
                pe.wait_ge(s_("lam_in"), 48)
                give(turn(take(("lam",))[:, 0:96], lrow[0:96, :], 96), ("lam",))
                pe.wait_ge(s_("conv_in"), 16 * 10)
                for l in range(2):
                    for a_ in range(2):
                        job = ("conv", l, a_)
                        give(turn(take(job)[:, 0:88], crow[:, 2 * l + a_, :], 88), job)
                for l in range(2):
                    for a_ in range(2):
                        job = ("state", l, a_)
                        o = take(job)
                        for n in range(4 if a_ == 0 else 2):
                            r = 4 * a_ + n
                            m = P if r < 5 else 64
                            ins = turn(o[:, n * P:n * P + m], srow[0:m, l, r, :], m)
                        give(ins, job)
                pe.wait_ge(s_("x_in"), 32)
                for k in range(KD):
                    o = take(("xT", k))
                    for c in range(4):
                        ins = turn(o[:, c * P:c * P + P], x_tok[:, c, k * P:k * P + P], P)
                    give(ins, ("xT", k))
                o = take(("xsT",))
                for k in range(KD):
                    ins = turn(o[:, k * NB:k * NB + NB], xs_tok[:, k * P:k * P + P], NB)
                give(ins, ("xsT",))

            for l in range(2):
                pe.wait_ge(s_("xlo_made"), (l + 1) * KD)
                phase(f"memkv{l}", cols=((l * NMEM, (l + 1) * NMEM),))
                for m in range(4):
                    job = ("memtok", l, m)
                    o = take(job)
                    q = PH[f"memkv{l}"][2] + m
                    pe.wait_ge(panel_read, q + 1)
                    src = mem_kT[:, l, m, :] if m < 2 else sq[:, m - 2, 0:NMEM]
                    for c in range(2):
                        ins = turn(o[:, c * P:c * P + P], src[:, c * P:c * P + P], P)
                    give(ins, job)
                if l == 0:
                    small_inputs()
            nsplit[0] += 2 * KD

            def c_turn(t):
                pe.wait_ge(s_("bc_in"), 16 * 6 * (t + 1))
                o = take(("cT", t))
                for ri in range(2):
                    for m in range(2):
                        ins = turn(o[:, 256 * ri + P * m:256 * ri + P * m + P],
                                   c_in[:, ri, m].rearrange("p d n -> p (d n)"), P)
                give(ins, ("cT", t))

            c_turn(0)
            stats_x("x0")
            phase("win0", wait_k=x_split)
            nsplit[0] += KD

            pe.wait_ge(s_("h0_in"), 64)
            for ri in range(2):
                for half in range(2):
                    job = ("h0", ri, half)
                    give(turn(take(job)[:, 0:96], hrow[:, ri, half, :], 96), job)
            W = NCH + NB

            def y_sums(t):
                pe.wait_ge(s_("toep_in"), 16 * CHUNK * (t + 1))
                pe.wait_ge(s_("hp_ready"), t + 1)
                for a_ in range(TG // 4):
                    job = ("Y", t, a_)
                    o = take(job)
                    for n, g in enumerate(same_side(a_)):
                        r = slice(STATE * (g % 2), STATE * (g % 2) + STATE)
                        oo = o[:, n * W:(n + 1) * W]
                        pe.matmul(oo, cp[t % 2][r, 0, g // 2, CH:], hp[t % 2][r, 0, g // 2, 0:W], start=True, stop=False)
                        pe.matmul(oo, cp[t % 2][r, 1, g // 2, CH:], hp[t % 2][r, 1, g // 2, 0:W], start=False, stop=False)
                        ins = pe.matmul(oo, toep[:, g, :], u[t % 2][:, g, 0:W], start=False, stop=True)
                    give(ins, job)

            for t in range(THIRDS):
                pe.wait_ge(s_("bp_ready"), t + 1)
                for a_ in range(TP // 2):
                    job = ("bT", t, a_)
                    o = take(job)
                    for n in range(4):
                        ins = turn(o[:, n * P:n * P + P], bp[:, n % 2, 2 * a_ + n // 2, :], P)
                    give(ins, job)
                pe.wait_ge(s_("u_in"), 16 * 10 * (t + 1 if t == 2 else 2))
                pe.wait_ge(s_("bT_ready"), t + 1)
                for a_ in range((TP + 2) // 3):
                    job = ("V", t, a_)
                    o = take(job)
                    for n in range(min(3, TP - 3 * a_)):
                        j = 3 * a_ + n
                        for ri in range(2):
                            for e in range(2):
                                r = slice(STATE * e, STATE * e + STATE)
                                ins = pe.matmul(o[r, (2 * n + ri) * W:(2 * n + ri + 1) * W], bT[:, j, ri, r],
                                                u[t % 2][:, 2 * j + e, NB:], start=True, stop=True)
                    give(ins, job)
                if t:
                    y_sums(t - 1)
                pe.wait_ge(s_("cp_ready"), t + 1)
                if t:
                    pe.wait_ge(s_("cp_re_ready"), t)
                for a_ in range(TG // 4):
                    job = ("K", t, a_)
                    o = take(job)
                    for n, g in enumerate(same_side(a_)):
                        r = slice(STATE * (g % 2), STATE * (g % 2) + STATE)
                        for ri in range(2):
                            ins = pe.matmul(o[0:CH, n * P:n * P + P], bb[t % 2][r, ri, g // 2, :], cp[t % 2][r, ri, g // 2, 0:P],
                                            start=(ri == 0), stop=(ri == 1))
                    give(ins, job)
                if t + 1 < THIRDS:
                    c_turn(t + 1)
            y_sums(THIRDS - 1)
            pe.wait_ge(s_("hfin_ready"), 1)
            for ri in range(2):
                job = ("fin", ri)
                o = take(job)
                for a_ in range(2):
                    ins = turn(o[0:108, a_ * P:a_ * P + P],
                               hfin[:, ri].rearrange("p b j -> p (b j)")[:, 108 * a_:108 * a_ + 108], P)
                give(ins, job)
            ndec = [0]

            def decode_max(jT, jM, jD, st, BH):
                ndec[0] += 1
                pe.wait_ge(s_("dmax1"), ndec[0])
                give(turn(take(jT)[0:BH, 0:P], st[:, 0, 0:BH], P), jT)
                pe.wait_ge(s_("dmax2"), ndec[0])
                give(pe.matmul(take(jM)[:, 0:BH], ones[0:BH, :], st[0:BH, 2, 0:BH], start=True, stop=True), jM)
                pe.wait_ge(s_("dsum"), ndec[0])
                give(pe.matmul(take(jD)[:, 0:BH], ones[:], st[:, 3, 0:BH], start=True, stop=True), jD)
                pe.wait_ge(s_("dp_ready"), ndec[0])

            def q_rows(l):
                for a_ in range(0 if l else 1, 2):
                    job = ("qrow", l, a_)
                    o = take(job)
                    for n in range(0 if l else 2, 4):
                        k = 4 * a_ + n
                        src = y[:, k, T:NT] if (k >= 6 or l == 0) else qs[:, k, :]
                        ins = turn(o[0:NB, n * P:n * P + P], src, P)
                    give(ins, job)

            def mem_head(l, m, h):
                r = slice(DH * (h % 2), DH * (h % 2) + DH)
                for a_ in range(2):
                    job = ("mS", l, h, a_)
                    o = take(job)
                    for qq in range(2):
                        c = (2 * a_ + qq) * P
                        ins = pe.matmul(o[:, 256 * qq:256 * qq + 256], y[r, 6 + h // 2, c:c + P],
                                        mem_kT[r, l, h // 2, :], start=True, stop=True)
                    give(ins, job)
                pe.wait_ge(s_("qrow_ready"), l + 1)
                for b in samples_of(l, h):
                    job = ("mq", l, b)
                    give(pe.matmul(take(job)[:, 0:256], sel[:, b, :], qrow[:, SEQW:D], start=True, stop=True), job)
                if l and h:
                    pv_sum(2 * h - 1)
                if l:
                    pv(2 * h)
                for a_ in range(2):
                    pe.wait_ge(s_("mp_ready"), 8 * l + 2 * h + a_ + 1)
                    job = ("mT", l, h, a_)
                    o = take(job)
                    for kc in range(2):
                        for qq in range(2):
                            ins = turn(o[:, (2 * kc + qq) * P:(2 * kc + qq + 1) * P],
                                       m["p"][:, a_, qq, kc * P:kc * P + P], P)
                    give(ins, job)
                if l:
                    pv_sum(2 * h)
                    pv(2 * h + 1)
                pe.wait_ge(s_("mpT_ready"), 4 * l + h + 1)
                job = ("mO", l, h)
                o = take(job)
                for kc in range(2):
                    ins = pe.matmul(o[r, :], mem_tok[:, l, kc, 256 + h * DH:256 + h * DH + DH], m["pT"][:, kc, :],
                                    start=(kc == 0), stop=(kc == 1))
                give(ins, job)

            def mem_samples(l, m):
                if l:
                    pv_sum(NB - 1)
                decode_max(("mmaxT", l), ("mmax", l), ("mden", l), m["dst"], NB * MEMH)
                pe.wait_ge(s_("mv_in"), 16 * (l + 1))
                job = ("mpv", l)
                o = take(job)
                for b in range(NB):
                    for f in range(2):
                        for c in range(2):
                            cc = (2 * b + f) * 2
                            ins = pe.matmul(o[:, cc:cc + 2], m["v"][:, b, c, f * P:f * P + P],
                                            m["s"][:, b, c, 2 * f:2 * f + 2], start=(c == 0), stop=(c == 1))
                give(ins, job)

            q_rows(0)
            mem_head(0, mb[0], 0)
            pe.wait_ge(s_("xlo_made"), nsplit[0] + 2 * KS)
            nsplit[0] += 2 * KS
            phase("glu")

            for h in range(1, MEMH):
                mem_head(0, mb[0], h)
            mem_samples(0, mb[0])
            nsplit[0] += KS
            pe.wait_ge(s_("xlo_made"), nsplit[0])
            pe.wait_ge(s_("mem_done"), 1)
            phase("wout0")

            def ffn(l):
                for f in range(2):
                    phase(f"up{l}{f}", wait_k=x_split if f == 0 else None,
                          then=(lambda: stats_x(f"f{l}")) if f == 0 else None)
                    if f == 0:
                        nsplit[0] += KD
                    h_half = lambda k: (h_hi[:, k, :], h_lo[:, k, :])
                    h_made = lambda k, f=f: pe.wait_ge(s_("h_made"), 2 + 22 * l + 11 * f + k)
                    if f == 0:
                        phase(f"down{l}{f}", h_half, wait_k=h_made)
                        continue
                    kb, n, base, _ = PH[f"down{l}{f}"]
                    for m in range(n):
                        product(base + m, (base + m) % 2, kb, h_half, HALF, h_made if m == 0 else None)
                        if m == 0:
                            pe.wait_ge(s_("tap_made"), 44 * (l + 1))
                        for a_ in conv_rows(m):
                            o = take(("cout", l, a_))
                            for n_ in range(4):
                                ins = turn(o[0:2 + NB, n_ * P:n_ * P + P], newconv[:, 4 * a_ + n_, :], P)
                            give(ins, ("cout", l, a_))

            stats_x("o0")
            ffn(0)
            stats_x("d0")

            kb, n, base, _ = PH["kv"]
            for m in range(n):
                product(base + m, (base + m) % 2, kb, xs_, HALF, x_split if m == 0 else None)
                if m == 1:
                    stats_x("x1")
                if m:
                    kv_turn(m - 1)
            nsplit[0] += KD
            kv_turn(11)
            q = PH["kvf"][2]
            pe.wait_ge(lo_made, q + 1)
            pe.wait_ge(panel_read, q - 1)
            for k in range(KD):
                for n_, (w, r_) in enumerate(((w_hi, x_hi), (w_hi, x_lo), (w_lo, x_hi))):
                    for b_, (c0, c1) in enumerate(HALF):
                        ins = pe.matmul(big[2 * (q % 2) + b_][:, 0:c1 - c0], w[q % 2][:, k, :], r_[:, k, c0:c1],
                                        start=(k == 0 and n_ == 0), stop=(k == KD - 1 and n_ == 2))
            ins.then_inc(panel_done, 1)
            def logf_turn():
                pe.wait_ge(s_("lf_ready"), 1)
                job = ("logf",)
                o = take(job)
                for c in range(4):
                    turn(o[:, 12 * c:12 * c + 12], lf[:, 1, c * P:c * P + P], HEADS)
                give(turn(o[0:NB, 48:60], lf[:, 1, T:NT], HEADS), job)

            phase("win1", wait_k=x_split, then=logf_turn)
            nsplit[0] += KD

            pe.wait_ge(s_("aug_in"), 32)
            pe.wait_ge(s_("q1_ready"), 1)
            pe.wait_ge(s_("kh_made"), 6)
            pe.wait_ge(s_("vtok_ready"), 6)
            q_rows(1)
            pe.wait_ge(panel_read, PH["win1"][2] + 8)
            all_read(misc_free, J[("mS", 1, 0, 0)])
            BH = NB * HEADS
            AQ = (((3, 0, 512),), ((2, 0, 384), (0, 384, 128)), ((1, 0, 256),))
            AK = (((0, 0, 512),), ((1, 0, 384), (3, 384, 128)), ((2, 0, 256),))
            PT_AT = (0, 512, 1024, 896)
            for i in range(STEPS):
                if i < HEADS:
                    for a_ in range(3):
                        o = take(("S", i, a_))
                        for qi, c, n in AQ[a_]:
                            ins = pe.matmul(o[:, c:c + n], qh[0:DH + 2, i, qi * P:qi * P + P], kh[0:DH + 2, i, 0:n],
                                            start=True, stop=True)
                        give(ins, ("S", i, a_))
                if i >= 3:
                    h = i - 3
                    o = take(("R", h))
                    pe.wait_ge(s_("rinv_ready"), h + 1)
                    r = slice(DH * (h % 2), DH * (h % 2) + DH)
                    give(pe.matmul(o[r, :], ones[0:1, 0:DH], rinv[:], start=True, stop=True), ("R", h))
                if 1 <= i <= HEADS:
                    h = i - 1
                    pe.wait_ge(s_("qrow_max"), i)
                    for a_ in range(3):
                        o = take(("T", h, a_))
                        for kc, c, n in AK[a_]:
                            ins = pe.matmul(o[:, c:c + n], kh[0:97, h, kc * P:kc * P + P], qh[0:97, h, T - n:T],
                                            start=True, stop=True)
                        give(ins, ("T", h, a_))
                for b in range(NB):
                    if q_step(b) == i:
                        pe.wait_ge(s_("qrow_ready"), 2)
                        for a_ in range(2):
                            o = take(("q", b, a_))
                            give(pe.matmul(o[:, 0:384], sel[:, b, :], qrow[:, 384 * a_:384 * a_ + 384], start=True,
                                           stop=True), ("q", b, a_))
                if i == DECAY_STEP:
                    pe.wait_ge(s_("pre_ready"), 1)
                    o = take(("dtot",))
                    pe.matmul(o[:, 0:BH], ones[:], fst[:, 5, 0:BH], start=True, stop=False)
                    give(pe.matmul(o[:, 0:BH], ones[0:NB, :], lmask[:].rearrange("r b h -> r (b h)"), start=False,
                                   stop=True), ("dtot",))
                    for a_ in range(2):
                        o = take(("dc", a_))
                        bs = slice(4 * a_, 4 * a_ + 4)
                        pe.matmul(o[:, 0:384], tri[:], logf[:, bs].rearrange("p b g h -> p (b g h)"), start=True,
                                  stop=False)
                        give(pe.matmul(o[:, 0:384], ones[:], pre[:, bs].rearrange("p b g h -> p (b g h)"),
                                       start=False, stop=True), ("dc", a_))
                if i < HEADS:
                    o = take(("M", i))
                    pe.wait_ge(s_("nmax_ready"), i + 1)
                    for qi in range(4):
                        ins = pe.matmul(o[0:1, qi * P:qi * P + P], nmax[i % 2][:, qi:qi + 1], ident[:], start=True,
                                        stop=True)
                    give(ins, ("M", i))
                if 2 <= i <= HEADS + 1:
                    h = i - 2
                    o = take(("O", h))
                    pe.wait_ge(s_("pt_ready"), h + 1)
                    for kc in range(4):
                        n = T - kc * P
                        ins = pe.matmul(o[0:DH + 1, T - n:T], vtok[:, kc, h, :], PT[h % 2][:, PT_AT[kc]:PT_AT[kc] + n],
                                        start=(kc == 0), stop=(kc == 3))
                    give(ins, ("O", h))
                if i == SOFTMAX_STEP:
                    decode_max(("fmaxT",), ("fmax",), ("fden",), fst, BH)
            all_read(fox_free, len(FJ))

            def pv(b):
                if b >= 2:
                    pe.wait_ge(s_("vm_ready"), b - 1)
                o = [big[2 * (b % 2) + a_] for a_ in range(2)]
                for pg in range(PAGES):
                    pe.wait_ge(s_(f"page_in{pg}"), 16 * (NB + b + 1))
                    for a_ in range(2):
                        ins = pe.matmul(o[a_][0:HEADS, 0:384], sc[:, b, pg, :], page[pg][:, 384 * a_:384 * a_ + 384],
                                        start=(pg == 0), stop=False)
                    ins.then_inc(s_("v_used"), 1)
                for a_ in range(2):
                    ins = pe.matmul(o[a_][0:HEADS, 0:384], sc[0:NB, b, PAGES, :], kvs[:, 1, 384 * a_:384 * a_ + 384],
                                    start=False, stop=True)
                ins.then_inc(s_("pv_done"), 1)

            def pv_sum(b):
                o = take(("fpv", b))
                pe.wait_ge(s_("vm_ready"), b + 1)
                for f in range(6):
                    ins = pe.matmul(o[:, f:f + 1], vm[0:HEADS, f * P:f * P + P], ones[0:HEADS, 0:1], start=True,
                                    stop=True)
                give(ins, ("fpv", b))

            for h in range(MEMH):
                mem_head(1, mb[1], h)
            mem_samples(1, mb[1])
            pe.wait_ge(s_("fox_done"), 1)
            pe.wait_ge(s_("mem_done"), 2)
            phase("wout1")
            stats_x("o1")
            ffn(1)
            stats_x("d1")
            for a_ in range(2):
                pe.wait_ge(s_("x_updated"), 24 + 4 * a_ + 4)
                for c in range(5):
                    o = take(("yT", c, a_))
                    for n in range(4):
                        k = 4 * a_ + n
                        if c < 4:
                            ins = turn(o[:, n * P:n * P + P], x[:, k, c * P:c * P + P], P)
                        else:
                            ins = turn(o[0:NB, n * P:n * P + P], x[:, k, T:NT], P)
                    give(ins, ("yT", c, a_))


OUTS = [
    ("y_prompt", (1, T, D)), ("y_sample", (NB, 1, D)),
    ("prompt_ssm_re", (1, 1, GROUPS, STATE)), ("prompt_ssm_im", (1, 1, GROUPS, STATE)),
    ("prompt_k", (1, T, HEADS, DH)), ("prompt_v", (1, T, HEADS, DH)), ("prompt_logf", (1, T, HEADS)),
    ("prompt_mem_k", (2, 1, NMEM, MEMH, DH)), ("prompt_mem_v", (2, 1, NMEM, MEMH, DH)),
    ("prompt_ffn_conv", (2, 1, 2, 2 * DFF)),
    ("sample_ssm_re", (1, NB, GROUPS, STATE)), ("sample_ssm_im", (1, NB, GROUPS, STATE)),
    ("sample_k", (NB, 1, HEADS, DH)), ("sample_v", (NB, 1, HEADS, DH)), ("sample_logf", (NB, 1, HEADS)),
    ("sample_ffn_conv", (2, NB, 2, 2 * DFF)),
]


def kernel(**inputs):
    from concourse import bacc
    from concourse.bass_utils import run_bass_kernel_spmd

    nc = bacc.Bacc("TRN2", target_bir_lowering=False, num_devices=1)
    arrays, ins, outs = {}, {}, {}
    for name, a in inputs.items():
        a = np.ascontiguousarray(a)
        arrays[f"in_{name}"] = a
        ins[name] = nc.dram_tensor(f"in_{name}", a.shape, mybir.dt.from_np(a.dtype), kind="ExternalInput").ap()
    for name, shape in OUTS:
        outs[name] = nc.dram_tensor(f"out_{name}", shape, F32, kind="ExternalOutput").ap()
    program(nc, ins, outs)
    r = run_bass_kernel_spmd(nc, [arrays], core_ids=[0])
    return tuple(r.results[0][f"out_{name}"] for name, _ in OUTS)
```
